# Optimizing a Trainium2 kernel written in Bass

```python
import jax, jax.numpy as jnp
from jax import lax
import numpy as np

D_MODEL = 1024
BATCH = 1
SEQ = 1024
DEPTH = 1
DEC_BATCH = 8
DEC_SEQ = 4
PAST_LEN = 8192
PAGE_SIZE = 128

C_A = D_MODEL
C_B = (3 * D_MODEL) // 2
CONV_WIDTH = 31
CHUNK = 128
N_GROUPS = 8
GROUP_DIM = C_B // N_GROUPS
D_FF = 4 * D_MODEL
P_DIM = 256
D_IN = 2 * C_A + 2 * C_B + 2 * D_MODEL
EPS = 1e-6

kernel_name = "gated_conformer_gmlp_decoder_step"

def _rmsnorm(x, g):
    xf = x.astype(jnp.float32)
    y = xf * lax.rsqrt(jnp.mean(xf * xf, axis=-1, keepdims=True) + EPS)
    return (y * g.astype(jnp.float32)).astype(x.dtype)

def _layernorm(x, g, b):
    xf = x.astype(jnp.float32)
    mu = jnp.mean(xf, axis=-1, keepdims=True)
    xc = xf - mu
    y = xc * lax.rsqrt(jnp.mean(xc * xc, axis=-1, keepdims=True) + EPS)
    return (y * g.astype(jnp.float32) + b.astype(jnp.float32)).astype(x.dtype)

def _depthwise_causal_conv(x_full, w, b):
    y = lax.conv_general_dilated(
        x_full, w[:, None, :], window_strides=(1,), padding='VALID',
        dimension_numbers=('NWC', 'WIO', 'NWC'), feature_group_count=x_full.shape[-1])
    return y + b

def _chunk_spatial_mix(v, w_s, b_s):
    bsz, t_len, _ = v.shape
    n_chunks = -(-t_len // CHUNK)
    pad = n_chunks * CHUNK - t_len
    vp = jnp.pad(v, ((0, 0), (0, pad), (0, 0))).reshape(bsz, n_chunks, CHUNK, N_GROUPS, GROUP_DIM)
    causal = jnp.tril(jnp.ones((CHUNK, CHUNK), dtype=bool))
    wm = jnp.where(causal[None], w_s, jnp.zeros_like(w_s))
    mixed = jnp.einsum('gts,bnsgc->bntgc', wm, vp) + jnp.transpose(b_s)[None, None, :, :, None]
    return mixed.reshape(bsz, n_chunks * CHUNK, C_B)[:, :t_len]

def _layer(x, conv_prev, p_l, g_mix, w_in, b_in, conv_w, conv_b, ln_a_g, ln_a_b, w_a_out,
           ln_v_g, ln_v_b, w_s, b_s, w_b_out, w_o, g_ffn, w_ff1, w_ff2,
           g_ple, w_ple, w_ple_gate, b_ple_gate):
    h = _rmsnorm(x, g_mix)
    z = h @ w_in + b_in
    a_lin = z[..., :C_A]
    a_gate = z[..., C_A:2 * C_A]
    zb = z[..., 2 * C_A:2 * C_A + 2 * C_B]
    g_a = z[..., 2 * C_A + 2 * C_B:2 * C_A + 2 * C_B + D_MODEL]
    g_b = z[..., 2 * C_A + 2 * C_B + D_MODEL:]
    glu = a_lin * jax.nn.sigmoid(a_gate)
    conv_in = jnp.concatenate([conv_prev, glu], axis=1)
    ya = _depthwise_causal_conv(conv_in, conv_w, conv_b)
    ya = jax.nn.silu(_layernorm(ya, ln_a_g, ln_a_b)) @ w_a_out
    new_conv = conv_in[:, -(CONV_WIDTH - 1):]
    zb = jax.nn.gelu(zb)
    u = zb[..., :C_B]
    v = _layernorm(zb[..., C_B:], ln_v_g, ln_v_b)
    yb = (u * _chunk_spatial_mix(v, w_s, b_s)) @ w_b_out
    m = jax.nn.sigmoid(g_a) * ya + jax.nn.sigmoid(g_b) * yb
    x = x + m @ w_o
    hf = _rmsnorm(x, g_ffn)
    x = x + jnp.square(jax.nn.relu(hf @ w_ff1)) @ w_ff2
    gate = jax.nn.sigmoid(_rmsnorm(x, g_ple) @ w_ple_gate + b_ple_gate)
    x = x + gate * (p_l @ w_ple)
    t_len = x.shape[1]
    start = ((t_len - 1) // CHUNK) * CHUNK
    return x, new_conv, v[:, start:]

def setup_inputs(seed: int = 0) -> dict:
    key = jax.random.key(seed)
    ks = jax.random.split(key, 32)

    def nrm(k, shape, scale):
        return (jax.random.normal(k, shape, dtype=jnp.float32) * scale).astype(jnp.float32)

    def gain(k, shape):
        return 1.0 + nrm(k, shape, 0.05)

    L = DEPTH
    return {
        "x_prompt": nrm(ks[0], (BATCH, SEQ, D_MODEL), 1.0),
        "x_sample": nrm(ks[1], (DEC_BATCH, DEC_SEQ, D_MODEL), 1.0),
        "state_conv": nrm(ks[2], (L, DEC_BATCH, CONV_WIDTH - 1, C_A), 0.5),
        "p_prompt": nrm(ks[3], (L, BATCH, SEQ, P_DIM), 1.0),
        "p_sample": nrm(ks[4], (L, DEC_BATCH, DEC_SEQ, P_DIM), 1.0),
        "g_mix": gain(ks[5], (L, D_MODEL)),
        "w_in": nrm(ks[6], (L, D_MODEL, D_IN), D_MODEL ** -0.5),
        "b_in": nrm(ks[7], (L, D_IN), 0.02),
        "conv_w": nrm(ks[8], (L, CONV_WIDTH, C_A), CONV_WIDTH ** -0.5),
        "conv_b": nrm(ks[9], (L, C_A), 0.02),
        "ln_a_g": gain(ks[10], (L, C_A)),
        "ln_a_b": nrm(ks[11], (L, C_A), 0.02),
        "w_a_out": nrm(ks[12], (L, C_A, D_MODEL), C_A ** -0.5),
        "ln_v_g": gain(ks[13], (L, C_B)),
        "ln_v_b": nrm(ks[14], (L, C_B), 0.02),
        "w_s": nrm(ks[15], (L, N_GROUPS, CHUNK, CHUNK), CHUNK ** -0.5),
        "b_s": 1.0 + nrm(ks[16], (L, N_GROUPS, CHUNK), 0.1),
        "w_b_out": nrm(ks[17], (L, C_B, D_MODEL), C_B ** -0.5),
        "w_o": nrm(ks[18], (L, D_MODEL, D_MODEL), D_MODEL ** -0.5),
        "g_ffn": gain(ks[19], (L, D_MODEL)),
        "w_ff1": nrm(ks[20], (L, D_MODEL, D_FF), D_MODEL ** -0.5),
        "w_ff2": nrm(ks[21], (L, D_FF, D_MODEL), D_FF ** -0.5),
        "g_ple": gain(ks[22], (L, D_MODEL)),
        "w_ple": nrm(ks[23], (L, P_DIM, D_MODEL), P_DIM ** -0.5),
        "w_ple_gate": nrm(ks[24], (L, D_MODEL, D_MODEL), D_MODEL ** -0.5),
        "b_ple_gate": nrm(ks[25], (L, D_MODEL), 0.02),
        "g_final": gain(ks[26], (D_MODEL,)),
    }

def reference(x_prompt, x_sample, state_conv, p_prompt, p_sample,
              g_mix, w_in, b_in, conv_w, conv_b, ln_a_g, ln_a_b, w_a_out,
              ln_v_g, ln_v_b, w_s, b_s, w_b_out, w_o, g_ffn, w_ff1, w_ff2,
              g_ple, w_ple, w_ple_gate, b_ple_gate, g_final):
    xp = x_prompt
    xs = x_sample
    conv_p_list, conv_s_list, v_p_list, v_s_list = [], [], [], []
    for i in range(DEPTH):
        w_i = (g_mix[i], w_in[i], b_in[i], conv_w[i], conv_b[i], ln_a_g[i], ln_a_b[i], w_a_out[i],
               ln_v_g[i], ln_v_b[i], w_s[i], b_s[i], w_b_out[i], w_o[i], g_ffn[i], w_ff1[i],
               w_ff2[i], g_ple[i], w_ple[i], w_ple_gate[i], b_ple_gate[i])
        zero_hist = jnp.zeros((xp.shape[0], CONV_WIDTH - 1, C_A), dtype=xp.dtype)
        xp, conv_p, v_p = _layer(xp, zero_hist, p_prompt[i], *w_i)
        xs, conv_s, v_s = _layer(xs, state_conv[i], p_sample[i], *w_i)
        conv_p_list.append(conv_p)
        conv_s_list.append(conv_s)
        v_p_list.append(v_p)
        v_s_list.append(v_s)
    y_prompt = _rmsnorm(xp, g_final)
    y_sample = _rmsnorm(xs, g_final)
    conv_prompt = jnp.stack(conv_p_list, axis=0)
    conv_sample = jnp.stack(conv_s_list, axis=0)
    v_prompt = jnp.stack(v_p_list, axis=0)
    v_sample = jnp.stack(v_s_list, axis=0)
    return (y_prompt, y_sample, conv_prompt, conv_sample, v_prompt, v_sample)


_drawn_inputs = setup_inputs


def setup_inputs(seed=0):
    import zlib

    import numpy as np

    out = dict(_drawn_inputs(seed))
    spreads = {}
    factors = {'conv_b': 4.678,
     'ln_a_g': 3.268,
     'ln_a_b': 8.0,
     'ln_v_b': 2.836,
     'g_ple': 27.215,
     'b_ple_gate': 64.0}
    for name, (base, spread) in spreads.items():
        noise = np.random.default_rng([zlib.crc32(name.encode()), seed]).standard_normal(out[name].shape)
        drawn = base * np.exp(spread * noise) if base else spread * noise
        out[name] = __import__('jax').numpy.asarray(drawn.astype(out[name].dtype))
    for name, factor in factors.items():
        out[name] = (out[name] * factor).astype(out[name].dtype)
    return out
```

```python
from contextlib import ExitStack

import concourse.bass as bass
from concourse import mybir

F32 = mybir.dt.float32
F32R = mybir.dt.float32r
ALU = mybir.AluOpType
ACT = mybir.ActivationFunctionType
AX_X = mybir.AxisListType.X

P = 128
D = 1024
C_B = 1536
D_FF = 4096
P_DIM = 256
SEQ = 1024
DEC_B, DEC_S = 8, 4
NS = DEC_B * DEC_S
T = SEQ + NS
CHUNK = 128
N_CHUNKS = SEQ // CHUNK
GROUPS = 8
TAPS = 31
HIST = TAPS - 1
EPS = 1e-6

KD = D // P
KB = C_B // P
KF = D_FF // P
KP = P_DIM // P
NC = 3
TC = T // NC
UNIT = 8
FG = 4
NG = KF // FG

B_LIN, B_GATE, B_U, B_V, B_GA, B_GB = 0, KD, 2 * KD, 2 * KD + KB, 2 * KD + 2 * KB, 3 * KD + 2 * KB
N_BIN = 4 * KD + 2 * KB
N_TOK = -(-T // P)

STAGES = [
    ("norm1", 2, 0), ("A", 2 * KD, 2 * KD), ("V", KB // 2, KB // 2), ("mean", 1, 0),
    ("U", KB // 2, KB // 2), ("B", KD // 2, KD // 2), ("var", 2, 0), ("AO", KD // 2, KD // 2),
    ("O", KD // 2, KD // 2), ("norm2", 2, 0), ("F", NG * (FG + KD) // 2, NG * (FG + KD) // 2),
    ("PE", KD // 2, KD // 2), ("norm3", 2, 0), ("G", KD // 2, KD // 2), ("norm4", 2, 0),
]
JOB = {}
_n0 = _n1 = 0
for _name, _a, _b in STAGES:
    JOB[_name] = (_n0, _n1)
    _n0 += _a
    _n1 += _b

SPLIT = {}
_n = 0
for _name, _k in (("H1", KD), ("GB", KB), ("A", KD), ("M", KD), ("H2", KD), ("F", KF), ("P", KP), ("H3", KD)):
    SPLIT[_name] = _n
    _n += _k

W0 = {}
_n = 0
for _name, _k in (("A", 4 * KD), ("V", KB), ("U", KB), ("B", KB), ("AO", KD), ("O", KD),
                  ("F", NG * 2 * FG), ("PE", KD * KP // UNIT), ("G", KD)):
    W0[_name] = _n
    _n += _k
N_UNITS = _n

NORM = {"norm1": 0, "var": 1, "norm2": 2, "norm3": 3, "norm4": 4}


def build(nc, io):
    ctx = ExitStack()
    with ctx:
        ROW = T * 4
        base = (nc.sbuf_base + 31) // 32 * 32

        def at(name, shape, dt, off):
            return nc.alloc_sbuf_tensor_at(name, shape, dt, offset=base + off)

        def rows(name, first, n, dt=F32):
            return at(name, [P, n, T], dt, first * ROW)

        h1_hi, h1_lo = rows("h1_hi", 0, KD, F32R), rows("h1_lo", 8, KD, F32R)
        x1 = rows("x1", 16, KD)
        sig, lin = rows("sig", 16, 1), rows("lin", 17, 1)
        gate_st = rows("gate_st", 18, 2)
        vt = rows("vt", 16, KB)
        conv_in = rows("conv_in", 26, 2)
        t0 = 28 * ROW
        glu = at("glu", [P, HIST + T + 2], F32, t0)
        acc0 = at("acc0", [P, SEQ], F32, t0 + 4352)
        acc1 = at("acc1", [P, SEQ], F32, t0 + 8448)
        conv_out = at("conv_out", [P, T], F32, t0 + 12544)
        prod = at("prod", [P, DEC_S, DEC_B, TAPS], F32, t0 + 16768)
        v_chunk = at("v_chunk", [P, KB, CHUNK], F32, t0)
        v_tok = at("v_tok", [P, C_B], F32, t0 + 6144)
        v_hi = at("v_hi", [P, C_B], F32R, t0 + 12288)
        v_lo = at("v_lo", [P, C_B], F32R, t0 + 18432)
        lnv_g = at("lnv_g", [P, C_B], F32, t0 + 24576)
        lnv_b = at("lnv_b", [P, C_B], F32, t0 + 30720)
        wm_hi = at("wm_hi", [P, GROUPS, CHUNK], F32R, t0 + 36864)
        wm_lo = at("wm_lo", [P, GROUPS, CHUNK], F32R, t0 + 40960)
        ws_hi = at("ws_hi", [P, GROUPS, NS], F32R, t0 + 45056)
        ws_lo = at("ws_lo", [P, GROUPS, NS], F32R, t0 + 46080)
        wm_raw = rows("wm_raw", 40, 1)
        ws_raw = at("ws_raw", [P, 1, GROUPS * NS], F32, t0 + 47104)
        conv_mean = rows("conv_mean", 40, 1)
        t1 = 41 * ROW
        u_st = rows("u_st", 41, 1)
        hist = at("hist", [P, KD * DEC_B, HIST + DEC_S], F32, t1)
        conv_tail = at("conv_tail", [P, KD, HIST], F32, t1 + 8704)
        bs_p = at("bs_p", [P, GROUPS, CHUNK], F32, t1 + ROW)
        bs_s = at("bs_s", [P, GROUPS, NS], F32, t1 + ROW + 4096)
        gb = rows("gb", 28, KB)
        gb_hi, gb_lo = rows("gb_hi", 16, KB, F32R), rows("gb_lo", 0, KB, F32R)
        mean_b = rows("mean_b", 12, 1)
        ssq_b, sB_st, sq_b = rows("ssq_b", 13, 1), rows("sB_st", 14, 1), rows("sq_b", 15, 1)
        mix = rows("mix", 28, KD)
        xc = rows("xc", 36, KD)
        a_hi, a_lo = rows("a_hi", 0, KD, F32R), rows("a_lo", 8, KD, F32R)
        m_hi, m_lo = rows("m_hi", 36, KD, F32R), rows("m_lo", 16, KD, F32R)
        rstd, ssq, val = rows("rstd", 24, 1), rows("ssq", 25, 1), rows("val", 26, 2)
        stage = rows("stage", 24, 2)
        x = rows("x", 28, KD)
        h2_hi, h2_lo = rows("h2_hi", 0, KD, F32R), rows("h2_lo", 8, KD, F32R)
        f_hi, f_lo = rows("f_hi", 16, FG, F32R), rows("f_lo", 20, FG, F32R)
        relu = rows("relu", 24, 1)
        p_raw = rows("p_raw", 36, KP)
        p_hi, p_lo = rows("p_hi", 38, KP, F32R), rows("p_lo", 40, KP, F32R)
        pe_out = rows("pe_out", 16, KD)
        h3_hi, h3_lo = rows("h3_hi", 0, KD, F32R), rows("h3_lo", 8, KD, F32R)
        c0 = 44 * ROW
        w_raw = at("w_raw", [P, 2, UNIT * P], F32, c0)
        w_hi = at("w_hi", [P, 2, UNIT * P], F32R, c0 + 8192)
        w_lo = at("w_lo", [P, 2, UNIT * P], F32R, c0 + 16384)
        c1 = c0 + 24576
        ones = at("ones", [P, P], F32, c1)
        ident = at("ident", [P, P], F32, c1 + 1024)
        cols = at("cols", [P, N_BIN + 8 * KD], F32, c1 + 512)
        taps = at("taps", [P, KD, 32], F32, t1 + 9728)
        tok = at("tok", [P, 2, 16], F32, c1 + 1600)
        diag = rows("diag", 26, 1)
        tap = at("tap", [P, 32], F32, c1 + 2048)
        stats = at("stats", [P, 3, 6], F32, c1 + 2176)
        mv = at("mv", [P, 2], F32, c1 + 2272)
        rs_v = at("rs_v", [P, 1], F32, c1 + 2304)
        w_col = at("w_col", [P, 1], F32, c1 + 1728)
        samp = at("samp", [P, NS], F32, t0 + 20736)
        G_MIX, G_FFN, G_PLE, G_FIN, LNA_G, LNA_B, B_PLE = (N_BIN + KD * n for n in range(7))

        ps = ctx.enter_context(nc.psum_tensor("ps", [P, 2, NC, 512], F32))
        pm = ctx.enter_context(nc.psum_tensor("pm", [P, 2, 512], F32))

        def scratch(name, n):
            return nc.dram_tensor(name, (n, P, T), F32, kind="Internal").ap()

        sA_d, sB_d, conv_d, u_d = scratch("sA_d", KD), scratch("sB_d", KD), scratch("conv_d", KD), scratch("u_d", KB)

        def sem(name):
            return ctx.enter_context(nc.semaphore(name))

        w_loaded = [sem("w_loaded0"), sem("w_loaded1")]
        w_hi_done = sem("w_hi_done")
        w_ready = sem("w_ready")
        w_started = sem("w_started")
        psum_ready = [sem("psum_ready0"), sem("psum_ready1")]
        psum_free = [sem("psum_free0"), sem("psum_free1")]
        x_loaded = [sem(f"x_loaded{i}") for i in range(4)]
        const_loaded = sem("const_loaded")
        tab_loaded = sem("tab_loaded")
        wm_loaded = sem("wm_loaded")
        ones_set = sem("ones_set")
        ws_zero, wm_masked, wm_split = sem("ws_zero"), sem("wm_masked"), sem("wm_split")
        ident_set = sem("ident_set")
        tok_ready, rms_ready, diag_ready = sem("tok_ready"), sem("rms_ready"), sem("diag_ready")
        rs_ready = sem("rs_ready")
        sq_done, ssq_done = sem("sq_done"), sem("ssq_done")
        val_ready = sem("val_ready")
        hi_ready, lo_ready = sem("hi_ready"), sem("lo_ready")
        glu_done, tap_set, conv_step = sem("glu_done"), sem("tap_set"), sem("conv_step")
        conv_done, conv_stored = sem("conv_done"), sem("conv_stored")
        gate_stored = [sem("gate_stored0"), sem("gate_stored1")]
        conv_back = [sem("conv_back0"), sem("conv_back1")]
        conv_sum = sem("conv_sum")
        bs_loaded, hist_stored, tail_stored = sem("bs_loaded"), sem("hist_stored"), sem("tail_stored")
        u_stored = sem("u_stored")
        vc_done = sem("vc_done")
        pm_ready, pm_free = [sem("pm_ready0"), sem("pm_ready1")], [sem("pm_free0"), sem("pm_free1")]
        vtok_copied, ln_step = sem("vtok_copied"), sem("ln_step")
        vhi_done, vlo_done = sem("vhi_done"), sem("vlo_done")
        vout = sem("vout")
        u_back = sem("u_back")
        mean_copied, xc_loaded, xc_done = sem("mean_copied"), sem("xc_loaded"), sem("xc_done")
        sB_loaded, st_loaded = sem("sB_loaded"), [sem("st_loaded0"), sem("st_loaded1")]
        norm_y, silu_done, gated, mix_done = sem("norm_y"), sem("silu_done"), sem("gated"), sem("mix_done")
        sq_f, p_loaded, sg_done, g_mul = sem("sq_f"), sem("p_loaded"), sem("sg_done"), sem("g_mul")
        x_done = sem("x_done")
        y_ready, y_stored = sem("y_ready"), [sem("y_stored0"), sem("y_stored1")]

        block = ctx.enter_context(nc.Block())

        def pieces(ap):
            return ap.rearrange("p (c t) -> p c t", c=NC)

        def row(tile, k):
            if isinstance(k, int):
                return tile[:, k, :]
            return tile[:, bass.ds(k, 1), :].rearrange("p a t -> p (a t)")

        def drow(dram, k):
            if isinstance(k, int):
                return dram[k, :, :]
            return dram[bass.ds(k, 1), :, :].rearrange("a p t -> p (a t)")

        def col(first, k):
            if isinstance(k, int):
                return cols[:, first + k:first + k + 1]
            return cols[:, bass.ds(first + k, 1)]

        def bank(slot):
            return ps[:, slot, :, 0:TC]

        def ready(eng, stage_name, slot, n):
            eng.wait_ge(psum_ready[slot], JOB[stage_name][slot] + n + 1)

        @block.sync
        def _(sp):
            for i in (0, 2):
                sp.dma_start(x1[:, 2 * i:2 * i + 2, :], io["xT"][2 * i:2 * i + 2].rearrange("k p t -> p k t"))\
                    .then_inc(x_loaded[i], 16)
            for s in range(2):
                sp.dma_start(w_raw[:, s, :], io["weights"][s]).then_inc(w_loaded[s], 16)
            with sp.Fori(1, N_UNITS // 2) as i:
                for s in range(2):
                    src = sp.snap(2 * i + s)
                    unit = io["weights"][bass.ds(src, 1)].rearrange("a p n -> p (a n)")
                    sp.wait_ge(w_ready, 2 * i + s - 1)
                    sp.dma_start(w_raw[:, s, :], unit).then_inc(w_loaded[s], 16)

        @block.gpsimd
        def _(pool):
            pool.memset(ws_raw[:, 0, 0:GROUPS * NS], 0.0).then_inc(ws_zero, 1)
            pool.memset(ident[:, :], 0.0).then_inc(ident_set, 1)
            pool.wait_ge(ident_set, 1)
            pool.affine_select(out=ident[:, :], in_=ident[:, :], compare_op=ALU.not_equal, fill=1.0, base=0,
                               pattern=[[-1, P]], channel_multiplier=1).then_inc(ident_set, 1)

            def split(s, n, u):
                pool.wait_ge(w_loaded[s], 16 * n)
                if not isinstance(u, int):
                    pool.wait_ge(w_started, u)
                    pool.tensor_tensor(w_col[:, :], w_raw[:, s, 0:1], w_raw[:, s, 1:2], ALU.add)
                pool.tensor_copy(w_hi[:, s, :], w_raw[:, s, :]).then_inc(w_hi_done, 1)
                pool.wait_ge(w_hi_done, u + 1)
                pool.tensor_tensor(w_lo[:, s, :], w_raw[:, s, :], w_hi[:, s, :].bitcast(F32), ALU.subtract)\
                    .then_inc(w_ready, 1)

            for s in range(2):
                split(s, 1, s)
            pool.wait_ge(wm_loaded, 16 * (1 + DEC_B))
            m1 = wm_raw[:, 0, 0:GROUPS * CHUNK].rearrange("p (g t) -> p g t", g=GROUPS)
            m2 = ws_raw[:, 0, 0:GROUPS * NS].rearrange("p (g t) -> p g t", g=GROUPS)
            pool.affine_select(out=m1, in_=m1, compare_op=ALU.is_ge, fill=0.0, base=0,
                               pattern=[[0, GROUPS], [1, CHUNK]], channel_multiplier=-1).then_inc(wm_masked, 1)
            pool.affine_select(out=m2, in_=m2, compare_op=ALU.is_ge, fill=0.0, base=0,
                               pattern=[[0, GROUPS], [1, NS]], channel_multiplier=-1).then_inc(wm_masked, 1)
            pool.wait_ge(wm_masked, 2)
            pool.tensor_copy(wm_hi[:, :, :], m1).then_inc(wm_split, 1)
            pool.tensor_copy(ws_hi[:, :, :], m2).then_inc(wm_split, 1)
            pool.wait_ge(wm_split, 2)
            pool.tensor_tensor(wm_lo[:, :, :], m1, wm_hi[:, :, :].bitcast(F32), ALU.subtract).then_inc(wm_split, 1)
            pool.tensor_tensor(ws_lo[:, :, :], m2, ws_hi[:, :, :].bitcast(F32), ALU.subtract).then_inc(wm_split, 1)
            with pool.Fori(1, N_UNITS // 2) as i:
                for s in range(2):
                    split(s, i + 1, 2 * i + s)

        @block.tensor
        def _(pe):
            def free(stage_name, slot, n):
                pe.wait_ge(psum_free[slot], JOB[stage_name][slot] + n + slot)

            def tile_product(slot, s, n, hi, lo, k, start, stop):
                first = last = None
                for w, a in ((w_hi, hi), (w_hi, lo), (w_lo, hi)):
                    for c in range(NC):
                        last = pe.matmul(ps[:, slot, c, 0:TC], w[:, s, n * P:(n + 1) * P],
                                         a[:, k, c * TC:(c + 1) * TC],
                                         start=start and w is w_hi and a is hi, stop=stop and w is w_lo)
                        if first is None:
                            first = last
                return first, last

            def product(stage_name, slot, n, u, s, hi, lo, base_k):
                free(stage_name, slot, n)
                pe.wait_ge(w_ready, u + 1)
                for k in range(KD):
                    pe.wait_ge(lo_ready, base_k + k + 1)
                    first, last = tile_product(slot, s, k, hi, lo, k, k == 0, k == KD - 1)
                    if k == 0:
                        first.then_inc(w_started, 1)
                last.then_inc(psum_ready[slot], 1)

            def mean_over_features(stage_name, src, count_sem, count):
                free(stage_name, 0, 0)
                pe.wait_ge(count_sem, count)
                for c in range(NC):
                    last = pe.matmul(ps[:, 0, c, 0:TC], ones[:, :], src[:, 0, c * TC:(c + 1) * TC],
                                     start=True, stop=True)
                last.then_inc(psum_ready[0], 1)

            def inverse_rms(stage_name, src):
                if JOB[stage_name][0]:
                    free(stage_name, 0, 0)
                pe.wait_ge(ssq_done, 10 * (NORM[stage_name] + 1))
                for c in range(N_TOK):
                    t = min(c * P, T - P)
                    last = pe.matmul(ps[:, 0, 0, c:c + 1], src[:, 0, t:t + P], ones[:, 0:1], start=True, stop=True)
                last.then_inc(psum_ready[0], 1)
                free(stage_name, 0, 1)
                pe.wait_ge(diag_ready, 2 * (NORM[stage_name] + 1))
                for c in range(NC):
                    last = pe.matmul(ps[:, 0, c, 0:TC], ones[:, :], diag[:, 0, c * TC:(c + 1) * TC],
                                     start=True, stop=True)
                last.then_inc(psum_ready[0], 1)

            pe.wait_ge(ones_set, 1)
            inverse_rms("norm1", ssq)

            with pe.Fori(0, KD) as i:
                for j in range(4):
                    product("A", j % 2, 2 * i + j // 2, W0["A"] + 4 * i + j, j % 2, h1_hi, h1_lo, SPLIT["H1"])
            with pe.Fori(0, KB // 2) as i:
                for j in range(2):
                    product("V", j, i, W0["V"] + 2 * i + j, j, h1_hi, h1_lo, SPLIT["H1"])
            mean_over_features("mean", conv_mean, conv_sum, 1 + KD)

            def u_product(j, par):
                product("U", par, (j - par) // 2 if isinstance(j, int) else j, 0, 0, None, None, 0)

            def transposes(n, b0, b1):
                pe.wait_ge(vc_done, n + 1)
                if isinstance(n, int) and n == 0:
                    pe.wait_ge(ident_set, 2)
                for g in range(3):
                    b = g % 2
                    before = (b0 + g // 2) if b == 0 else b1
                    if not (isinstance(before, int) and before == 0):
                        pe.wait_ge(pm_free[b], before)
                    for q in range(4):
                        last = pe.transpose(pm[:, b, q * P:(q + 1) * P], v_chunk[:, 4 * g + q, :], ident[:, :])
                    last.then_inc(pm_ready[b], 1)

            def mixing(n, b0, b1, w, hi, lo):
                pe.wait_ge(vlo_done, n + 1)
                if isinstance(n, int) and n == 0:
                    pe.wait_ge(wm_split, 4)
                for q in range(4):
                    b = (q + 1) % 2
                    before = (b0 if b == 0 else b1) + q // 2
                    pe.wait_ge(pm_free[b], before)
                    for c, g, ng, off in ((3 * q, 2 * q, 1, 0), (3 * q + 1, 2 * q, 2, 128), (3 * q + 2, 2 * q + 1, 1, 384)):
                        for n_pass, (vv, ww) in enumerate(((v_hi, hi), (v_hi, lo), (v_lo, hi))):
                            last = pe.matmul(pm[:, b, off:off + ng * w], vv[:, c * P:(c + 1) * P],
                                             ww[:, g:g + ng, :], start=n_pass == 0, stop=n_pass == 2)
                    last.then_inc(pm_ready[b], 1)

            def u_slot(i, par, prod_n):
                product("U", par, prod_n, W0["U"] + 2 * prod_n + par, par, h1_hi, h1_lo, SPLIT["H1"])

            u_slot(0, 0, 0)
            transposes(0, 0, 0)
            with pe.Fori(0, 4) as i:
                for h in range(2):
                    n = 2 * i + h + 1
                    u_slot(n, (h + 1) % 2, i + (h + 1) // 2)
                    transposes(n, 2 + 4 * (n - 1), 1 + 3 * (n - 1))
                    mixing(n - 1, 4 * n, 1 + 3 * (n - 1) , CHUNK, wm_hi, wm_lo) if False else \
                        mixing(n - 1, 4 * n, 3 * n - 1, CHUNK, wm_hi, wm_lo)
            u_slot(9, 1, 4)
            mixing(8, 4 * 8 + 2, 3 * 8 + 1, NS, ws_hi, ws_lo)
            u_slot(10, 0, 5)
            u_slot(11, 1, 5)

            with pe.Fori(0, 2) as i:
                for unit in range(6):
                    pe.wait_ge(w_ready, W0["B"] + 6 * i + unit + 1)
                    for n in range(UNIT):
                        m, k = divmod(unit * UNIT + n, KB)
                        if k == 0:
                            free("B", m % 2, 2 * i + m // 2)
                        pe.wait_ge(lo_ready, SPLIT["GB"] + k + 1)
                        first, last = tile_product(m % 2, unit % 2, n, gb_hi, gb_lo, k, k == 0, k == KB - 1)
                        if n == 0:
                            first.then_inc(w_started, 1)
                        if k == KB - 1:
                            last.then_inc(psum_ready[m % 2], 1)
            inverse_rms("var", ssq_b)
            with pe.Fori(0, KD // 2) as i:
                for j in range(2):
                    product("AO", j, i, W0["AO"] + 2 * i + j, j, a_hi, a_lo, SPLIT["A"])
            with pe.Fori(0, KD // 2) as i:
                for j in range(2):
                    product("O", j, i, W0["O"] + 2 * i + j, j, m_hi, m_lo, SPLIT["M"])
            inverse_rms("norm2", ssq)

            with pe.Fori(0, NG) as g:
                per = (FG + KD) // 2
                for j in range(FG):
                    product("F", j % 2, per * g + j // 2, W0["F"] + 8 * g + j, j % 2, h2_hi, h2_lo, SPLIT["H2"])
                for m in range(KD):
                    free("F", m % 2, per * g + (FG + m) // 2)
                    if m % 2 == 0:
                        pe.wait_ge(w_ready, W0["F"] + 8 * g + FG + m // 2 + 1)
                    for k in range(FG):
                        pe.wait_ge(lo_ready, SPLIT["F"] + FG * g + k + 1)
                        first, last = tile_product(m % 2, (m // 2) % 2, (m % 2) * FG + k, f_hi, f_lo, k, k == 0, k == FG - 1)
                        if m % 2 == 0 and k == 0:
                            first.then_inc(w_started, 1)
                    last.then_inc(psum_ready[m % 2], 1)

            for m in range(KD):
                unit = m * KP // UNIT
                free("PE", m % 2, m // 2)
                pe.wait_ge(w_ready, W0["PE"] + unit + 1)
                for k in range(KP):
                    pe.wait_ge(lo_ready, SPLIT["P"] + k + 1)
                    first, last = tile_product(m % 2, unit % 2, (m * KP + k) % UNIT, p_hi, p_lo, k, k == 0, k == KP - 1)
                    if (m * KP + k) % UNIT == 0:
                        first.then_inc(w_started, 1)
                last.then_inc(psum_ready[m % 2], 1)
            inverse_rms("norm3", ssq)
            with pe.Fori(0, KD // 2) as i:
                for j in range(2):
                    product("G", j, i, W0["G"] + 2 * i + j, j, h3_hi, h3_lo, SPLIT["H3"])
            inverse_rms("norm4", ssq)

        @block.scalar
        def _(act):
            for i in (1, 3):
                act.dma_start(x1[:, 2 * i:2 * i + 2, :], io["xT"][2 * i:2 * i + 2].rearrange("k p t -> p k t"))\
                    .then_inc(x_loaded[i], 16)
            act.dma_start(cols[:, 0:N_BIN + 7 * KD], io["cols"]).then_inc(const_loaded, 16)
            act.dma_start(taps[:, :, :], io["taps"]).then_inc(const_loaded, 16)
            act.dma_start(wm_raw[:, 0, 0:GROUPS * CHUNK], io["wsT"].rearrange("s g t -> s (g t)")).then_inc(wm_loaded, 16)
            act.wait_ge(ws_zero, 1)
            m2 = ws_raw[:, 0, 0:GROUPS * NS].rearrange("p (g t) -> p g t", g=GROUPS)
            for b in range(DEC_B):
                act.dma_start(m2[b * DEC_S:(b + 1) * DEC_S, :, b * DEC_S:(b + 1) * DEC_S],
                              io["wsT"][0:DEC_S, :, 0:DEC_S]).then_inc(wm_loaded, 16)
            act.dma_start(hist[:, :, 0:HIST], io["state"]).then_inc(tab_loaded, 16)
            act.dma_start(lnv_g[:, :], io["lnv_g"].partition_broadcast(P)).then_inc(tab_loaded, 16)
            act.dma_start(lnv_b[:, :], io["lnv_b"].partition_broadcast(P)).then_inc(tab_loaded, 16)

            def squares(norm, src, dst):
                with act.Fori(0, KD // 2) as i:
                    for s in range(2):
                        k = 2 * i + s
                        act.wait_ge(ssq_done, 10 * NORM[norm] + k + 1)
                        act.activation(dst[:, s, :], row(src, k), ACT.Square).then_inc(sq_done, 1)

            def high_parts(name, n, src, dst, base_val):
                with act.Fori(0, n // 2) as i:
                    for s in range(2):
                        act.wait_ge(val_ready, base_val + 2 * i + s + 1)
                        act.activation(row(dst, 2 * i + s), src[:, s, :], ACT.Copy).then_inc(hi_ready, 1)

            def root(norm):
                act.wait_ge(tok_ready, NORM[norm] + 1)
                act.activation(tok[:, 1, 0:N_TOK], tok[:, 0, 0:N_TOK], ACT.Sqrt, scale=float(D * D)).then_inc(rms_ready, 1)

            for k in range(KD):
                if k % 2 == 0:
                    act.wait_ge(x_loaded[k // 2], 16)
                act.wait_ge(ssq_done, k + 1)
                act.activation(val[:, k % 2, :], x1[:, k, :], ACT.Square).then_inc(sq_done, 1)
            root("norm1")
            high_parts("H1", KD, val, h1_hi, 0)
            act.wait_ge(const_loaded, 32)

            def glu_and_gates(i, first):
                act.wait_ge(glu_done, i + 1)
                ready(act, "A", 0, 2 * i)
                act.activation(pieces(sig[:, 0, :]), bank(0), ACT.Sigmoid, bias=col(B_GATE, i)).then_inc(psum_free[0], 1)
                ready(act, "A", 1, 2 * i)
                act.activation(pieces(lin[:, 0, :]), bank(1), ACT.Identity, bias=col(B_LIN, i)).then_inc(psum_free[1], 1)
                for s, (bias, dst) in enumerate(((B_GA, sA_d), (B_GB, sB_d))):
                    ready(act, "A", s, 2 * i + 1)
                    act.activation(pieces(gate_st[:, s, :]), bank(s), ACT.Sigmoid, bias=col(bias, i)).then_inc(psum_free[s], 1)
                    out = drow(dst, i if first else act.snap(i))
                    act.wait_ge(psum_free[s], JOB["A"][s] + 2 * i + 2 + s)
                    act.dma_start(out, gate_st[:, s, :]).then_inc(gate_stored[s], 16)
                if not first:
                    out = drow(conv_d, act.snap(i - 1))
                    act.wait_ge(conv_done, i)
                    act.dma_start(out, conv_out[:, :]).then_inc(conv_stored, 16)
                for s in range(2):
                    act.wait_ge(gate_stored[s], 16 * (i + 1))

            glu_and_gates(0, True)
            with act.Fori(1, KD) as i:
                glu_and_gates(i, False)

            def v_pair(i):
                for s in range(2):
                    ready(act, "V", s, i)
                    act.activation(pieces(row(vt, 2 * i + s)), bank(s), ACT.Gelu_apprx_tanh, bias=col(B_V, 2 * i + s))\
                        .then_inc(psum_free[s], 1)

            act.wait_ge(glu_done, KD + 1)
            v_pair(0)
            act.wait_ge(conv_done, KD)
            act.dma_start(conv_d[KD - 1], conv_out[:, :]).then_inc(conv_stored, 16)
            act.dma_start(io["conv_sample"], hist[:, :, DEC_S:HIST + DEC_S]).then_inc(hist_stored, 16)
            act.dma_start(io["conv_prompt"], conv_tail[:, :, :]).then_inc(tail_stored, 16)
            act.wait_ge(conv_stored, 16 * (KD + 1))
            with act.Fori(1, KD // 2 + 1) as i:
                for s in range(2):
                    src = drow(conv_d, act.snap(2 * i - 2 + s))
                    act.wait_ge(conv_sum, 2 * i - 1)
                    act.dma_start(conv_in[:, s, :], src).then_inc(conv_back[s], 16)
                v_pair(i)
            act.wait_ge(conv_sum, 1 + KD)
            act.wait_ge(hist_stored, 16)
            act.wait_ge(tail_stored, 16)
            act.dma_start(bs_p[:, :, :].rearrange("p g t -> p (g t)"), io["bs_p"].partition_broadcast(P)).then_inc(bs_loaded, 16)
            act.dma_start(bs_s[:, :, :].rearrange("p g t -> p (g t)"), io["bs_s"].partition_broadcast(P)).then_inc(bs_loaded, 16)
            v_pair(KB // 2 - 1)
            ready(act, "mean", 0, 0)
            act.activation(pieces(conv_mean[:, 0, :]), bank(0), ACT.Identity).then_inc(psum_free[0], 1)

            def u_out(j, par, n):
                ready(act, "U", par, n)
                act.wait_ge(u_stored, 16 * j) if not (isinstance(j, int) and j == 0) else None
                act.activation(pieces(u_st[:, 0, :]), bank(par), ACT.Gelu_apprx_tanh, bias=col(B_U, j)).then_inc(psum_free[par], 1)
                out = drow(u_d, j if isinstance(j, int) else act.snap(j))
                act.wait_ge(psum_free[par], JOB["U"][par] + n + 1 + par)
                act.dma_start(out, u_st[:, 0, :]).then_inc(u_stored, 16)

            def tokens_major(n, b0, b1):
                if not (isinstance(n, int) and n == 0):
                    act.wait_ge(vlo_done, n)
                for g in range(3):
                    b = g % 2
                    act.wait_ge(pm_ready[b], (b0 + g // 2 if b == 0 else b1) + 1)
                    act.activation(v_tok[:, g * 512:(g + 1) * 512], pm[:, b, :], ACT.Copy).then_inc(pm_free[b], 1)

            def v_high(n):
                act.wait_ge(ln_step, LN_STEPS * n + 6)
                act.activation(rs_v[:, :], rs_v[:, :], ACT.Sqrt).then_inc(rs_ready, 1)
                act.wait_ge(ln_step, LN_STEPS * (n + 1))
                act.activation(v_hi[:, :], v_tok[:, :], ACT.Copy).then_inc(vhi_done, 1)

            u_out(0, 0, 0)
            tokens_major(0, 0, 0)
            v_high(0)

            def chunk(n, par, product_n):
                u_out(n, par, product_n)
                tokens_major(n, 2 + 4 * (n - 1), 1 + 3 * (n - 1))
                v_high(n)

            with act.Fori(0, 3) as i:
                chunk(2 * i + 1, 1, i)
                chunk(2 * i + 2, 0, i + 1)
            chunk(N_CHUNKS - 1, 1, 3)
            act.wait_ge(vlo_done, N_CHUNKS)
            act.dma_start(io["v_prompt"], v_tok[:, :]).then_inc(vout, 16)
            act.wait_ge(vout, 16)
            chunk(N_CHUNKS, 0, 4)
            act.wait_ge(vlo_done, 9)
            act.dma_start(io["v_sample"], v_tok[0:NS, :]).then_inc(vout, 16)
            u_out(9, 1, 4)
            u_out(10, 0, 5)
            u_out(11, 1, 5)

            act.wait_ge(vout, 32)
            act.wait_ge(pm_free[1], PM1_END)
            act.wait_ge(pm_free[0], PM0_END)
            act.wait_ge(u_stored, 16 * KB)
            for q in range(3):
                act.dma_start(gb[:, 4 * q:4 * q + 4, :], u_d[4 * q:4 * q + 4].rearrange("k p t -> p k t")).then_inc(u_back, 16)
                act.wait_ge(u_back, 16 * (q + 1))
            with act.Fori(0, KB) as k:
                act.wait_ge(val_ready, KD + k + 1)
                act.activation(row(gb_hi, k), row(gb, k), ACT.Copy).then_inc(hi_ready, 1)

            act.wait_ge(lo_ready, SPLIT["GB"] + KB)
            act.wait_ge(mean_copied, 1)
            act.dma_start(xc[:, :, :], conv_d.rearrange("k p t -> p k t")).then_inc(xc_loaded, 16)
            with act.Fori(0, KD // 2) as i:
                for s in range(2):
                    m = 2 * i + s
                    src = drow(sB_d, act.snap(m))
                    act.wait_ge(gated, m + 1)
                    act.dma_start(sB_st[:, 0, :], src).then_inc(sB_loaded, 16)
                    act.wait_ge(xc_done, m + 1)
                    act.wait_ge(ssq_done, 10 * NORM["var"] + 2 + m)
                    act.activation(sq_b[:, 0, :], row(xc, m), ACT.Square).then_inc(sq_done, 1)

            root("var")
            with act.Fori(0, KD) as k:
                act.wait_ge(norm_y, k + 1)
                act.activation(row(xc, k), row(xc, k), ACT.Silu, bias=col(LNA_B, k), scale=col(LNA_G, k)).then_inc(silu_done, 1)
                act.wait_ge(silu_done, k + 1)
                act.activation(row(a_hi, k), row(xc, k), ACT.Copy).then_inc(hi_ready, 1)
            with act.Fori(0, KD // 2) as i:
                for s in range(2):
                    m = 2 * i + s
                    src = drow(sA_d, act.snap(m))
                    act.wait_ge(lo_ready, SPLIT["A"] + KD)
                    act.wait_ge(gated, KD + 1 + m)
                    act.dma_start(stage[:, 1, :], src).then_inc(st_loaded[0], 16)
                    act.wait_ge(mix_done, m + 1)
                    act.activation(row(m_hi, m), row(mix, m), ACT.Copy).then_inc(hi_ready, 1)
            with act.Fori(0, KD // 2) as i:
                for s in range(2):
                    m = 2 * i + s
                    src = drow(io["xT"], act.snap(m))
                    act.wait_ge(x_done, m + 1)
                    act.dma_start(stage[:, 1, :], src).then_inc(st_loaded[1], 16)
            squares("norm2", x, val)
            root("norm2")
            high_parts("H2", KD, val, h2_hi, KD + KB)

            act.dma_start(p_raw[:, :, :], io["pT"].rearrange("k p t -> p k t")).then_inc(p_loaded, 16)
            with act.Fori(0, NG) as g:
                per = (FG + KD) // 2
                for j in range(FG):
                    ready(act, "F", j % 2, per * g + j // 2)
                    act.activation(pieces(relu[:, 0, :]), bank(j % 2), ACT.Relu).then_inc(psum_free[j % 2], 1)
                    act.wait_ge(psum_free[j % 2], JOB["F"][j % 2] + per * g + j // 2 + 1 + j % 2)
                    act.activation(f_hi[:, j, :], relu[:, 0, :], ACT.Square).then_inc(sq_f, 1)
                    act.wait_ge(lo_ready, SPLIT["F"] + FG * g + j - 1)
                    act.activation(val[:, j % 2, :], relu[:, 0, :], ACT.Square).then_inc(hi_ready, 1)
                    act.wait_ge(hi_ready, SPLIT["F"] + FG * g + j + 1)
            act.wait_ge(p_loaded, 16)
            for k in range(KP):
                act.activation(p_hi[:, k, :], p_raw[:, k, :], ACT.Copy).then_inc(hi_ready, 1)
            act.wait_ge(psum_free[0], JOB["PE"][0])
            act.wait_ge(psum_free[1], JOB["PE"][1] + 1)
            squares("norm3", x, val)
            root("norm3")
            high_parts("H3", KD, val, h3_hi, KD + KB + KD)
            with act.Fori(0, KD // 2) as i:
                for s in range(2):
                    m = 2 * i + s
                    ready(act, "G", s, i)
                    act.wait_ge(g_mul, 2 * i + s + 1)
                    act.activation(pieces(val[:, s, :]), bank(s), ACT.Sigmoid, bias=col(B_PLE, m)).then_inc(psum_free[s], 1)
            act.wait_ge(x_done, 1 + KD + KD)
            squares("norm4", x, val)
            root("norm4")
            with act.Fori(0, KD // 2) as i:
                for s in range(2):
                    out = drow(io["y"], act.snap(2 * i + s))
                    act.wait_ge(y_ready, 2 * i + s + 1)
                    act.dma_start(out, val[:, s, :]).then_inc(y_stored[s], 16)
            for s in range(2):
                act.wait_ge(y_stored[s], 16 * (KD // 2 + 1))

        @block.vector
        def _(dve):
            dve.memset(ones[:, :], 1.0 / D).then_inc(ones_set, 1)
            dve.sem_inc(psum_free[1], 1)
            dve.sem_inc(conv_stored, 16)

            def sum_rows(norm, src):
                dve.memset(ssq[:, 0, :], 0.0).then_inc(ssq_done, 2)
                b = 10 * NORM[norm]
                with dve.Fori(0, KD // 2) as i:
                    for s in range(2):
                        dve.wait_ge(sq_done, KD * NORM[norm] + 2 * i + s + 1)
                        dve.wait_ge(ssq_done, b + 2 + 2 * i + s)
                        dve.tensor_tensor(ssq[:, 0, :], ssq[:, 0, :], src[:, s, :], ALU.add).then_inc(ssq_done, 1)

            def inverse_root(stage_name, dst):
                n = NORM[stage_name]
                ready(dve, stage_name, 0, 0)
                dve.tensor_scalar(tok[:, 0, 0:N_TOK], ps[:, 0, 0, 0:N_TOK], EPS, None, ALU.add).then_inc(psum_free[0], 1)
                dve.wait_ge(psum_free[0], JOB[stage_name][0] + 1)
                dve.reciprocal(tok[:, 0, 0:N_TOK], tok[:, 0, 0:N_TOK]).then_inc(tok_ready, 1)
                dve.wait_ge(rms_ready, n + 1)
                full = SEQ // P
                dve.tensor_tensor(diag[:, 0, 0:SEQ].rearrange("p (c t) -> p c t", c=full),
                                  ident[:, :].unsqueeze(1).to_broadcast([P, full, P]),
                                  tok[:, 1, 0:full].unsqueeze(2).to_broadcast([P, full, P]), ALU.mult).then_inc(diag_ready, 1)
                dve.tensor_scalar(diag[:, 0, SEQ:T], ident[:, P - NS:P], tok[:, 1, full:full + 1], None, ALU.mult)\
                    .then_inc(diag_ready, 1)
                ready(dve, stage_name, 0, 1)
                dve.tensor_copy(pieces(dst[:, 0, :]), bank(0)).then_inc(psum_free[0], 1)
                dve.wait_ge(psum_free[0], JOB[stage_name][0] + 2)

            def normalise(name, src, gain, lo, hi, base_val):
                with dve.Fori(0, KD // 2) as i:
                    for s in range(2):
                        dve.scalar_tensor_tensor(out=val[:, s, :], in0=row(src, 2 * i + s), scalar=col(gain, 2 * i + s),
                                                 in1=rstd[:, 0, :], op0=ALU.mult, op1=ALU.mult).then_inc(val_ready, 1)
                    for s in range(2):
                        dve.wait_ge(hi_ready, SPLIT[name] + 2 * i + s + 1)
                        dve.tensor_tensor(row(lo, 2 * i + s), val[:, s, :], row(hi, 2 * i + s).bitcast(F32),
                                          ALU.subtract).then_inc(lo_ready, 1)
                    dve.wait_ge(lo_ready, SPLIT[name] + 2 * i + 2)

            sum_rows("norm1", val)
            dve.wait_ge(ident_set, 2)
            inverse_root("norm1", rstd)
            dve.wait_ge(const_loaded, 32)
            normalise("H1", x1, G_MIX, h1_lo, h1_hi, 0)

            dve.memset(glu[:, 0:HIST], 0.0).then_inc(glu_done, 1)
            dve.wait_ge(tab_loaded, 48)

            with dve.Fori(0, KD) as i:
                step = CONV_STEPS * i
                dve.tensor_copy(tap[:, :], taps[:, bass.ds(i, 1), :].rearrange("p a n -> p (a n)")).then_inc(tap_set, 1)
                dve.wait_ge(psum_free[1], JOB["A"][1] + 2 * i + 2)
                dve.tensor_tensor(glu[:, HIST:HIST + T], lin[:, 0, :], sig[:, 0, :], ALU.mult).then_inc(glu_done, 1)
                dve.wait_ge(glu_done, i + 2)
                dve.wait_ge(tap_set, i + 1)
                new = glu[:, HIST + SEQ:HIST + T].rearrange("p (b t) -> p b t", b=DEC_B)
                h_i = hist[:, bass.ds(DEC_B * i, DEC_B), :]
                dve.tensor_copy(h_i[:, :, HIST:HIST + DEC_S], new).then_inc(conv_step, 1)
                dve.tensor_copy(conv_tail[:, bass.ds(i, 1), :].rearrange("p a n -> p (a n)"),
                                glu[:, SEQ:SEQ + HIST]).then_inc(conv_step, 1)
                dve.tensor_scalar(acc0[:, :], glu[:, 0:SEQ], tap[:, 0:1], tap[:, TAPS:TAPS + 1], ALU.mult, ALU.add)\
                    .then_inc(conv_step, 1)
                dve.tensor_scalar(acc1[:, :], glu[:, 1:1 + SEQ], tap[:, 1:2], None, ALU.mult).then_inc(conv_step, 1)
                for j in range(2, TAPS):
                    acc = acc0 if j % 2 == 0 else acc1
                    dve.wait_ge(conv_step, step + 2 + j - 1)
                    dve.scalar_tensor_tensor(out=acc[:, :], in0=glu[:, j:j + SEQ], scalar=tap[:, j:j + 1], in1=acc[:, :],
                                             op0=ALU.mult, op1=ALU.add).then_inc(conv_step, 1)
                w = tap[:, 0:TAPS].unsqueeze(1).to_broadcast([P, DEC_B, TAPS])
                for t in range(DEC_S):
                    dve.tensor_tensor(prod[:, t, :, :], h_i[:, :, t:t + TAPS], w, ALU.mult).then_inc(conv_step, 1)
                dve.wait_ge(conv_step, step + 2 + TAPS + DEC_S)
                dve.tensor_reduce(samp[:, :].rearrange("p (t b) -> p t b", t=DEC_S), prod[:, :, :, :], AX_X, ALU.add)\
                    .then_inc(conv_step, 1)
                dve.wait_ge(conv_step, step + CONV_STEPS)
                dve.wait_ge(conv_stored, 16 * i + 16)
                dve.tensor_scalar(conv_out[:, SEQ:T].rearrange("p (b t) -> p t b", b=DEC_B),
                                  samp[:, :].rearrange("p (t b) -> p t b", t=DEC_S), tap[:, TAPS:TAPS + 1], None, ALU.add)
                dve.tensor_tensor(conv_out[:, 0:SEQ], acc0[:, :], acc1[:, :], ALU.add).then_inc(conv_done, 1)
                dve.wait_ge(conv_done, i + 1)

            dve.memset(conv_mean[:, 0, :], 0.0).then_inc(conv_sum, 1)
            with dve.Fori(0, KD // 2) as i:
                for s in range(2):
                    dve.wait_ge(conv_back[s], 16 * (i + 1))
                    dve.wait_ge(conv_sum, 2 * i + s + 1)
                    dve.tensor_tensor(conv_mean[:, 0, :], conv_mean[:, 0, :], conv_in[:, s, :], ALU.add).then_inc(conv_sum, 1)

            dve.wait_ge(psum_free[1], JOB["U"][1] + 1)
            dve.wait_ge(psum_free[0], JOB["mean"][0])
            dve.wait_ge(bs_loaded, 32)

            def take_chunk(n, w):
                if not (isinstance(n, int) and n == 0):
                    dve.wait_ge(pm_ready[0], 4 * n - 2)
                src = vt[:, :, bass.ds(n * CHUNK, w)]
                dve.tensor_copy(v_chunk[:, :, 0:w], src).then_inc(vc_done, 1)

            def layer_norm(n, b0, b1):
                s = LN_STEPS * n
                dve.wait_ge(pm_free[0], b0 + 2)
                dve.wait_ge(pm_free[1], b1 + 1)
                for g in range(3):
                    dve.bn_stats(stats[:, g, :], v_tok[:, g * 512:(g + 1) * 512]).then_inc(ln_step, 1)
                dve.wait_ge(ln_step, s + 3)
                dve.memset(rs_v[:, :], EPS)
                dve.bn_aggr(mv[:, :], stats[:, :, :]).then_inc(ln_step, 1)
                dve.wait_ge(ln_step, s + 4)
                dve.tensor_tensor(rs_v[:, :], rs_v[:, :], mv[:, 1:2], ALU.add).then_inc(ln_step, 1)
                dve.wait_ge(ln_step, s + 5)
                dve.reciprocal(rs_v[:, :], rs_v[:, :]).then_inc(ln_step, 1)
                dve.wait_ge(rs_ready, n + 1)
                dve.tensor_scalar(v_tok[:, :], v_tok[:, :], mv[:, 0:1], rs_v[:, 0:1], ALU.subtract, ALU.mult).then_inc(ln_step, 1)
                dve.wait_ge(ln_step, s + 7)
                dve.tensor_tensor(v_tok[:, :], v_tok[:, :], lnv_g[:, :], ALU.mult).then_inc(ln_step, 1)
                dve.wait_ge(ln_step, s + 8)
                dve.tensor_tensor(v_tok[:, :], v_tok[:, :], lnv_b[:, :], ALU.add).then_inc(ln_step, 1)
                dve.wait_ge(ln_step, s + 9)
                dve.wait_ge(vhi_done, n + 1)
                dve.tensor_tensor(v_lo[:, :], v_tok[:, :], v_hi[:, :].bitcast(F32), ALU.subtract).then_inc(vlo_done, 1)

            def mixed_out(n, b0, b1, w, bs):
                for q in range(4):
                    b = (q + 1) % 2
                    dve.wait_ge(pm_ready[b], (b0 if b == 0 else b1) + q // 2 + 1)
                    for c, p0, p1, off, g in ((0, 0, P, 0, 0), (1, 0, 64, 128, 0), (1, 64, P, 128 + w, 1), (2, 0, P, 384, 1)):
                        dst = vt[p0:p1, 3 * q + c, bass.ds(n * CHUNK, w)]
                        last = dve.tensor_tensor(dst, pm[p0:p1, b, off:off + w], bs[p0:p1, 2 * q + g, :], ALU.add)
                    last.then_inc(pm_free[b], 1)

            take_chunk(0, CHUNK)
            layer_norm(0, 0, 0)
            with dve.Fori(1, N_CHUNKS) as n:
                take_chunk(n, CHUNK)
                mixed_out(n - 1, 4 * n, 3 * n - 1, CHUNK, bs_p)
                layer_norm(n, 4 * n - 2, 3 * n - 2)
            n = N_CHUNKS
            take_chunk(n, NS)
            mixed_out(n - 1, 4 * n, 3 * n - 1, CHUNK, bs_p)
            layer_norm(n, 4 * n - 2, 3 * n - 2)
            mixed_out(n, 4 * n + 2, 3 * n + 1, NS, bs_s)

            dve.wait_ge(pm_free[0], PM0_END)
            dve.wait_ge(pm_free[1], PM1_END)
            for q in range(3):
                dve.wait_ge(u_back, 16 * (q + 1))
                with dve.Fori(4 * q, 4 * q + 4) as k:
                    dve.tensor_tensor(row(gb, k), row(gb, k), row(vt, k), ALU.mult).then_inc(val_ready, 1)
            ready(dve, "U", 1, KB // 2 - 1)
            with dve.Fori(0, KB) as k:
                dve.wait_ge(hi_ready, SPLIT["GB"] + k + 1)
                dve.tensor_tensor(row(gb_lo, k), row(gb, k), row(gb_hi, k).bitcast(F32), ALU.subtract).then_inc(lo_ready, 1)
            dve.tensor_copy(mean_b[:, 0, :], conv_mean[:, 0, :]).then_inc(mean_copied, 1)
            dve.memset(ssq_b[:, 0, :], 0.0).then_inc(ssq_done, 2)
            dve.sem_inc(gated, 1)
            dve.wait_ge(mean_copied, 1)
            dve.wait_ge(xc_loaded, 16)
            with dve.Fori(0, KD // 2) as i:
                for s in range(2):
                    m = 2 * i + s
                    dve.tensor_tensor(row(xc, m), row(xc, m), mean_b[:, 0, :], ALU.subtract).then_inc(xc_done, 1)
                    ready(dve, "B", s, i)
                    dve.wait_ge(sB_loaded, 16 * (m + 1))
                    dve.tensor_tensor(pieces(row(mix, m)), bank(s), pieces(sB_st[:, 0, :]), ALU.mult).then_inc(psum_free[s], 1)
                    dve.wait_ge(psum_free[s], JOB["B"][s] + i + 1 + s)
                    dve.wait_ge(sq_done, KD * NORM["var"] + m + 1)
                    dve.wait_ge(ssq_done, 10 * NORM["var"] + 2 + m)
                    dve.tensor_tensor(ssq_b[:, 0, :], ssq_b[:, 0, :], sq_b[:, 0, :], ALU.add).then_inc(ssq_done, 1)
                    dve.sem_inc(gated, 1)

            inverse_root("var", rstd)
            with dve.Fori(0, KD) as k:
                dve.tensor_tensor(row(xc, k), row(xc, k), rstd[:, 0, :], ALU.mult).then_inc(norm_y, 1)
            with dve.Fori(0, KD) as k:
                dve.wait_ge(hi_ready, SPLIT["A"] + k + 1)
                dve.tensor_tensor(row(a_lo, k), row(xc, k), row(a_hi, k).bitcast(F32), ALU.subtract).then_inc(lo_ready, 1)
            with dve.Fori(0, KD // 2) as i:
                for s in range(2):
                    m = 2 * i + s
                    ready(dve, "AO", s, i)
                    dve.wait_ge(st_loaded[0], 16 * (m + 1))
                    dve.tensor_tensor(pieces(val[:, s, :]), bank(s), pieces(stage[:, 1, :]), ALU.mult).then_inc(psum_free[s], 1)
                    dve.wait_ge(psum_free[s], JOB["AO"][s] + i + 1 + s)
                    dve.sem_inc(gated, 1)
                    dve.tensor_tensor(row(mix, m), row(mix, m), val[:, s, :], ALU.add).then_inc(mix_done, 1)
                    dve.wait_ge(hi_ready, SPLIT["M"] + m + 1)
                    dve.tensor_tensor(row(m_lo, m), row(mix, m), row(m_hi, m).bitcast(F32), ALU.subtract).then_inc(lo_ready, 1)
            dve.wait_ge(lo_ready, SPLIT["M"] + KD)
            dve.sem_inc(x_done, 1)
            with dve.Fori(0, KD // 2) as i:
                for s in range(2):
                    m = 2 * i + s
                    ready(dve, "O", s, i)
                    dve.wait_ge(st_loaded[1], 16 * (m + 1))
                    dve.tensor_tensor(pieces(row(x, m)), bank(s), pieces(stage[:, 1, :]), ALU.add).then_inc(psum_free[s], 1)
                    dve.wait_ge(psum_free[s], JOB["O"][s] + i + 1 + s)
                    dve.sem_inc(x_done, 1)
            sum_rows("norm2", val)
            inverse_root("norm2", rstd)
            normalise("H2", x, G_FFN, h2_lo, h2_hi, 0)

            with dve.Fori(0, NG) as g:
                per = (FG + KD) // 2
                for j in range(FG):
                    dve.wait_ge(hi_ready, SPLIT["F"] + FG * g + j + 1)
                    dve.tensor_tensor(f_lo[:, j, :], val[:, j % 2, :], f_hi[:, j, :].bitcast(F32), ALU.subtract)\
                        .then_inc(lo_ready, 1)
                for m in range(KD):
                    ready(dve, "F", m % 2, per * g + (FG + m) // 2)
                    dve.tensor_tensor(pieces(x[:, m, :]), bank(m % 2), pieces(x[:, m, :]), ALU.add).then_inc(psum_free[m % 2], 1)
            for k in range(KP):
                dve.wait_ge(hi_ready, SPLIT["P"] + k + 1)
                dve.tensor_tensor(p_lo[:, k, :], p_raw[:, k, :], p_hi[:, k, :].bitcast(F32), ALU.subtract).then_inc(lo_ready, 1)
            sum_rows("norm3", val)
            with dve.Fori(0, KD // 2) as i:
                for s in range(2):
                    ready(dve, "PE", s, i)
                    dve.tensor_copy(pieces(row(pe_out, 2 * i + s)), bank(s)).then_inc(psum_free[s], 1)
            inverse_root("norm3", rstd)
            normalise("H3", x, G_PLE, h3_lo, h3_hi, 0)
            dve.sem_inc(g_mul, 2)
            with dve.Fori(0, KD // 2) as i:
                for s in range(2):
                    m = 2 * i + s
                    dve.wait_ge(psum_free[s], JOB["G"][s] + i + 1 + s)
                    dve.tensor_tensor(row(pe_out, m), row(pe_out, m), val[:, s, :], ALU.mult).then_inc(g_mul, 1)
                    dve.wait_ge(g_mul, m + 3)
                    dve.tensor_tensor(row(x, m), row(x, m), row(pe_out, m), ALU.add).then_inc(x_done, 1)
            sum_rows("norm4", val)
            inverse_root("norm4", rstd)
            for s in range(2):
                dve.sem_inc(y_stored[s], 16)
            with dve.Fori(0, KD // 2) as i:
                for s in range(2):
                    dve.wait_ge(y_stored[s], 16 * (i + 1))
                    dve.scalar_tensor_tensor(out=val[:, s, :], in0=row(x, 2 * i + s), scalar=col(G_FIN, 2 * i + s),
                                             in1=rstd[:, 0, :], op0=ALU.mult, op1=ALU.mult).then_inc(y_ready, 1)


LN_STEPS = 9
CONV_STEPS = 2 + TAPS + DEC_S + 1
PM0_END = 4 * (N_CHUNKS + 1)
PM1_END = 3 * (N_CHUNKS + 1)


def kernel(**inputs):
    import numpy as np
    import concourse.bacc as bacc
    from concourse.bass_utils import run_bass_kernel_spmd

    a = {k: np.asarray(v) for k, v in inputs.items()}

    def tokens(prompt, sample, k):
        both = np.concatenate([prompt.reshape(SEQ, -1), sample.reshape(NS, -1)], axis=0)
        return np.ascontiguousarray(both.T).reshape(k, P, T)

    def by_output(w):
        k, n = w.shape[0] // P, w.shape[1] // P
        return w.reshape(k, P, n, P).transpose(2, 1, 0, 3).reshape(n, P, k * P)

    def by_tile(w):
        return w.reshape(w.shape[0] // P, P, w.shape[1] // P, P).transpose(2, 0, 1, 3)

    def packed(tiles):
        return tiles.reshape(-1, UNIT, P, P).transpose(0, 2, 1, 3).reshape(-1, P, UNIT * P)

    w_in = by_output(a["w_in"][0])
    order = [b + m for m in range(KD) for b in (B_GATE, B_LIN, B_GA, B_GB)]
    order += [B_V + m for m in range(KB)] + [B_U + m for m in range(KB)]
    ff1 = by_output(a["w_ff1"][0]).reshape(NG, FG, P, UNIT * P)
    ff2 = np.stack([packed(by_tile(a["w_ff2"][0][g * FG * P:(g + 1) * FG * P])) for g in range(NG)])
    weights = np.concatenate([
        w_in[order], packed(by_tile(a["w_b_out"][0])), by_output(a["w_a_out"][0]), by_output(a["w_o"][0]),
        np.concatenate([ff1, ff2], axis=1).reshape(-1, P, UNIT * P),
        packed(by_tile(a["w_ple"][0])), by_output(a["w_ple_gate"][0])])

    def column(v):
        return v.reshape(-1, P).T

    arrays = {
        "xT": tokens(a["x_prompt"], a["x_sample"], KD),
        "pT": tokens(a["p_prompt"][0], a["p_sample"][0], KP),
        "weights": weights,
        "cols": np.concatenate([column(v) for v in (
            a["b_in"][0], a["g_mix"][0], a["g_ffn"][0], a["g_ple"][0], a["g_final"], a["ln_a_g"][0],
            a["ln_a_b"][0], a["b_ple_gate"][0])], axis=1),
        "taps": np.concatenate([a["conv_w"][0], a["conv_b"]], axis=0).reshape(TAPS + 1, KD, P).transpose(2, 1, 0),
        "state": a["state_conv"][0].reshape(DEC_B, HIST, KD, P).transpose(3, 2, 0, 1).reshape(P, KD * DEC_B, HIST),
        "wsT": a["w_s"][0].transpose(2, 0, 1),
        "lnv_g": a["ln_v_g"][0],
        "lnv_b": a["ln_v_b"][0],
        "bs_p": a["b_s"][0].reshape(-1),
        "bs_s": np.tile(a["b_s"][0][:, None, :DEC_S], (1, DEC_B, 1)).reshape(-1),
    }
    outs = {"y": (KD, P, T), "conv_prompt": (P, KD, HIST), "conv_sample": (P, KD * DEC_B, HIST),
            "v_prompt": (CHUNK, C_B), "v_sample": (NS, C_B)}
    nc = bacc.Bacc("TRN2", target_bir_lowering=False, num_devices=1)
    io = {}
    arrays = {k: np.ascontiguousarray(v) for k, v in arrays.items()}
    for k, v in arrays.items():
        io[k] = nc.dram_tensor(k, v.shape, mybir.dt.from_np(v.dtype), kind="ExternalInput").ap()
    for k, shape in outs.items():
        io[k] = nc.dram_tensor(k, shape, F32, kind="ExternalOutput").ap()
    build(nc, io)
    r = run_bass_kernel_spmd(nc, [arrays], core_ids=[0]).results[0]
    y = r["y"].reshape(D, T).T
    conv_p = r["conv_prompt"].transpose(2, 1, 0).reshape(1, 1, HIST, D)
    conv_s = r["conv_sample"].reshape(P, KD, DEC_B, HIST).transpose(2, 3, 1, 0).reshape(1, DEC_B, HIST, D)
    return (np.ascontiguousarray(y[:SEQ]).reshape(1, SEQ, D), np.ascontiguousarray(y[SEQ:]).reshape(DEC_B, DEC_S, D),
            np.ascontiguousarray(conv_p), np.ascontiguousarray(conv_s),
            r["v_prompt"].reshape(1, 1, CHUNK, C_B), r["v_sample"].reshape(1, DEC_B, DEC_S, C_B))
```

```python
from contextlib import ExitStack

import concourse.bass as bass
from concourse import mybir

F32 = mybir.dt.float32
F32R = mybir.dt.float32r
ALU = mybir.AluOpType
ACT = mybir.ActivationFunctionType
AX_X = mybir.AxisListType.X

P = 128
D = 1024
C_B = 1536
D_FF = 4096
P_DIM = 256
SEQ = 1024
DEC_B, DEC_S = 8, 4
NS = DEC_B * DEC_S
T = SEQ + NS
CHUNK = 128
N_CHUNKS = SEQ // CHUNK
GROUPS = 8
TAPS = 31
HIST = TAPS - 1
EPS = 1e-6

KD = D // P
KB = C_B // P
KF = D_FF // P
KP = P_DIM // P
NC = 3
TC = T // NC
UNIT = 8
FG = 4
NG = KF // FG

B_LIN, B_GATE, B_U, B_V, B_GA, B_GB = 0, KD, 2 * KD, 2 * KD + KB, 2 * KD + 2 * KB, 3 * KD + 2 * KB
N_BIN = 4 * KD + 2 * KB
N_TOK = -(-T // P)

STAGES = [
    ("A", 2 * KD, 2 * KD), ("V", KB // 2, KB // 2), ("mean", 1, 0),
    ("U", KB // 2, KB // 2), ("B", KD // 2, KD // 2), ("AO", KD // 2, KD // 2),
    ("O", KD // 2, KD // 2), ("F", NG * (FG + KD) // 2, NG * (FG + KD) // 2),
    ("PE", KD // 2, KD // 2), ("G", KD // 2, KD // 2),
]
JOB = {}
_n0 = _n1 = 0
for _name, _a, _b in STAGES:
    JOB[_name] = (_n0, _n1)
    _n0 += _a
    _n1 += _b

SPLIT = {}
_n = 0
for _name, _k in (("H1", KD), ("GB", KB), ("A", KD), ("M", KD), ("H2", KD), ("P", KP), ("F", KF), ("H3", KD)):
    SPLIT[_name] = _n
    _n += _k

W0 = {}
_n = 0
for _name, _k in (("A", 4 * KD), ("V", KB), ("U", KB), ("B", KB), ("AO", KD), ("O", KD),
                  ("F", NG * 2 * FG), ("PE", KD * KP // UNIT), ("G", KD)):
    W0[_name] = _n
    _n += _k
N_UNITS = _n

Y_DVE = 5

NORM = {"norm1": 0, "var": 1, "norm2": 2, "norm3": 3, "norm4": 4}


def build(nc, io):
    ctx = ExitStack()
    with ctx:
        ROW = T * 4
        base = (nc.sbuf_base + 31) // 32 * 32

        def at(name, shape, dt, off):
            return nc.alloc_sbuf_tensor_at(name, shape, dt, offset=base + off)

        def rows(name, first, n, dt=F32):
            return at(name, [P, n, T], dt, first * ROW)

        h1_hi, h1_lo = rows("h1_hi", 0, KD, F32R), rows("h1_lo", 8, KD, F32R)
        x1 = rows("x1", 16, KD)
        x1g_hi, x1g_lo = rows("x1g_hi", 28, KD, F32R), rows("x1g_lo", 36, KD, F32R)
        sig, lin = rows("sig", 16, 1), rows("lin", 17, 1)
        gate_st = rows("gate_st", 18, 2)
        vt = rows("vt", 16, KB)
        conv_in = rows("conv_in", 26, 2)
        t0 = 28 * ROW
        glu = at("glu", [P, HIST + T + 2], F32, t0)
        acc0 = at("acc0", [P, SEQ], F32, t0 + 4352)
        acc1 = at("acc1", [P, SEQ], F32, t0 + 8448)
        conv_out = at("conv_out", [P, T], F32, t0 + 12544)
        prod = at("prod", [P, DEC_S, DEC_B, TAPS], F32, t0 + 16768)
        v_chunk = at("v_chunk", [P, KB, CHUNK], F32, t0)
        v_tok = at("v_tok", [P, C_B], F32, t0 + 6144)
        v_hi = at("v_hi", [P, C_B], F32R, t0 + 12288)
        v_lo = at("v_lo", [P, C_B], F32R, t0 + 18432)
        lnv_g = at("lnv_g", [P, C_B], F32, t0 + 24576)
        lnv_b = at("lnv_b", [P, C_B], F32, t0 + 30720)
        wm_hi = at("wm_hi", [P, GROUPS, CHUNK], F32R, t0 + 36864)
        wm_lo = at("wm_lo", [P, GROUPS, CHUNK], F32R, t0 + 40960)
        ws_hi = at("ws_hi", [P, GROUPS, NS], F32R, t0 + 45056)
        ws_lo = at("ws_lo", [P, GROUPS, NS], F32R, t0 + 46080)
        wm_raw = rows("wm_raw", 40, 1)
        ws_raw = at("ws_raw", [P, 1, GROUPS * NS], F32, t0 + 47104)
        conv_mean = rows("conv_mean", 40, 1)
        t1 = 41 * ROW
        u_st = rows("u_st", 41, 1)
        hist = at("hist", [P, KD * DEC_B, HIST + DEC_S], F32, t1)
        conv_tail = at("conv_tail", [P, KD, HIST], F32, t1 + 8704)
        bs_p = at("bs_p", [P, GROUPS, CHUNK], F32, t1 + ROW)
        bs_s = at("bs_s", [P, GROUPS, NS], F32, t1 + ROW + 4096)
        gb = rows("gb", 28, KB)
        gb_hi, gb_lo = rows("gb_hi", 16, KB, F32R), rows("gb_lo", 28, KB, F32R)
        mix = rows("mix", 0, KD)
        xc = rows("xc", 8, KD)
        ssq_b, sB_st, sq_b = rows("ssq_b", 41, 1), rows("sB_st", 42, 1), rows("sq_b", 43, 1)
        diag_b, rstd_b = rows("diag_b", 41, 1), rows("rstd_b", 43, 1)
        a_hi, a_lo = rows("a_hi", 16, KD, F32R), rows("a_lo", 28, KD, F32R)
        sA_st = rows("sA_st", 24, 2)
        m_hi, m_lo = rows("m_hi", 8, KD, F32R), rows("m_lo", 36, KD, F32R)
        rstd, ssq, val = rows("rstd", 24, 1), rows("ssq", 25, 1), rows("val", 26, 2)
        x = rows("x", 28, KD)
        xg_hi, xg_lo = rows("xg_hi", 0, KD, F32R), rows("xg_lo", 16, KD, F32R)
        f_hi, f_lo = rows("f_hi", 8, FG, F32R), rows("f_lo", 12, FG, F32R)
        relu = rows("relu", 42, 1)
        p_raw = rows("p_raw", 36, KP)
        p_hi, p_lo = rows("p_hi", 38, KP, F32R), rows("p_lo", 40, KP, F32R)
        pe_out = rows("pe_out", 8, KD)
        sq_g = rows("sq_g", 36, 2)
        z_g = rows("z_g", 42, 2)
        y = rows("y", 0, KD)
        c0 = 44 * ROW
        w_raw = at("w_raw", [P, 2, UNIT * P], F32, c0)
        w_hi = at("w_hi", [P, 2, UNIT * P], F32R, c0 + 8192)
        w_lo = at("w_lo", [P, 2, UNIT * P], F32R, c0 + 16384)
        c1 = c0 + 24576
        ones = at("ones", [P, P], F32, c1)
        ident = at("ident", [P, P], F32, c1 + 1024)
        cols = at("cols", [P, N_BIN + 8 * KD], F32, c1 + 512)
        taps = at("taps", [P, KD, 32], F32, t1 + 9728)
        tok = at("tok", [P, 2, 16], F32, c1 + 1600)
        diag = rows("diag", 26, 1)
        tap = at("tap", [P, 32], F32, c1 + 2048)
        stats = at("stats", [P, 3, 6], F32, c1 + 2176)
        mv = at("mv", [P, 2], F32, c1 + 2272)
        rs_v = at("rs_v", [P, 2], F32, c1 + 2304)
        w_col = at("w_col", [P, 1], F32, c1 + 1728)
        samp = at("samp", [P, NS], F32, t0 + 20736)
        G_MIX, G_FFN, G_PLE, G_FIN, LNA_G, LNA_B, B_PLE = (N_BIN + KD * n for n in range(7))

        ps = ctx.enter_context(nc.psum_tensor("ps", [P, 2, NC, 512], F32))
        pm = ctx.enter_context(nc.psum_tensor("pm", [P, 2, 512], F32))

        def scratch(name, n):
            return nc.dram_tensor(name, (n, P, T), F32, kind="Internal").ap()

        sA_d, sB_d, conv_d, u_d = scratch("sA_d", KD), scratch("sB_d", KD), scratch("conv_d", KD), scratch("u_d", KB)

        def sem(name):
            return ctx.enter_context(nc.semaphore(name))

        w_loaded = [sem("w_loaded0"), sem("w_loaded1")]
        w_hi_done = sem("w_hi_done")
        w_ready = sem("w_ready")
        w_passed = sem("w_passed")
        psum_ready = [sem("psum_ready0"), sem("psum_ready1")]
        psum_free = [sem("psum_free0"), sem("psum_free1")]
        x_loaded = [sem(f"x_loaded{i}") for i in range(4)]
        const_loaded = sem("const_loaded")
        tab_loaded = sem("tab_loaded")
        wm_loaded = sem("wm_loaded")
        ones_set = sem("ones_set")
        ws_zero, wm_masked, wm_split = sem("ws_zero"), sem("wm_masked"), sem("wm_split")
        ident_set = sem("ident_set")
        tok_ready, rms_ready, diag_ready = sem("tok_ready"), sem("rms_ready"), sem("diag_ready")
        rs_ready = sem("rs_ready")
        sq_done, ssq_done = sem("sq_done"), sem("ssq_done")
        val_ready = sem("val_ready")
        hi_ready, lo_ready = sem("hi_ready"), sem("lo_ready")
        glu_done, tap_set, conv_step = sem("glu_done"), sem("tap_set"), sem("conv_step")
        conv_done, conv_stored = sem("conv_done"), sem("conv_stored")
        gate_stored = [sem("gate_stored0"), sem("gate_stored1")]
        conv_back = [sem("conv_back0"), sem("conv_back1")]
        conv_sum = sem("conv_sum")
        bs_loaded, hist_stored, tail_stored = sem("bs_loaded"), sem("hist_stored"), sem("tail_stored")
        u_stored = sem("u_stored")
        vc_done = sem("vc_done")
        pm_ready, pm_free = [sem("pm_ready0"), sem("pm_ready1")], [sem("pm_free0"), sem("pm_free1")]
        vtok_copied, ln_step = sem("vtok_copied"), sem("ln_step")
        vhi_done, vlo_done = sem("vhi_done"), sem("vlo_done")
        vout = sem("vout")
        u_back = [sem(f"u_back{i}") for i in range(3)]
        xc_loaded, xc_done = sem("xc_loaded"), sem("xc_done")
        sB_loaded = sem("sB_loaded")
        sA_loaded, x_back = [sem("sA_loaded0"), sem("sA_loaded1")], [sem("x_back0"), sem("x_back1")]
        norm_ready, norm_free = sem("norm_ready"), sem("norm_free")
        x1g_hi_done, x1g_lo_done, scaled = sem("x1g_hi_done"), sem("x1g_lo_done"), sem("scaled")
        relu_done, z_ready = sem("relu_done"), sem("z_ready")
        norm_y, silu_done, gated, mix_done = sem("norm_y"), sem("silu_done"), sem("gated"), sem("mix_done")
        v_normed, xg_done = sem("v_normed"), sem("xg_done")
        sq_f, p_loaded, sg_done, g_mul = sem("sq_f"), sem("p_loaded"), sem("sg_done"), sem("g_mul")
        x_done = sem("x_done")
        y_ready, y_pool, rstd_set, y_stored = sem("y_ready"), sem("y_pool"), sem("rstd_set"), sem("y_stored")

        block = ctx.enter_context(nc.Block())

        def pieces(ap):
            return ap.rearrange("p (c t) -> p c t", c=NC)

        def row(tile, k):
            if isinstance(k, int):
                return tile[:, k, :]
            return tile[:, bass.ds(k, 1), :].rearrange("p a t -> p (a t)")

        def drow(dram, k):
            if isinstance(k, int):
                return dram[k, :, :]
            return dram[bass.ds(k, 1), :, :].rearrange("a p t -> p (a t)")

        def col(first, k):
            if isinstance(k, int):
                return cols[:, first + k:first + k + 1]
            return cols[:, bass.ds(first + k, 1)]

        def bank(slot):
            return ps[:, slot, :, 0:TC]

        m1 = wm_raw[:, 0, 0:GROUPS * CHUNK].rearrange("p (g t) -> p g t", g=GROUPS)
        m2 = ws_raw[:, 0, 0:GROUPS * NS].rearrange("p (g t) -> p g t", g=GROUPS)

        def ready(eng, stage_name, slot, n):
            eng.wait_ge(psum_ready[slot], JOB[stage_name][slot] + n + 1)

        @block.sync
        def _(sp):
            for s in range(2):
                sp.dma_start(w_raw[:, s, :], io["weights"][s]).then_inc(w_loaded[s], 16)
                sp.dma_start(x1[:, 4 * s:4 * s + 2, :], io["xT"][4 * s:4 * s + 2].rearrange("k p t -> p k t"))\
                    .then_inc(x_loaded[2 * s], 16)
            with sp.Fori(1, N_UNITS // 2) as i:
                for s in range(2):
                    src = sp.snap(2 * i + s)
                    unit = io["weights"][bass.ds(src, 1)].rearrange("a p n -> p (a n)")
                    sp.wait_ge(w_ready, 2 * i + s - 1)
                    sp.dma_start(w_raw[:, s, :], unit).then_inc(w_loaded[s], 16)
            for k in range(Y_DVE):
                sp.wait_ge(y_ready, k + 1)
                sp.dma_start(io["y"][k], y[:, k, :]).then_inc(y_stored, 16)

        @block.gpsimd
        def _(pool):
            pool.memset(ident[:, :], 0.0).then_inc(ident_set, 1)
            pool.wait_ge(ident_set, 1)
            pool.affine_select(out=ident[:, :], in_=ident[:, :], compare_op=ALU.not_equal, fill=1.0, base=0,
                               pattern=[[-1, P]], channel_multiplier=1).then_inc(ident_set, 1)

            def split(s, n, u):
                pool.wait_ge(w_loaded[s], 16 * n)
                if not isinstance(u, int) or u > 1:
                    pool.wait_ge(w_passed, u)
                    pool.tensor_tensor(w_col[:, :], w_raw[:, s, 0:1], w_raw[:, s, 1:2], ALU.add)
                pool.tensor_copy(w_hi[:, s, :], w_raw[:, s, :]).then_inc(w_hi_done, 1)
                pool.wait_ge(w_hi_done, u + 1)
                pool.tensor_tensor(w_lo[:, s, :], w_raw[:, s, :], w_hi[:, s, :].bitcast(F32), ALU.subtract)\
                    .then_inc(w_ready, 1)

            for s in range(2):
                split(s, 1, s)
            ready(pool, "A", 0, 0)
            ready(pool, "A", 1, 0)
            pool.memset(ws_raw[:, 0, 0:GROUPS * NS], 0.0).then_inc(ws_zero, 1)
            for s in range(2):
                split(s, 2, 2 + s)
            split(0, 3, 4)
            pool.wait_ge(wm_loaded, 16 * (1 + DEC_B))
            pool.affine_select(out=m1, in_=m1, compare_op=ALU.is_ge, fill=0.0, base=0,
                               pattern=[[0, GROUPS], [1, CHUNK]], channel_multiplier=-1).then_inc(wm_masked, 1)
            pool.affine_select(out=m2, in_=m2, compare_op=ALU.is_ge, fill=0.0, base=0,
                               pattern=[[0, GROUPS], [1, NS]], channel_multiplier=-1).then_inc(wm_masked, 1)
            split(1, 3, 5)
            pool.wait_ge(wm_split, 2)
            pool.tensor_tensor(wm_lo[:, :, :], m1, wm_hi[:, :, :].bitcast(F32), ALU.subtract).then_inc(wm_split, 1)
            pool.tensor_tensor(ws_lo[:, :, :], m2, ws_hi[:, :, :].bitcast(F32), ALU.subtract).then_inc(wm_split, 1)
            with pool.Fori(3, N_UNITS // 2) as i:
                for s in range(2):
                    split(s, i + 1, 2 * i + s)
            pool.wait_ge(rstd_set, 1)
            for k in range(Y_DVE, KD):
                pool.wait_ge(xg_done, k - Y_DVE + 1)
                pool.tensor_tensor(y[:, k, :], x[:, k, :], rstd[:, 0, :], ALU.mult).then_inc(y_pool, 1)

        @block.tensor
        def _(pe):
            def free(stage_name, slot, n):
                if JOB[stage_name][slot] + slot or not isinstance(n, int) or n:
                    pe.wait_ge(psum_free[slot], JOB[stage_name][slot] + n + slot)

            def tile_product(slot, s, n, hi, lo, k, start, stop):
                first = last = None
                for w, a in ((w_hi, hi), (w_hi, lo), (w_lo, hi)):
                    for c in range(NC):
                        last = pe.matmul(ps[:, slot, c, 0:TC], w[:, s, n * P:(n + 1) * P],
                                         a[:, k, c * TC:(c + 1) * TC],
                                         start=start and w is w_hi and a is hi, stop=stop and w is w_lo)
                        if first is None:
                            first = last
                return first, last

            def product(stage_name, slot, n, u, s, hi, lo, base_k, between=()):
                free(stage_name, slot, n)
                pe.wait_ge(w_ready, u + 1)
                for k in range(KD):
                    pe.wait_ge(lo_ready, base_k + k + 1)
                    first, last = tile_product(slot, s, k, hi, lo, k, k == 0, k == KD - 1)
                    if k == 0:
                        first.then_inc(w_passed, 1)
                    if k == KD - 1:
                        last.then_inc(psum_ready[slot], 1)
                    if k in between:
                        between[k]()

            def pair(stage_name, n, u, hi, lo, lag, made, base_k, between=()):
                order = []
                for k in range(KD + lag):
                    order += [(0, k)] * (k < KD) + [(1, k - lag)] * (k >= lag)
                for at_step, (s, k) in enumerate(order):
                    if k == 0:
                        free(stage_name, s, n)
                        pe.wait_ge(w_ready, u + s + 1)
                    pe.wait_ge(made, base_k + k + 1)
                    first, last = tile_product(s, s, k, hi, lo, k, k == 0, k == KD - 1)
                    if at_step == 0 or order[at_step - 1] == (0, KD - 1):
                        first.then_inc(w_passed, 1)
                    if k == KD - 1:
                        last.then_inc(psum_ready[s], 1)
                    if (s, k) in between:
                        between[s, k]()

            def mean_over_features(stage_name, src, count_sem, count):
                free(stage_name, 0, 0)
                pe.wait_ge(count_sem, count)
                for c in range(NC):
                    last = pe.matmul(ps[:, 0, c, 0:TC], ones[:, :], src[:, 0, c * TC:(c + 1) * TC],
                                     start=True, stop=True)
                last.then_inc(psum_ready[0], 1)

            def token_means(norm, src):
                n = NORM[norm]
                if n:
                    pe.wait_ge(norm_free, 4 * n)
                pe.wait_ge(ssq_done, 10 * (n + 1))
                for c in range(N_TOK):
                    t = min(c * P, T - P)
                    last = pe.matmul(pm[:, 0, c:c + 1], src[:, 0, t:t + P], ones[:, 0:1], start=True, stop=True)
                last.then_inc(norm_ready, 1)

            def spread(norm, src):
                n = NORM[norm]
                pe.wait_ge(diag_ready, 2 * (n + 1))
                for j, (b, t, w) in enumerate(NORM_PIECES):
                    if b == 0:
                        pe.wait_ge(norm_free, 4 * n + 1 + j // 2)
                    pe.matmul(pm[:, b, 0:w], ones[:, :], src[:, 0, t:t + w], start=True, stop=True).then_inc(norm_ready, 1)

            pe.wait_ge(ones_set, 1)
            for _ in range(WARM_UP):
                pe.matmul(pm[:, 1, 0:P], ones[:, :], ones[:, :], start=True, stop=True)

            pair("A", 0, W0["A"], x1g_hi, x1g_lo, 1, x1g_lo_done, 0, {(1, KD - 3): lambda: token_means("norm1", ssq)})
            spread("norm1", diag)
            pair("A", 1, W0["A"] + 2, h1_hi, h1_lo, 4, lo_ready, SPLIT["H1"])
            with pe.Fori(1, KD) as i:
                for j in range(4):
                    product("A", j % 2, 2 * i + j // 2, W0["A"] + 4 * i + j, j % 2, h1_hi, h1_lo, SPLIT["H1"])
            with pe.Fori(0, KB // 2) as i:
                for j in range(2):
                    product("V", j, i, W0["V"] + 2 * i + j, j, h1_hi, h1_lo, SPLIT["H1"])
            mean_over_features("mean", conv_mean, conv_sum, 1 + KD)

            def transpose_group(n, g):
                b = g % 2
                if g == 0:
                    pe.wait_ge(vc_done, n + 1)
                if isinstance(n, int) and n == 0:
                    if g == 2:
                        pe.wait_ge(pm_free[b], 1)
                else:
                    pe.wait_ge(pm_free[b], 4 * n - 2 + g // 2 if b == 0 else 3 * n - 2)
                for q in range(4):
                    last = pe.transpose(pm[:, b, q * P:(q + 1) * P], v_chunk[:, 4 * g + q, :], ident[:, :])
                last.then_inc(pm_ready[b], 1)

            def mix_quarter(n, q, w, hi, lo, last_chunk=False):
                b = (q + 1) % 2
                if q == 0:
                    pe.wait_ge(vlo_done, n + 1)
                    pe.wait_ge(wm_split, 4)
                before = (4 * n + 4 - 2 * last_chunk if b == 0 else 3 * n + 2 - last_chunk) + q // 2
                pe.wait_ge(pm_free[b], before)
                for c, g, ng, off in ((3 * q, 2 * q, 1, 0), (3 * q + 1, 2 * q, 2, 128), (3 * q + 2, 2 * q + 1, 1, 384)):
                    for n_pass, (vv, ww) in enumerate(((v_hi, hi), (v_hi, lo), (v_lo, hi))):
                        last = pe.matmul(pm[:, b, off:off + ng * w], vv[:, c * P:(c + 1) * P],
                                         ww[:, g:g + ng, :], start=n_pass == 0, stop=n_pass == 2)
                last.then_inc(pm_ready[b], 1)

            def u_slot(par, n, between=()):
                product("U", par, n, W0["U"] + 2 * n + par, par, h1_hi, h1_lo, SPLIT["H1"], between)

            def steps(j, trans, mixed):
                out = {}
                if trans:
                    out |= {1 + g: (lambda g=g: transpose_group(j, g)) for g in range(3)}
                if mixed == "prompt":
                    out |= {4 + q: (lambda q=q: mix_quarter(j - 1, q, CHUNK, wm_hi, wm_lo)) for q in range(4)}
                if mixed == "samples":
                    out |= {4 + q: (lambda q=q: mix_quarter(j - 1, q, NS, ws_hi, ws_lo, True)) for q in range(4)}
                return out

            u_slot(0, 0, steps(0, True, None))
            with pe.Fori(0, N_CHUNKS // 2) as i:
                u_slot(1, i, steps(2 * i + 1, True, "prompt"))
                u_slot(0, i + 1, steps(2 * i + 2, True, "prompt"))
            u_slot(1, 4, steps(N_CHUNKS + 1, False, "samples"))
            u_slot(0, 5)
            u_slot(1, 5)

            for unit in range(KB):
                pe.wait_ge(w_ready, W0["B"] + unit + 1)
                for n in range(UNIT):
                    m, k = divmod(unit * UNIT + n, KB)
                    if k == 0 and m == 4:
                        token_means("var", ssq_b)
                    if k == 0 and m == 6:
                        spread("var", diag_b)
                    if k == 0:
                        free("B", m % 2, m // 2)
                    if m == 0:
                        pe.wait_ge(lo_ready, SPLIT["GB"] + k + 1)
                    first, last = tile_product(m % 2, unit % 2, n, gb_hi, gb_lo, k, k == 0, k == KB - 1)
                    if n == 0:
                        first.then_inc(w_passed, 1)
                    if k == KB - 1:
                        last.then_inc(psum_ready[m % 2], 1)
            with pe.Fori(0, KD // 2) as i:
                for j in range(2):
                    product("AO", j, i, W0["AO"] + 2 * i + j, j, a_hi, a_lo, SPLIT["A"])
            with pe.Fori(0, KD // 2) as i:
                for j in range(2):
                    product("O", j, i, W0["O"] + 2 * i + j, j, m_hi, m_lo, SPLIT["M"])
            def mixer_group(g, between=({}, {})):
                per = (FG + KD) // 2
                for j in range(FG):
                    product("F", j % 2, per * g + j // 2, W0["F"] + 8 * g + j, j % 2, xg_hi, xg_lo, SPLIT["H2"],
                            between[j] if j < 2 else {})
                for unit in range(KD // 2):
                    pe.wait_ge(w_ready, W0["F"] + 8 * g + FG + unit + 1)
                    if unit == 0:
                        order = [(k, m) for k in range(FG) for m in range(2)]
                    else:
                        order = [(k, m) for m in range(2) for k in range(FG)]
                    for k, m in order:
                        if k == 0:
                            free("F", m, per * g + FG // 2 + unit)
                        pe.wait_ge(lo_ready, SPLIT["F"] + FG * g + k + 1)
                        first, last = tile_product(m, unit % 2, m * FG + k, f_hi, f_lo, k, k == 0, k == FG - 1)
                        if (k, m) == (0, 0):
                            first.then_inc(w_passed, 1)
                        if k == FG - 1:
                            last.then_inc(psum_ready[m], 1)

            mixer_group(0, ({KD - 2: lambda: token_means("norm2", ssq)}, {KD // 2: lambda: spread("norm2", diag)}))
            with pe.Fori(1, NG) as g:
                mixer_group(g)

            for m in range(KD):
                unit = m * KP // UNIT
                if m == 2:
                    token_means("norm3", ssq)
                if m == 4:
                    spread("norm3", diag)
                free("PE", m % 2, m // 2)
                pe.wait_ge(w_ready, W0["PE"] + unit + 1)
                for k in range(KP):
                    pe.wait_ge(lo_ready, SPLIT["P"] + k + 1)
                    first, last = tile_product(m % 2, unit % 2, (m * KP + k) % UNIT, p_hi, p_lo, k, k == 0, k == KP - 1)
                    if (m * KP + k) % UNIT == 0:
                        first.then_inc(w_passed, 1)
                last.then_inc(psum_ready[m % 2], 1)
            with pe.Fori(0, KD // 2) as i:
                for j in range(2):
                    product("G", j, i, W0["G"] + 2 * i + j, j, xg_hi, xg_lo, SPLIT["H3"])
            token_means("norm4", ssq)
            spread("norm4", diag)

        @block.scalar
        def _(act):
            act.dma_start(cols[:, 0:N_BIN + 7 * KD], io["cols"]).then_inc(const_loaded, 16)
            for i in (1, 3):
                act.dma_start(x1[:, 2 * i:2 * i + 2, :], io["xT"][2 * i:2 * i + 2].rearrange("k p t -> p k t"))\
                    .then_inc(x_loaded[i], 16)

            def load_tables():
                act.wait_ge(ws_zero, 1)
                act.dma_start(taps[:, :, :], io["taps"]).then_inc(tab_loaded, 16)
                act.dma_start(hist[:, :, 0:HIST], io["state"]).then_inc(tab_loaded, 16)
                act.dma_start(lnv_g[:, :], io["lnv_g"].partition_broadcast(P)).then_inc(tab_loaded, 16)
                act.dma_start(lnv_b[:, :], io["lnv_b"].partition_broadcast(P)).then_inc(tab_loaded, 16)

            def load_mixing_weights():
                act.dma_start(wm_raw[:, 0, 0:GROUPS * CHUNK], io["wsT"].rearrange("s g t -> s (g t)")).then_inc(wm_loaded, 16)
                for b in range(DEC_B):
                    act.dma_start(m2[b * DEC_S:(b + 1) * DEC_S, :, b * DEC_S:(b + 1) * DEC_S],
                                  io["wsT"][0:DEC_S, :, 0:DEC_S]).then_inc(wm_loaded, 16)

            def root(norm):
                act.wait_ge(tok_ready, NORM[norm] + 1)
                act.activation(tok[:, 1, 0:N_TOK], tok[:, 0, 0:N_TOK], ACT.Sqrt, scale=float(D * D)).then_inc(rms_ready, 1)

            act.wait_ge(const_loaded, 16)
            for k in range(KD):
                if k % 2 == 0:
                    act.wait_ge(x_loaded[k // 2], 16)
                act.wait_ge(ssq_done, k + 1)
                act.activation(val[:, k % 2, :], x1[:, k, :], ACT.Square).then_inc(sq_done, 1)
                act.activation(x1g_hi[:, k, :], x1[:, k, :], ACT.Copy, scale=col(G_MIX, k)).then_inc(x1g_hi_done, 1)
            root("norm1")

            def h1_high(k):
                act.wait_ge(val_ready, k + 1)
                act.activation(h1_hi[:, k, :], val[:, k % 2, :], ACT.Copy).then_inc(hi_ready, 1)

            def glu_and_gates(i, first):
                if first:
                    h1_high(0)
                    act.wait_ge(scaled, 1)
                else:
                    act.wait_ge(glu_done, i + 1)
                    ready(act, "A", 0, 2 * i)
                act.activation(pieces(sig[:, 0, :]), bank(0), ACT.Sigmoid, bias=col(B_GATE, i)).then_inc(psum_free[0], 1)
                if first:
                    h1_high(1)
                    h1_high(2)
                    act.wait_ge(scaled, 2)
                else:
                    ready(act, "A", 1, 2 * i)
                act.activation(pieces(lin[:, 0, :]), bank(1), ACT.Identity, bias=col(B_LIN, i)).then_inc(psum_free[1], 1)
                if first:
                    h1_high(3)
                    load_tables()
                    for k in range(4, KD):
                        h1_high(k)
                    load_mixing_weights()
                for s, (bias, dst) in enumerate(((B_GA, sA_d), (B_GB, sB_d))):
                    ready(act, "A", s, 2 * i + 1)
                    act.activation(pieces(gate_st[:, s, :]), bank(s), ACT.Sigmoid, bias=col(bias, i)).then_inc(psum_free[s], 1)
                    out = drow(dst, i if first else act.snap(i))
                    act.wait_ge(psum_free[s], JOB["A"][s] + 2 * i + 2 + s)
                    act.dma_start(out, gate_st[:, s, :]).then_inc(gate_stored[s], 16)
                if not first:
                    out = drow(conv_d, act.snap(i - 1))
                    act.wait_ge(conv_done, i)
                    act.dma_start(out, conv_out[:, :]).then_inc(conv_stored, 16)
                for s in range(2):
                    act.wait_ge(gate_stored[s], 16 * (i + 1))

            glu_and_gates(0, True)
            act.wait_ge(wm_masked, 2)
            act.activation(wm_hi[:, :, :], m1, ACT.Copy).then_inc(wm_split, 1)
            act.activation(ws_hi[:, :, :], m2, ACT.Copy).then_inc(wm_split, 1)
            with act.Fori(1, KD) as i:
                glu_and_gates(i, False)

            def v_pair(i):
                for s in range(2):
                    ready(act, "V", s, i)
                    act.activation(pieces(row(vt, 2 * i + s)), bank(s), ACT.Gelu_apprx_tanh, bias=col(B_V, 2 * i + s))\
                        .then_inc(psum_free[s], 1)

            act.wait_ge(glu_done, KD + 1)
            v_pair(0)
            v_pair(1)
            act.wait_ge(conv_done, KD)
            act.dma_start(conv_d[KD - 1], conv_out[:, :]).then_inc(conv_stored, 16)
            act.dma_start(io["conv_sample"], hist[:, :, DEC_S:HIST + DEC_S]).then_inc(hist_stored, 16)
            act.dma_start(io["conv_prompt"], conv_tail[:, :, :]).then_inc(tail_stored, 16)
            act.wait_ge(conv_stored, 16 * (KD + 1))
            def convolved_back(i):
                for s in range(2):
                    src = drow(conv_d, 2 * i - 2 + s if isinstance(i, int) else act.snap(2 * i - 2 + s))
                    act.wait_ge(conv_sum, 2 * i - 1)
                    act.dma_start(conv_in[:, s, :], src).then_inc(conv_back[s], 16)

            with act.Fori(1, KD // 2) as i:
                convolved_back(i)
                v_pair(i + 1)
            convolved_back(KD // 2)
            act.wait_ge(conv_sum, 1 + KD)
            act.wait_ge(hist_stored, 16)
            act.wait_ge(tail_stored, 16)
            act.dma_start(bs_p[:, :, :].rearrange("p g t -> p (g t)"), io["bs_p"].partition_broadcast(P)).then_inc(bs_loaded, 16)
            act.dma_start(bs_s[:, :, :].rearrange("p g t -> p (g t)"), io["bs_s"].partition_broadcast(P)).then_inc(bs_loaded, 16)
            v_pair(KB // 2 - 1)
            ready(act, "mean", 0, 0)
            act.activation(pieces(conv_mean[:, 0, :]), bank(0), ACT.Identity).then_inc(psum_free[0], 1)

            def u_out(j, par, n):
                ready(act, "U", par, n)
                act.wait_ge(u_stored, 16 * j) if not (isinstance(j, int) and j == 0) else None
                act.activation(pieces(u_st[:, 0, :]), bank(par), ACT.Gelu_apprx_tanh, bias=col(B_U, j)).then_inc(psum_free[par], 1)
                out = drow(u_d, j if isinstance(j, int) else act.snap(j))
                act.wait_ge(psum_free[par], JOB["U"][par] + n + 1 + par)
                act.dma_start(out, u_st[:, 0, :]).then_inc(u_stored, 16)

            def u_stays(j, par, n):
                ready(act, "U", par, n)
                act.activation(pieces(gb[:, j, :]), bank(par), ACT.Gelu_apprx_tanh, bias=col(B_U, j)).then_inc(psum_free[par], 1)

            def take_chunk(n, w):
                if not (isinstance(n, int) and n == 0):
                    act.wait_ge(pm_ready[0], 4 * n - 2)
                src = vt[:, :, bass.ds(n * CHUNK, w)]
                act.activation(v_chunk[:, :, 0:w], src, ACT.Copy).then_inc(vc_done, 1)

            def layer_norm(n, next_width, store=None):
                if not (isinstance(n, int) and n == 0):
                    act.wait_ge(vlo_done, n)
                for g in range(3):
                    b = g % 2
                    before = 0 if isinstance(n, int) and n == 0 else (4 * n - 2 if b == 0 else 3 * n - 2)
                    act.wait_ge(pm_ready[b], before + g // 2 + 1)
                    act.activation(v_tok[:, g * 512:(g + 1) * 512], pm[:, b, :], ACT.Copy).then_inc(pm_free[b], 1)
                act.wait_ge(ln_step, LN_STEPS * n + 6)
                act.activation(rs_v[:, 0:1], rs_v[:, 0:1], ACT.Sqrt).then_inc(rs_ready, 1)
                act.wait_ge(ln_step, LN_STEPS * n + 7)
                act.activation(v_tok[:, :], v_tok[:, :], ACT.Identity, scale=rs_v[:, 0:1], bias=rs_v[:, 1:2])\
                    .then_inc(v_normed, 1)
                if next_width:
                    take_chunk(n + 1, next_width)
                act.wait_ge(ln_step, LN_STEPS * (n + 1))
                if store is not None:
                    act.dma_start(*store).then_inc(vout, 16)
                if not (isinstance(n, int) and n == 0):
                    act.wait_ge(pm_ready[0], 4 * n + 2)
                act.activation(v_hi[:, :], v_tok[:, :], ACT.Copy).then_inc(vhi_done, 1)

            def slot(n, par, product_n, next_width=CHUNK, store=None):
                layer_norm(n, next_width, store)
                u_out(n, par, product_n)

            act.wait_ge(psum_free[0], JOB["mean"][0])
            act.wait_ge(psum_free[1], JOB["U"][1] + 1)
            take_chunk(0, CHUNK)
            slot(0, 0, 0)
            with act.Fori(0, 3) as i:
                slot(2 * i + 1, 1, i)
                slot(2 * i + 2, 0, i + 1)
            slot(N_CHUNKS - 1, 1, 3, NS, (io["v_prompt"], v_tok[:, :]))
            act.wait_ge(vout, 16)
            slot(N_CHUNKS, 0, 4, 0, (io["v_sample"], v_tok[0:NS, :]))
            u_stays(9, 1, 4)
            act.wait_ge(vout, 32)
            act.wait_ge(pm_free[1], PM1_END)
            act.wait_ge(pm_free[0], PM0_END)
            act.wait_ge(u_stored, 16 * 9)
            for q in range(3):
                act.dma_start(gb[:, 3 * q:3 * q + 3, :], u_d[3 * q:3 * q + 3].rearrange("k p t -> p k t")).then_inc(u_back[q], 16)
            u_stays(10, 0, 5)

            def gb_high(a, b):
                with act.Fori(a, b) as k:
                    act.wait_ge(val_ready, KD + k + 1)
                    act.activation(row(gb_hi, k), row(gb, k), ACT.Copy).then_inc(hi_ready, 1)

            gb_high(0, 9)
            u_stays(11, 1, 5)
            act.dma_start(xc[:, :, :], conv_d.rearrange("k p t -> p k t")).then_inc(xc_loaded, 16)
            gb_high(9, KB)

            def gate_back(m):
                act.wait_ge(gated, m + 1)
                act.dma_start(sB_st[:, 0, :], sB_d[m]).then_inc(sB_loaded, 16)

            def centred_square(m):
                act.wait_ge(xc_done, m + 1)
                act.wait_ge(ssq_done, 10 * NORM["var"] + 2 + m)
                act.activation(sq_b[:, 0, :], row(xc, m), ACT.Square).then_inc(sq_done, 1)

            gate_back(0)
            with act.Fori(0, KD - 1) as m:
                centred_square(m)
            gate_back(1)
            centred_square(KD - 1)
            gate_back(2)
            gate_back(3)
            root("var")
            for m in range(4, 7):
                gate_back(m)
            with act.Fori(0, KD) as k:
                act.wait_ge(norm_y, k + 1)
                act.activation(row(xc, k), row(xc, k), ACT.Silu, bias=col(LNA_B, k), scale=col(LNA_G, k)).then_inc(silu_done, 1)
            gate_back(7)
            def branch_a_high(a, b):
                with act.Fori(a, b) as k:
                    act.activation(row(a_hi, k), row(xc, k), ACT.Copy).then_inc(hi_ready, 1)

            act.wait_ge(silu_done, KD)
            act.wait_ge(w_passed, W0["B"] + KB)
            branch_a_high(0, KD // 2)
            ready(act, "B", 1, KD // 2 - 1)
            branch_a_high(KD // 2, KD)

            def staged(m, par, dram, dst, loaded, freed, count):
                src = drow(dram, m if isinstance(m, int) else act.snap(m))
                act.wait_ge(freed, count)
                act.dma_start(dst[:, par, :], src).then_inc(loaded[par], 16)

            for m in range(2):
                staged(m, m, sA_d, sA_st, sA_loaded, gated, KD + 1)

            def mixed_high(m):
                act.wait_ge(mix_done, m + 1)
                act.activation(row(m_hi, m), row(mix, m), ACT.Copy).then_inc(hi_ready, 1)

            with act.Fori(0, KD // 2 - 1) as i:
                for s in range(2):
                    mixed_high(2 * i + s)
                    staged(2 * i + s + 2, s, sA_d, sA_st, sA_loaded, gated, KD + 2 + 2 * i + s)
            for m in (KD - 2, KD - 1):
                mixed_high(m)

            ready(act, "AO", 1, KD // 2 - 1)
            for m in range(2):
                act.dma_start(x[:, m, :], io["xT"][m]).then_inc(x_back[m], 16)

            def square_and_high(norm, name, gain, k, s, src):
                act.wait_ge(ssq_done, 10 * NORM[norm] + k + 1)
                act.activation(val[:, s, :], src, ACT.Square).then_inc(sq_done, 1)
                act.activation(row(xg_hi, k), src, ACT.Copy, scale=col(gain, k)).then_inc(hi_ready, 1)

            def x_sum_done(m, s):
                act.wait_ge(x_done, m + 2)
                square_and_high("norm2", "H2", G_FFN, m, s, row(x, m))

            with act.Fori(0, KD // 2 - 1) as i:
                for s in range(2):
                    m = 2 * i + s
                    src, dst = drow(io["xT"], act.snap(m + 2)), row(x, act.snap(m + 2))
                    x_sum_done(m, s)
                    act.dma_start(dst, src).then_inc(x_back[s], 16)
            for m in (KD - 2, KD - 1):
                x_sum_done(m, m % 2)
            root("norm2")
            act.dma_start(p_raw[:, :, :], io["pT"].rearrange("k p t -> p k t")).then_inc(p_loaded, 16)

            act.wait_ge(p_loaded, 16)
            for k in range(KP):
                act.activation(p_hi[:, k, :], p_raw[:, k, :], ACT.Copy).then_inc(hi_ready, 1)

            def wide_tiles(g):
                for j in range(FG):
                    act.wait_ge(relu_done, FG * g + j + 1)
                    act.wait_ge(lo_ready, SPLIT["F"] + FG * g + j - 1)
                    act.activation(f_hi[:, j, :], relu[:, 0, :], ACT.Square).then_inc(sq_f, 1)
                    act.activation(val[:, j % 2, :], relu[:, 0, :], ACT.Square).then_inc(hi_ready, 1)
                    act.wait_ge(hi_ready, SPLIT["F"] + FG * g + j + 1)

            with act.Fori(0, NG) as g:
                wide_tiles(g)
            for m in range(KD):
                act.wait_ge(psum_free[m % 2], JOB["PE"][m % 2] + m % 2 - KD // 2 + m // 2 + 1)
                square_and_high("norm3", "H3", G_PLE, m, m % 2, x[:, m, :])

            for m in range(KD):
                ready(act, "PE", m % 2, m // 2)
                act.activation(pieces(pe_out[:, m, :]), bank(m % 2), ACT.Identity).then_inc(psum_free[m % 2], 1)
                if m == 1:
                    root("norm3")
            def gate(m, s, i):
                act.wait_ge(z_ready, m + 1)
                act.wait_ge(g_mul, m + 1)
                act.activation(val[:, s, :], z_g[:, s, :], ACT.Sigmoid, bias=col(B_PLE, m)).then_inc(sg_done, 1)

            def y_square(m, s):
                act.wait_ge(x_done, 1 + KD + m + 1)
                act.wait_ge(ssq_done, 10 * NORM["norm4"] + m + 1)
                act.activation(sq_g[:, s, :], row(x, m), ACT.Square).then_inc(sq_done, 1)

            with act.Fori(0, KD // 2) as i:
                for s in range(2):
                    gate(2 * i + s, s, i)
                    y_square(2 * i + s, s)
            root("norm4")
            for k in range(Y_DVE, KD):
                act.activation(x[:, k, :], x[:, k, :], ACT.Copy, scale=col(G_FIN, k)).then_inc(xg_done, 1)
            for k in range(Y_DVE, KD):
                act.wait_ge(y_pool, k - Y_DVE + 1)
                act.dma_start(io["y"][k], y[:, k, :]).then_inc(y_stored, 16)
            act.wait_ge(y_stored, 16 * KD)

        @block.vector
        def _(dve):
            dve.memset(ones[:, :], 1.0 / D).then_inc(ones_set, 1)
            dve.sem_inc(psum_free[1], 1)
            dve.sem_inc(conv_stored, 16)

            def token_diagonals(norm, dst):
                n = NORM[norm]
                dve.wait_ge(norm_ready, 4 * n + 1)
                dve.tensor_scalar(tok[:, 0, 0:N_TOK], pm[:, 0, 0:N_TOK], EPS, None, ALU.add).then_inc(norm_free, 1)
                dve.wait_ge(norm_free, 4 * n + 1)
                dve.reciprocal(tok[:, 0, 0:N_TOK], tok[:, 0, 0:N_TOK]).then_inc(tok_ready, 1)
                dve.wait_ge(rms_ready, n + 1)
                full = SEQ // P
                dve.tensor_tensor(dst[:, 0, 0:SEQ].rearrange("p (c t) -> p c t", c=full),
                                  ident[:, :].unsqueeze(1).to_broadcast([P, full, P]),
                                  tok[:, 1, 0:full].unsqueeze(2).to_broadcast([P, full, P]), ALU.mult).then_inc(diag_ready, 1)
                dve.tensor_scalar(dst[:, 0, SEQ:T], ident[:, P - NS:P], tok[:, 1, full:full + 1], None, ALU.mult)\
                    .then_inc(diag_ready, 1)

            def spread_out(norm, dst):
                n = NORM[norm]
                for j, (b, t, w) in enumerate(NORM_PIECES):
                    dve.wait_ge(norm_ready, 4 * n + 2 + j)
                    dve.tensor_copy(dst[:, 0, t:t + w], pm[:, b, 0:w]).then_inc(norm_free, 1)
                dve.wait_ge(norm_free, 4 * n + 4)

            def add_row(norm, k, src):
                dve.wait_ge(sq_done, KD * NORM[norm] + k + 1)
                dve.wait_ge(ssq_done, 10 * NORM[norm] + 2 + k)
                dve.tensor_tensor(ssq[:, 0, :], ssq[:, 0, :], src, ALU.add).then_inc(ssq_done, 1)

            def gain_low(name, gain, k):
                dve.wait_ge(hi_ready, SPLIT[name] + k + 1)
                dve.scalar_tensor_tensor(out=row(xg_lo, k), in0=row(x, k), scalar=col(gain, k), in1=row(xg_hi, k).bitcast(F32),
                                         op0=ALU.mult, op1=ALU.subtract).then_inc(lo_ready, 1)

            dve.memset(ssq[:, 0, :], 0.0).then_inc(ssq_done, 2)
            dve.wait_ge(const_loaded, 16)
            for k in range(KD):
                add_row("norm1", k, val[:, k % 2, :])
                dve.wait_ge(x1g_hi_done, k + 1)
                dve.scalar_tensor_tensor(out=x1g_lo[:, k, :], in0=x1[:, k, :], scalar=col(G_MIX, k),
                                         in1=x1g_hi[:, k, :].bitcast(F32), op0=ALU.mult, op1=ALU.subtract)\
                    .then_inc(x1g_lo_done, 1)
            dve.wait_ge(ident_set, 2)
            token_diagonals("norm1", diag)
            spread_out("norm1", rstd)

            def scale(s):
                ready(dve, "A", s, 0)
                dve.tensor_tensor(bank(s), bank(s), pieces(rstd[:, 0, :]), ALU.mult).then_inc(scaled, 1)

            def h1_value(k):
                dve.scalar_tensor_tensor(out=val[:, k % 2, :], in0=x1[:, k, :], scalar=col(G_MIX, k), in1=rstd[:, 0, :],
                                         op0=ALU.mult, op1=ALU.mult).then_inc(val_ready, 1)

            def h1_low(k):
                dve.wait_ge(hi_ready, SPLIT["H1"] + k + 1)
                dve.tensor_tensor(h1_lo[:, k, :], val[:, k % 2, :], h1_hi[:, k, :].bitcast(F32), ALU.subtract).then_inc(lo_ready, 1)
                dve.wait_ge(lo_ready, SPLIT["H1"] + k + 1)

            scale(0)
            h1_value(0)
            for k in range(1, KD):
                h1_value(k)
                h1_low(k - 1)
                if k == 2:
                    scale(1)
            h1_low(KD - 1)

            dve.memset(glu[:, 0:HIST], 0.0).then_inc(glu_done, 1)
            dve.wait_ge(tab_loaded, 64)

            with dve.Fori(0, KD) as i:
                step = CONV_STEPS * i
                dve.tensor_copy(tap[:, :], taps[:, bass.ds(i, 1), :].rearrange("p a n -> p (a n)")).then_inc(tap_set, 1)
                dve.wait_ge(psum_free[1], JOB["A"][1] + 2 * i + 2)
                dve.tensor_tensor(glu[:, HIST:HIST + T], lin[:, 0, :], sig[:, 0, :], ALU.mult).then_inc(glu_done, 1)
                dve.wait_ge(glu_done, i + 2)
                dve.wait_ge(tap_set, i + 1)
                new = glu[:, HIST + SEQ:HIST + T].rearrange("p (b t) -> p b t", b=DEC_B)
                h_i = hist[:, bass.ds(DEC_B * i, DEC_B), :]
                dve.tensor_copy(h_i[:, :, HIST:HIST + DEC_S], new).then_inc(conv_step, 1)
                dve.tensor_copy(conv_tail[:, bass.ds(i, 1), :].rearrange("p a n -> p (a n)"),
                                glu[:, SEQ:SEQ + HIST]).then_inc(conv_step, 1)
                dve.tensor_scalar(acc0[:, :], glu[:, 0:SEQ], tap[:, 0:1], tap[:, TAPS:TAPS + 1], ALU.mult, ALU.add)\
                    .then_inc(conv_step, 1)
                dve.tensor_scalar(acc1[:, :], glu[:, 1:1 + SEQ], tap[:, 1:2], None, ALU.mult).then_inc(conv_step, 1)
                for j in range(2, TAPS):
                    acc = acc0 if j % 2 == 0 else acc1
                    dve.wait_ge(conv_step, step + 2 + j - 1)
                    dve.scalar_tensor_tensor(out=acc[:, :], in0=glu[:, j:j + SEQ], scalar=tap[:, j:j + 1], in1=acc[:, :],
                                             op0=ALU.mult, op1=ALU.add).then_inc(conv_step, 1)
                w = tap[:, 0:TAPS].unsqueeze(1).to_broadcast([P, DEC_B, TAPS])
                for t in range(DEC_S):
                    dve.tensor_tensor(prod[:, t, :, :], h_i[:, :, t:t + TAPS], w, ALU.mult).then_inc(conv_step, 1)
                dve.wait_ge(conv_step, step + 2 + TAPS + DEC_S)
                dve.tensor_reduce(samp[:, :].rearrange("p (t b) -> p t b", t=DEC_S), prod[:, :, :, :], AX_X, ALU.add)\
                    .then_inc(conv_step, 1)
                dve.wait_ge(conv_step, step + CONV_STEPS)
                dve.wait_ge(conv_stored, 16 * i + 16)
                dve.tensor_scalar(conv_out[:, SEQ:T].rearrange("p (b t) -> p t b", b=DEC_B),
                                  samp[:, :].rearrange("p (t b) -> p t b", t=DEC_S), tap[:, TAPS:TAPS + 1], None, ALU.add)
                dve.tensor_tensor(conv_out[:, 0:SEQ], acc0[:, :], acc1[:, :], ALU.add).then_inc(conv_done, 1)
                dve.wait_ge(conv_done, i + 1)

            dve.memset(conv_mean[:, 0, :], 0.0).then_inc(conv_sum, 1)
            with dve.Fori(0, KD // 2) as i:
                for s in range(2):
                    dve.wait_ge(conv_back[s], 16 * (i + 1))
                    dve.wait_ge(conv_sum, 2 * i + s + 1)
                    dve.tensor_tensor(conv_mean[:, 0, :], conv_mean[:, 0, :], conv_in[:, s, :], ALU.add).then_inc(conv_sum, 1)

            dve.wait_ge(psum_free[1], JOB["U"][1] + 1)
            dve.wait_ge(psum_free[0], JOB["mean"][0])
            dve.wait_ge(bs_loaded, 32)

            def statistics(n):
                s = LN_STEPS * n
                first = isinstance(n, int) and n == 0
                dve.wait_ge(pm_free[0], 2 if first else 4 * n)
                dve.wait_ge(pm_free[1], 1 if first else 3 * n - 1)
                for g in range(3):
                    dve.bn_stats(stats[:, g, :], v_tok[:, g * 512:(g + 1) * 512]).then_inc(ln_step, 1)
                dve.wait_ge(ln_step, s + 3)
                dve.memset(rs_v[:, 0:1], EPS)
                dve.bn_aggr(mv[:, :], stats[:, :, :]).then_inc(ln_step, 1)
                dve.wait_ge(ln_step, s + 4)
                dve.tensor_tensor(rs_v[:, 0:1], rs_v[:, 0:1], mv[:, 1:2], ALU.add).then_inc(ln_step, 1)
                dve.wait_ge(ln_step, s + 5)
                dve.reciprocal(rs_v[:, 0:1], rs_v[:, 0:1]).then_inc(ln_step, 1)

            def shift(n):
                dve.wait_ge(rs_ready, n + 1)
                dve.scalar_tensor_tensor(out=rs_v[:, 1:2], in0=mv[:, 0:1], scalar=-1.0, in1=rs_v[:, 0:1],
                                         op0=ALU.mult, op1=ALU.mult).then_inc(ln_step, 1)

            def gain(n):
                dve.wait_ge(v_normed, n + 1)
                dve.tensor_tensor(v_tok[:, :], v_tok[:, :], lnv_g[:, :], ALU.mult).then_inc(ln_step, 1)

            def bias(n):
                dve.wait_ge(ln_step, LN_STEPS * n + 8)
                dve.tensor_tensor(v_tok[:, :], v_tok[:, :], lnv_b[:, :], ALU.add).then_inc(ln_step, 1)

            def low(n):
                dve.wait_ge(vhi_done, n + 1)
                dve.tensor_tensor(v_lo[:, :], v_tok[:, :], v_hi[:, :].bitcast(F32), ALU.subtract).then_inc(vlo_done, 1)

            def mixed_out(n, q, w, bs, last_chunk=False):
                b = (q + 1) % 2
                before = (4 * n + 4 - 2 * last_chunk if b == 0 else 3 * n + 2 - last_chunk) + q // 2
                dve.wait_ge(pm_ready[b], before + 1)
                for c, p0, p1, off, g in ((0, 0, P, 0, 0), (1, 0, 64, 128, 0), (1, 64, P, 128 + w, 1), (2, 0, P, 384, 1)):
                    dst = vt[p0:p1, 3 * q + c, bass.ds(n * CHUNK, w)]
                    last = dve.tensor_tensor(dst, pm[p0:p1, b, off:off + w], bs[p0:p1, 2 * q + g, :], ALU.add)
                last.then_inc(pm_free[b], 1)

            statistics(0)
            shift(0)
            gain(0)
            bias(0)
            low(0)

            def slot(n):
                statistics(n)
                shift(n)
                mixed_out(n - 1, 0, CHUNK, bs_p)
                mixed_out(n - 1, 1, CHUNK, bs_p)
                gain(n)
                mixed_out(n - 1, 2, CHUNK, bs_p)
                bias(n)
                mixed_out(n - 1, 3, CHUNK, bs_p)
                low(n)

            with dve.Fori(1, N_CHUNKS + 1) as n:
                slot(n)
            for q in range(4):
                mixed_out(N_CHUNKS, q, NS, bs_s, True)

            dve.wait_ge(pm_free[0], PM0_END)
            dve.wait_ge(pm_free[1], PM1_END)

            def gb_product(a, b):
                with dve.Fori(a, b) as k:
                    dve.tensor_tensor(row(gb, k), row(gb, k), row(vt, k), ALU.mult).then_inc(val_ready, 1)

            def gb_low(a, b):
                with dve.Fori(a, b) as k:
                    dve.wait_ge(hi_ready, SPLIT["GB"] + k + 1)
                    dve.tensor_tensor(row(gb_lo, k), row(gb, k), row(gb_hi, k).bitcast(F32), ALU.subtract).then_inc(lo_ready, 1)

            for q in range(3):
                dve.wait_ge(u_back[q], 16)
                gb_product(3 * q, 3 * q + 3)
                if q:
                    gb_low(3 * q - 3, 3 * q)
            gb_low(6, 9)
            dve.wait_ge(psum_free[1], JOB["U"][1] + 5 + 1)
            dve.wait_ge(psum_free[0], JOB["U"][0] + 6)
            gb_product(9, 11)
            dve.wait_ge(psum_free[1], JOB["U"][1] + 6 + 1)
            gb_product(11, KB)
            gb_low(9, KB)
            dve.memset(ssq_b[:, 0, :], 0.0).then_inc(ssq_done, 2)
            dve.sem_inc(gated, 1)
            dve.wait_ge(xc_loaded, 16)

            def centre(m):
                dve.tensor_tensor(row(xc, m), row(xc, m), conv_mean[:, 0, :], ALU.subtract).then_inc(xc_done, 1)

            def add_square(m):
                dve.wait_ge(sq_done, KD * NORM["var"] + m + 1)
                dve.wait_ge(ssq_done, 10 * NORM["var"] + 2 + m)
                dve.tensor_tensor(ssq_b[:, 0, :], ssq_b[:, 0, :], sq_b[:, 0, :], ALU.add).then_inc(ssq_done, 1)

            def gate_b(m):
                s, n = m % 2, m // 2
                ready(dve, "B", s, n)
                dve.wait_ge(sB_loaded, 16 * (m + 1))
                dve.tensor_tensor(pieces(mix[:, m, :]), bank(s), pieces(sB_st[:, 0, :]), ALU.mult).then_inc(psum_free[s], 1)
                dve.wait_ge(psum_free[s], JOB["B"][s] + n + 1 + s)
                dve.sem_inc(gated, 1)

            centre(0)
            with dve.Fori(1, KD - 1) as m:
                centre(m)
                add_square(m - 1)
            gate_b(0)
            centre(KD - 1)
            add_square(KD - 2)
            add_square(KD - 1)
            for m in range(1, 4):
                gate_b(m)
            token_diagonals("var", diag_b)
            for m in range(4, 6):
                gate_b(m)
            spread_out("var", rstd_b)
            with dve.Fori(0, KD) as k:
                dve.tensor_tensor(row(xc, k), row(xc, k), rstd_b[:, 0, :], ALU.mult).then_inc(norm_y, 1)
            gate_b(6)

            def branch_a_low(a, b):
                with dve.Fori(a, b) as k:
                    dve.wait_ge(hi_ready, SPLIT["A"] + k + 1)
                    dve.tensor_tensor(row(a_lo, k), row(xc, k), row(a_hi, k).bitcast(F32), ALU.subtract).then_inc(lo_ready, 1)

            branch_a_low(0, KD // 2)
            gate_b(7)
            branch_a_low(KD // 2, KD)
            with dve.Fori(0, KD // 2) as i:
                for s in range(2):
                    m = 2 * i + s
                    ready(dve, "AO", s, i)
                    dve.wait_ge(sA_loaded[s], 16 * (i + 1))
                    dve.tensor_tensor(pieces(val[:, s, :]), bank(s), pieces(sA_st[:, s, :]), ALU.mult).then_inc(psum_free[s], 1)
                    dve.wait_ge(psum_free[s], JOB["AO"][s] + i + 1 + s)
                    dve.sem_inc(gated, 1)
                    dve.tensor_tensor(row(mix, m), row(mix, m), val[:, s, :], ALU.add).then_inc(mix_done, 1)
                    dve.wait_ge(hi_ready, SPLIT["M"] + m + 1)
                    dve.tensor_tensor(row(m_lo, m), row(mix, m), row(m_hi, m).bitcast(F32), ALU.subtract).then_inc(lo_ready, 1)
            dve.wait_ge(lo_ready, SPLIT["M"] + KD)
            dve.sem_inc(x_done, 1)

            dve.memset(ssq[:, 0, :], 0.0).then_inc(ssq_done, 2)
            with dve.Fori(0, KD // 2) as i:
                for s in range(2):
                    m = 2 * i + s
                    ready(dve, "O", s, i)
                    dve.wait_ge(x_back[s], 16 * (i + 1))
                    dve.tensor_tensor(pieces(row(x, m)), bank(s), pieces(row(x, m)), ALU.add).then_inc(psum_free[s], 1)
                    dve.wait_ge(psum_free[s], JOB["O"][s] + i + 1 + s)
                    dve.sem_inc(x_done, 1)
                    add_row("norm2", m, val[:, s, :])
                    gain_low("H2", G_FFN, m)
            token_diagonals("norm2", diag)
            spread_out("norm2", rstd)

            per = (FG + KD) // 2

            def wide_low(g):
                for j in range(FG):
                    ready(dve, "F", j % 2, per * g + j // 2)
                    dve.scalar_tensor_tensor(out=pieces(relu[:, 0, :]), in0=bank(j % 2), scalar=0.0, in1=pieces(rstd[:, 0, :]),
                                             op0=ALU.max, op1=ALU.mult).then_inc(psum_free[j % 2], 1)
                    dve.wait_ge(psum_free[j % 2], JOB["F"][j % 2] + per * g + j // 2 + 1 + j % 2)
                    dve.sem_inc(relu_done, 1)
                    dve.wait_ge(hi_ready, SPLIT["F"] + FG * g + j + 1)
                    dve.tensor_tensor(f_lo[:, j, :], val[:, j % 2, :], f_hi[:, j, :].bitcast(F32), ALU.subtract)\
                        .then_inc(lo_ready, 1)

            def add_to_x(g, m):
                ready(dve, "F", m % 2, per * g + (FG + m) // 2)
                dve.tensor_tensor(pieces(x[:, m, :]), bank(m % 2), pieces(x[:, m, :]), ALU.add).then_inc(psum_free[m % 2], 1)

            def embedding_low():
                for k in range(KP):
                    dve.wait_ge(hi_ready, SPLIT["P"] + k + 1)
                    dve.tensor_tensor(p_lo[:, k, :], p_raw[:, k, :], p_hi[:, k, :].bitcast(F32), ALU.subtract).then_inc(lo_ready, 1)

            embedding_low()
            with dve.Fori(0, NG - 1) as g:
                wide_low(g)
                for m in range(KD):
                    add_to_x(g, m)
            wide_low(NG - 1)
            dve.memset(ssq[:, 0, :], 0.0).then_inc(ssq_done, 2)
            for m in range(KD):
                add_to_x(NG - 1, m)
                if m:
                    add_row("norm3", m - 1, val[:, (m - 1) % 2, :])
                    gain_low("H3", G_PLE, m - 1)
            add_row("norm3", KD - 1, val[:, (KD - 1) % 2, :])
            gain_low("H3", G_PLE, KD - 1)
            token_diagonals("norm3", diag)
            spread_out("norm3", rstd)
            dve.sem_inc(g_mul, 2)
            dve.memset(ssq[:, 0, :], 0.0).then_inc(ssq_done, 2)
            with dve.Fori(0, KD // 2) as i:
                for s in range(2):
                    m = 2 * i + s
                    ready(dve, "G", s, i)
                    dve.tensor_tensor(pieces(z_g[:, s, :]), bank(s), pieces(rstd[:, 0, :]), ALU.mult).then_inc(psum_free[s], 1)
                    dve.wait_ge(psum_free[s], JOB["G"][s] + i + 1 + s)
                    dve.sem_inc(z_ready, 1)
                    dve.wait_ge(sg_done, m + 1)
                    dve.tensor_tensor(row(pe_out, m), row(pe_out, m), val[:, s, :], ALU.mult).then_inc(g_mul, 1)
                    dve.wait_ge(g_mul, m + 3)
                    dve.tensor_tensor(row(x, m), row(x, m), row(pe_out, m), ALU.add).then_inc(x_done, 1)
                    add_row("norm4", m, sq_g[:, s, :])
            token_diagonals("norm4", diag)
            spread_out("norm4", rstd)
            dve.sem_inc(rstd_set, 1)
            for k in range(Y_DVE):
                dve.scalar_tensor_tensor(out=y[:, k, :], in0=x[:, k, :], scalar=col(G_FIN, k), in1=rstd[:, 0, :],
                                         op0=ALU.mult, op1=ALU.mult).then_inc(y_ready, 1)


WARM_UP = 20
LN_STEPS = 9
NORM_PIECES = ((0, 0, 512), (1, 512, 512), (0, 1024, T - 1024))
CONV_STEPS = 2 + TAPS + DEC_S + 1
PM0_END = 4 * (N_CHUNKS + 1)
PM1_END = 3 * (N_CHUNKS + 1)


def kernel(**inputs):
    import numpy as np
    import concourse.bacc as bacc
    from concourse.bass_utils import run_bass_kernel_spmd

    a = {k: np.asarray(v) for k, v in inputs.items()}

    def tokens(prompt, sample, k):
        both = np.concatenate([prompt.reshape(SEQ, -1), sample.reshape(NS, -1)], axis=0)
        return np.ascontiguousarray(both.T).reshape(k, P, T)

    def by_output(w):
        k, n = w.shape[0] // P, w.shape[1] // P
        return w.reshape(k, P, n, P).transpose(2, 1, 0, 3).reshape(n, P, k * P)

    def by_tile(w):
        return w.reshape(w.shape[0] // P, P, w.shape[1] // P, P).transpose(2, 0, 1, 3)

    def packed(tiles):
        return tiles.reshape(-1, UNIT, P, P).transpose(0, 2, 1, 3).reshape(-1, P, UNIT * P)

    w_in = by_output(a["w_in"][0])
    order = [b + m for m in range(KD) for b in (B_GATE, B_LIN, B_GA, B_GB)]
    order += [B_V + m for m in range(KB)] + [B_U + m for m in range(KB)]
    ff1 = by_output(a["w_ff1"][0]).reshape(NG, FG, P, UNIT * P)
    ff2 = np.stack([packed(by_tile(a["w_ff2"][0][g * FG * P:(g + 1) * FG * P])) for g in range(NG)])
    weights = np.concatenate([
        w_in[order], packed(by_tile(a["w_b_out"][0])), by_output(a["w_a_out"][0]), by_output(a["w_o"][0]),
        np.concatenate([ff1, ff2], axis=1).reshape(-1, P, UNIT * P),
        packed(by_tile(a["w_ple"][0])), by_output(a["w_ple_gate"][0])])

    def column(v):
        return v.reshape(-1, P).T

    arrays = {
        "xT": tokens(a["x_prompt"], a["x_sample"], KD),
        "pT": tokens(a["p_prompt"][0], a["p_sample"][0], KP),
        "weights": weights,
        "cols": np.concatenate([column(v) for v in (
            a["b_in"][0], a["g_mix"][0], a["g_ffn"][0], a["g_ple"][0], a["g_final"], a["ln_a_g"][0],
            a["ln_a_b"][0], a["b_ple_gate"][0])], axis=1),
        "taps": np.concatenate([a["conv_w"][0], a["conv_b"]], axis=0).reshape(TAPS + 1, KD, P).transpose(2, 1, 0),
        "state": a["state_conv"][0].reshape(DEC_B, HIST, KD, P).transpose(3, 2, 0, 1).reshape(P, KD * DEC_B, HIST),
        "wsT": a["w_s"][0].transpose(2, 0, 1),
        "lnv_g": a["ln_v_g"][0],
        "lnv_b": a["ln_v_b"][0],
        "bs_p": a["b_s"][0].reshape(-1),
        "bs_s": np.tile(a["b_s"][0][:, None, :DEC_S], (1, DEC_B, 1)).reshape(-1),
    }
    outs = {"y": (KD, P, T), "conv_prompt": (P, KD, HIST), "conv_sample": (P, KD * DEC_B, HIST),
            "v_prompt": (CHUNK, C_B), "v_sample": (NS, C_B)}
    nc = bacc.Bacc("TRN2", target_bir_lowering=False, num_devices=1)
    io = {}
    arrays = {k: np.ascontiguousarray(v) for k, v in arrays.items()}
    for k, v in arrays.items():
        io[k] = nc.dram_tensor(k, v.shape, mybir.dt.from_np(v.dtype), kind="ExternalInput").ap()
    for k, shape in outs.items():
        io[k] = nc.dram_tensor(k, shape, F32, kind="ExternalOutput").ap()
    build(nc, io)
    r = run_bass_kernel_spmd(nc, [arrays], core_ids=[0]).results[0]
    y = r["y"].reshape(D, T).T
    conv_p = r["conv_prompt"].transpose(2, 1, 0).reshape(1, 1, HIST, D)
    conv_s = r["conv_sample"].reshape(P, KD, DEC_B, HIST).transpose(2, 3, 1, 0).reshape(1, DEC_B, HIST, D)
    return (np.ascontiguousarray(y[:SEQ]).reshape(1, SEQ, D), np.ascontiguousarray(y[SEQ:]).reshape(DEC_B, DEC_S, D),
            np.ascontiguousarray(conv_p), np.ascontiguousarray(conv_s),
            r["v_prompt"].reshape(1, 1, CHUNK, C_B), r["v_sample"].reshape(1, DEC_B, DEC_S, C_B))
```

```python
from contextlib import ExitStack

import concourse.bass as bass
from concourse import mybir

F32 = mybir.dt.float32
F32R = mybir.dt.float32r
ALU = mybir.AluOpType
ACT = mybir.ActivationFunctionType
AX_X = mybir.AxisListType.X

P = 128
D = 1024
C_B = 1536
D_FF = 4096
P_DIM = 256
SEQ = 1024
DEC_B, DEC_S = 8, 4
NS = DEC_B * DEC_S
T = SEQ + NS
CHUNK = 128
N_CHUNKS = SEQ // CHUNK
GROUPS = 8
TAPS = 31
HIST = TAPS - 1
EPS = 1e-6

KD = D // P
KB = C_B // P
KF = D_FF // P
KP = P_DIM // P
NC = 3
TC = T // NC
UNIT = 8
FG = 4
NG = KF // FG

B_LIN, B_GATE, B_U, B_V, B_GA, B_GB = 0, KD, 2 * KD, 2 * KD + KB, 2 * KD + 2 * KB, 3 * KD + 2 * KB
N_BIN = 4 * KD + 2 * KB
N_TOK = -(-T // P)

STAGES = [
    ("A", 2 * KD, 2 * KD), ("V", KB // 2, KB // 2), ("mean", 1, 0),
    ("U", KB // 2, KB // 2), ("B", KD // 2, KD // 2), ("AO", KD // 2, KD // 2),
    ("O", KD // 2, KD // 2), ("F", NG * (FG + KD) // 2, NG * (FG + KD) // 2),
    ("PE", KD // 2, KD // 2), ("G", KD // 2, KD // 2),
]
JOB = {}
_n0 = _n1 = 0
for _name, _a, _b in STAGES:
    JOB[_name] = (_n0, _n1)
    _n0 += _a
    _n1 += _b

SPLIT = {}
_n = 0
for _name, _k in (("H1", KD), ("GB", KB), ("A", KD), ("M", KD), ("H2", KD), ("P", KP), ("F", KF), ("H3", KD)):
    SPLIT[_name] = _n
    _n += _k

W0 = {}
_n = 0
for _name, _k in (("A", 4 * KD), ("V", KB), ("U", KB), ("B", KB), ("AO", KD), ("O", KD),
                  ("F", NG * 2 * FG), ("PE", KD * KP // UNIT), ("G", KD)):
    W0[_name] = _n
    _n += _k
N_UNITS = _n

Y_DVE = 5

NORM = {"norm1": 0, "var": 1, "norm2": 2, "norm3": 3, "norm4": 4}


def build(nc, io):
    ctx = ExitStack()
    with ctx:
        ROW = T * 4
        base = (nc.sbuf_base + 31) // 32 * 32

        def at(name, shape, dt, off):
            return nc.alloc_sbuf_tensor_at(name, shape, dt, offset=base + off)

        def rows(name, first, n, dt=F32):
            return at(name, [P, n, T], dt, first * ROW)

        h1_hi, h1_lo = rows("h1_hi", 0, KD, F32R), rows("h1_lo", 8, KD, F32R)
        x1 = rows("x1", 16, KD)
        x1g_hi, x1g_lo = rows("x1g_hi", 28, KD, F32R), rows("x1g_lo", 36, KD, F32R)
        sig, lin = rows("sig", 16, 1), rows("lin", 17, 1)
        gate_st = rows("gate_st", 18, 2)
        vt = rows("vt", 16, KB)
        conv_in = rows("conv_in", 26, 2)
        t0 = 28 * ROW
        glu = at("glu", [P, HIST + T + 2], F32, t0)
        acc0 = at("acc0", [P, SEQ], F32, t0 + 4352)
        acc1 = at("acc1", [P, SEQ], F32, t0 + 8448)
        conv_out = at("conv_out", [P, T], F32, t0 + 12544)
        prod = at("prod", [P, DEC_S, DEC_B, TAPS], F32, t0 + 16768)
        v_chunk = at("v_chunk", [P, KB, CHUNK], F32, t0)
        v_tok = at("v_tok", [P, C_B], F32, t0 + 6144)
        v_hi = at("v_hi", [P, C_B], F32R, t0 + 12288)
        v_lo = at("v_lo", [P, C_B], F32R, t0 + 18432)
        lnv_g = at("lnv_g", [P, C_B], F32, t0 + 24576)
        lnv_b = at("lnv_b", [P, C_B], F32, t0 + 30720)
        wm_hi = at("wm_hi", [P, GROUPS, CHUNK], F32R, t0 + 36864)
        wm_lo = at("wm_lo", [P, GROUPS, CHUNK], F32R, t0 + 40960)
        ws_hi = at("ws_hi", [P, GROUPS, NS], F32R, t0 + 45056)
        ws_lo = at("ws_lo", [P, GROUPS, NS], F32R, t0 + 46080)
        wm_raw = rows("wm_raw", 40, 1)
        ws_raw = at("ws_raw", [P, 1, GROUPS * NS], F32, t0 + 47104)
        conv_mean = rows("conv_mean", 40, 1)
        t1 = 41 * ROW
        u_st = rows("u_st", 41, 1)
        hist = at("hist", [P, KD * DEC_B, HIST + DEC_S], F32, t1)
        conv_tail = at("conv_tail", [P, KD, HIST], F32, t1 + 8704)
        bs_p = at("bs_p", [P, GROUPS, CHUNK], F32, t1 + ROW)
        bs_s = at("bs_s", [P, GROUPS, NS], F32, t1 + ROW + 4096)
        gb = rows("gb", 28, KB)
        gb_hi, gb_lo = rows("gb_hi", 16, KB, F32R), rows("gb_lo", 28, KB, F32R)
        mix = rows("mix", 0, KD)
        xc = rows("xc", 8, KD)
        ssq_b, sB_st, sq_b = rows("ssq_b", 41, 1), rows("sB_st", 42, 1), rows("sq_b", 43, 1)
        diag_b, rstd_b = rows("diag_b", 41, 1), rows("rstd_b", 43, 1)
        a_hi, a_lo = rows("a_hi", 16, KD, F32R), rows("a_lo", 28, KD, F32R)
        sA_st = rows("sA_st", 24, 2)
        m_hi, m_lo = rows("m_hi", 8, KD, F32R), rows("m_lo", 36, KD, F32R)
        rstd, ssq, val = rows("rstd", 24, 1), rows("ssq", 25, 1), rows("val", 26, 2)
        x = rows("x", 28, KD)
        xg_hi, xg_lo = rows("xg_hi", 0, KD, F32R), rows("xg_lo", 16, KD, F32R)
        f_hi, f_lo = rows("f_hi", 8, FG, F32R), rows("f_lo", 12, FG, F32R)
        relu = rows("relu", 42, 1)
        p_raw = rows("p_raw", 36, KP)
        p_hi, p_lo = rows("p_hi", 38, KP, F32R), rows("p_lo", 40, KP, F32R)
        pe_out = rows("pe_out", 8, KD)
        sq_g = rows("sq_g", 36, 2)
        z_g = rows("z_g", 42, 2)
        y = rows("y", 0, KD)
        c0 = 44 * ROW
        w_raw = at("w_raw", [P, 2, UNIT * P], F32, c0)
        w_hi = at("w_hi", [P, 2, UNIT * P], F32R, c0 + 8192)
        w_lo = at("w_lo", [P, 2, UNIT * P], F32R, c0 + 16384)
        c1 = c0 + 24576
        ones = at("ones", [P, P], F32, c1)
        ident = at("ident", [P, P], F32, c1 + 1024)
        cols = at("cols", [P, N_BIN + 8 * KD], F32, c1 + 512)
        taps = at("taps", [P, KD, 32], F32, t1 + 9728)
        tok = at("tok", [P, 2, 16], F32, c1 + 1600)
        diag = rows("diag", 26, 1)
        tap = at("tap", [P, 32], F32, c1 + 2048)
        stats = at("stats", [P, 3, 6], F32, c1 + 2176)
        mv = at("mv", [P, 2], F32, c1 + 2272)
        rs_v = at("rs_v", [P, 2], F32, c1 + 2304)
        w_col = at("w_col", [P, 1], F32, c1 + 1728)
        samp = at("samp", [P, NS], F32, t0 + 20736)
        G_MIX, G_FFN, G_PLE, G_FIN, LNA_G, LNA_B, B_PLE = (N_BIN + KD * n for n in range(7))

        ps = ctx.enter_context(nc.psum_tensor("ps", [P, 2, NC, 512], F32))
        pm = ctx.enter_context(nc.psum_tensor("pm", [P, 2, 512], F32))

        def scratch(name, n):
            return nc.dram_tensor(name, (n, P, T), F32, kind="Internal").ap()

        sA_d, sB_d, conv_d, u_d = scratch("sA_d", KD), scratch("sB_d", KD), scratch("conv_d", KD), scratch("u_d", KB)

        def sem(name):
            return ctx.enter_context(nc.semaphore(name))

        w_loaded = [sem("w_loaded0"), sem("w_loaded1")]
        w_hi_done = sem("w_hi_done")
        w_ready = sem("w_ready")
        w_passed = sem("w_passed")
        psum_ready = [sem("psum_ready0"), sem("psum_ready1")]
        psum_free = [sem("psum_free0"), sem("psum_free1")]
        x_loaded = [sem(f"x_loaded{k}") for k in range(KD)]
        const_loaded = sem("const_loaded")
        tab_loaded, lnv_loaded = sem("tab_loaded"), sem("lnv_loaded")
        wm_loaded = sem("wm_loaded")
        ones_set = sem("ones_set")
        ws_zero, wm_masked, wm_split = sem("ws_zero"), sem("wm_masked"), sem("wm_split")
        ident_set = sem("ident_set")
        tok_ready, rms_ready, diag_ready = sem("tok_ready"), sem("rms_ready"), sem("diag_ready")
        rs_ready = sem("rs_ready")
        sq_done, ssq_done = sem("sq_done"), sem("ssq_done")
        val_ready = sem("val_ready")
        hi_ready, lo_ready = sem("hi_ready"), sem("lo_ready")
        glu_done, tap_set, conv_step = sem("glu_done"), sem("tap_set"), sem("conv_step")
        conv_done, conv_stored = sem("conv_done"), sem("conv_stored")
        gate_stored = [sem("gate_stored0"), sem("gate_stored1")]
        conv_back = [sem("conv_back0"), sem("conv_back1")]
        conv_sum = sem("conv_sum")
        bs_loaded, hist_stored, tail_stored = sem("bs_loaded"), sem("hist_stored"), sem("tail_stored")
        u_stored = sem("u_stored")
        vc_done = sem("vc_done")
        pm_ready, pm_free = [sem("pm_ready0"), sem("pm_ready1")], [sem("pm_free0"), sem("pm_free1")]
        ln_step = sem("ln_step")
        vhi_done, vlo_done = sem("vhi_done"), sem("vlo_done")
        vout = sem("vout")
        u_back = [sem(f"u_back{i}") for i in range(3)]
        xc_loaded, xc_done = sem("xc_loaded"), sem("xc_done")
        sB_loaded = sem("sB_loaded")
        sA_loaded, x_back = [sem("sA_loaded0"), sem("sA_loaded1")], [sem("x_back0"), sem("x_back1")]
        norm_ready, norm_free = sem("norm_ready"), sem("norm_free")
        x1g_hi_done, x1g_lo_done, scaled = sem("x1g_hi_done"), sem("x1g_lo_done"), sem("scaled")
        relu_done, z_ready = sem("relu_done"), sem("z_ready")
        norm_y, silu_done, gated, mix_done = sem("norm_y"), sem("silu_done"), sem("gated"), sem("mix_done")
        v_normed, xg_done = sem("v_normed"), sem("xg_done")
        sq_f, p_loaded, sg_done, g_mul = sem("sq_f"), sem("p_loaded"), sem("sg_done"), sem("g_mul")
        x_done = sem("x_done")
        last_ready = sem("last_ready")
        y_ready, y_pool, y_stored = sem("y_ready"), sem("y_pool"), sem("y_stored")

        block = ctx.enter_context(nc.Block())

        def pieces(ap):
            return ap.rearrange("p (c t) -> p c t", c=NC)

        def row(tile, k):
            if isinstance(k, int):
                return tile[:, k, :]
            return tile[:, bass.ds(k, 1), :].rearrange("p a t -> p (a t)")

        def drow(dram, k):
            if isinstance(k, int):
                return dram[k, :, :]
            return dram[bass.ds(k, 1), :, :].rearrange("a p t -> p (a t)")

        def col(first, k):
            if isinstance(k, int):
                return cols[:, first + k:first + k + 1]
            return cols[:, bass.ds(first + k, 1)]

        def piece(c):
            return slice(c * TC, (c + 1) * TC)

        def bank(slot):
            return ps[:, slot, :, 0:TC]

        m1 = wm_raw[:, 0, 0:GROUPS * CHUNK].rearrange("p (g t) -> p g t", g=GROUPS)
        m2 = ws_raw[:, 0, 0:GROUPS * NS].rearrange("p (g t) -> p g t", g=GROUPS)

        def ready(eng, stage_name, slot, n):
            eng.wait_ge(psum_ready[slot], JOB[stage_name][slot] + n + 1)

        @block.sync
        def _(sp):
            for s in range(2):
                sp.dma_start(w_raw[:, s, :], io["weights"][s]).then_inc(w_loaded[s], 16)
                for k in (4 * s, 4 * s + 2):
                    sp.dma_start(x1[:, k, :], io["xT"][k]).then_inc(x_loaded[k], 16)
            with sp.Fori(1, N_UNITS // 2) as i:
                for s in range(2):
                    src = sp.snap(2 * i + s)
                    unit = io["weights"][bass.ds(src, 1)].rearrange("a p n -> p (a n)")
                    sp.wait_ge(w_ready, 2 * i + s - 1)
                    sp.dma_start(w_raw[:, s, :], unit).then_inc(w_loaded[s], 16)
            for c in range(NC):
                sp.wait_ge(y_ready, Y_DVE * (c + 1))
                sp.dma_start(io["y"][0:Y_DVE, :, piece(c)].rearrange("k p t -> p k t"), y[:, 0:Y_DVE, piece(c)])\
                    .then_inc(y_stored, 16)

        @block.gpsimd
        def _(pool):
            pool.memset(ident[:, :], 0.0).then_inc(ident_set, 1)
            pool.wait_ge(ident_set, 1)
            pool.affine_select(out=ident[:, :], in_=ident[:, :], compare_op=ALU.not_equal, fill=1.0, base=0,
                               pattern=[[-1, P]], channel_multiplier=1).then_inc(ident_set, 1)

            def split(s, n, u):
                pool.wait_ge(w_loaded[s], 16 * n)
                if not isinstance(u, int) or u > 1:
                    pool.wait_ge(w_passed, u)
                    pool.tensor_tensor(w_col[:, :], w_raw[:, s, 0:1], w_raw[:, s, 1:2], ALU.add)
                if not isinstance(u, int) or u:
                    pool.tensor_copy(w_hi[:, s, :], w_raw[:, s, :]).then_inc(w_hi_done, 1)
                pool.wait_ge(w_hi_done, u + 1)
                pool.tensor_tensor(w_lo[:, s, :], w_raw[:, s, :], w_hi[:, s, :].bitcast(F32), ALU.subtract)\
                    .then_inc(w_ready, 1)

            for s in range(2):
                split(s, 1, s)
            for s in range(2):
                split(s, 2, 2 + s)
            split(0, 3, 4)
            for s in range(2):
                ready(pool, "A", s, 1)
            pool.memset(ws_raw[:, 0, 0:GROUPS * NS], 0.0).then_inc(ws_zero, 1)
            split(1, 3, 5)
            pool.wait_ge(wm_loaded, 16 * (1 + DEC_B))
            pool.affine_select(out=m1, in_=m1, compare_op=ALU.is_ge, fill=0.0, base=0,
                               pattern=[[0, GROUPS], [1, CHUNK]], channel_multiplier=-1).then_inc(wm_masked, 1)
            pool.affine_select(out=m2, in_=m2, compare_op=ALU.is_ge, fill=0.0, base=0,
                               pattern=[[0, GROUPS], [1, NS]], channel_multiplier=-1).then_inc(wm_masked, 1)
            split(0, 4, 6)
            pool.wait_ge(wm_split, 2)
            pool.tensor_tensor(wm_lo[:, :, :], m1, wm_hi[:, :, :].bitcast(F32), ALU.subtract).then_inc(wm_split, 1)
            pool.tensor_tensor(ws_lo[:, :, :], m2, ws_hi[:, :, :].bitcast(F32), ALU.subtract).then_inc(wm_split, 1)
            split(1, 4, 7)
            with pool.Fori(4, N_UNITS // 2) as i:
                for s in range(2):
                    split(s, i + 1, 2 * i + s)
            pool.wait_ge(xg_done, KD - Y_DVE)
            for c in range(NC):
                pool.wait_ge(norm_free, 4 * NORM["norm4"] + 2 * c + 2)
                for k in range(Y_DVE, KD):
                    pool.tensor_tensor(y[:, k, piece(c)], x[:, k, piece(c)], rstd[:, 0, piece(c)], ALU.mult).then_inc(y_pool, 1)

        @block.tensor
        def _(pe):
            def free(stage_name, slot, n):
                if JOB[stage_name][slot] + slot or not isinstance(n, int) or n:
                    pe.wait_ge(psum_free[slot], JOB[stage_name][slot] + n + slot)

            def tile_product(slot, s, n, hi, lo, k, start, stop):
                first = last = None
                for w, a in ((w_hi, hi), (w_hi, lo), (w_lo, hi)):
                    for c in range(NC):
                        last = pe.matmul(ps[:, slot, c, 0:TC], w[:, s, n * P:(n + 1) * P],
                                         a[:, k, c * TC:(c + 1) * TC],
                                         start=start and w is w_hi and a is hi, stop=stop and w is w_lo)
                        if first is None:
                            first = last
                return first, last

            def product(stage_name, slot, n, u, s, hi, lo, base_k, between=()):
                free(stage_name, slot, n)
                pe.wait_ge(w_ready, u + 1)
                for k in range(KD):
                    if base_k is not None:
                        pe.wait_ge(lo_ready, base_k + k + 1)
                    first, last = tile_product(slot, s, k, hi, lo, k, k == 0, k == KD - 1)
                    if k == 0:
                        first.then_inc(w_passed, 1)
                    if k == KD - 1:
                        last.then_inc(psum_ready[slot], 1)
                    if k in between:
                        between[k]()

            def first_pair(between):
                order = []
                for k in range(KD + LAG):
                    order += [(0, k)] * (k < KD) + [(1, k - LAG)] * (k >= LAG)
                for s, k in order:
                    if k == 0:
                        if s:
                            free("A", s, 0)
                        pe.wait_ge(w_ready, W0["A"] + s + 1)
                    pe.wait_ge(x1g_lo_done, k + 1)
                    first, last = tile_product(s, s, k, x1g_hi, x1g_lo, k, k == 0, k == KD - 1)
                    if (s, k) in ((0, 0), (1, KD - 1 - LAG)):
                        first.then_inc(w_passed, 1)
                    if k == KD - 1:
                        last.then_inc(psum_ready[s], 1)
                    if (s, k) in between:
                        between[s, k]()

            def mean_over_features(stage_name, src, count_sem, count):
                free(stage_name, 0, 0)
                pe.wait_ge(count_sem, count)
                for c in range(NC):
                    last = pe.matmul(ps[:, 0, c, 0:TC], ones[:, :], src[:, 0, c * TC:(c + 1) * TC],
                                     start=True, stop=True)
                last.then_inc(psum_ready[0], 1)

            def token_means(norm, src):
                n = NORM[norm]
                if n:
                    pe.wait_ge(norm_free, 4 * n)
                pe.wait_ge(ssq_done, 10 * (n + 1))
                for c in range(N_TOK):
                    t = min(c * P, T - P)
                    last = pe.matmul(pm[:, 0, c:c + 1], src[:, 0, t:t + P], ones[:, 0:1], start=True, stop=True)
                last.then_inc(norm_ready, 1)

            def spread(norm, src):
                n = NORM[norm]
                pe.wait_ge(diag_ready, 2 * (n + 1))
                for j, (b, t, w) in enumerate(NORM_PIECES):
                    if b == 0:
                        pe.wait_ge(norm_free, 4 * n + 1 + j // 2)
                    pe.matmul(pm[:, b, 0:w], ones[:, :], src[:, 0, t:t + w], start=True, stop=True).then_inc(norm_ready, 1)

            pe.wait_ge(ones_set, 1)
            for _ in range(WARM_UP):
                pe.matmul(pm[:, 1, 0:P], ones[:, :], ones[:, :], start=True, stop=True)

            first_pair({(0, KD - 2): lambda: token_means("norm1", ssq), (0, KD - 1): lambda: spread("norm1", diag)})
            for j in range(2):
                product("A", j, 1, W0["A"] + 2 + j, j, x1g_hi, x1g_lo, None)
            with pe.Fori(1, KD) as i:
                for j in range(4):
                    product("A", j % 2, 2 * i + j // 2, W0["A"] + 4 * i + j, j % 2, h1_hi, h1_lo, SPLIT["H1"])
            with pe.Fori(0, KB // 2) as i:
                for j in range(2):
                    product("V", j, i, W0["V"] + 2 * i + j, j, h1_hi, h1_lo, SPLIT["H1"])
            mean_over_features("mean", conv_mean, conv_sum, 1 + KD)

            def transpose_group(n, g):
                b = g % 2
                if g == 0:
                    pe.wait_ge(vc_done, n + 1)
                if isinstance(n, int) and n == 0:
                    if g == 2:
                        pe.wait_ge(pm_free[b], 1)
                else:
                    pe.wait_ge(pm_free[b], 4 * n - 2 + g // 2 if b == 0 else 3 * n - 2)
                for q in range(4):
                    last = pe.transpose(pm[:, b, q * P:(q + 1) * P], v_chunk[:, 4 * g + q, :], ident[:, :])
                last.then_inc(pm_ready[b], 1)

            def mix_quarter(n, q, w, hi, lo, last_chunk=False):
                b = (q + 1) % 2
                if q == 0:
                    pe.wait_ge(vlo_done, n + 1)
                    pe.wait_ge(wm_split, 4)
                before = (4 * n + 4 - 2 * last_chunk if b == 0 else 3 * n + 2 - last_chunk) + q // 2
                pe.wait_ge(pm_free[b], before)
                for c, g, ng, off in ((3 * q, 2 * q, 1, 0), (3 * q + 1, 2 * q, 2, 128), (3 * q + 2, 2 * q + 1, 1, 384)):
                    for n_pass, (vv, ww) in enumerate(((v_hi, hi), (v_hi, lo), (v_lo, hi))):
                        last = pe.matmul(pm[:, b, off:off + ng * w], vv[:, c * P:(c + 1) * P],
                                         ww[:, g:g + ng, :], start=n_pass == 0, stop=n_pass == 2)
                last.then_inc(pm_ready[b], 1)

            def u_slot(par, n, between=()):
                product("U", par, n, W0["U"] + 2 * n + par, par, h1_hi, h1_lo, SPLIT["H1"], between)

            def steps(j, mixed):
                out = {}
                if mixed == "prompt":
                    out |= {1 + g: (lambda g=g: transpose_group(j, g)) for g in range(3)}
                if mixed == "prompt":
                    out |= {4 + q: (lambda q=q: mix_quarter(j - 1, q, CHUNK, wm_hi, wm_lo)) for q in range(4)}
                if mixed == "samples":
                    out |= {4 + q: (lambda q=q: mix_quarter(j - 1, q, NS, ws_hi, ws_lo, True)) for q in range(4)}
                return out

            u_slot(0, 0, {0: lambda: [transpose_group(0, g) for g in (0, 1)], 1: lambda: transpose_group(0, 2)})
            with pe.Fori(0, N_CHUNKS // 2) as i:
                u_slot(1, i, steps(2 * i + 1, "prompt"))
                u_slot(0, i + 1, steps(2 * i + 2, "prompt"))
            u_slot(1, 4, steps(N_CHUNKS + 1, "samples"))
            u_slot(0, 5)
            u_slot(1, 5)

            for unit in range(KB):
                pe.wait_ge(w_ready, W0["B"] + unit + 1)
                for n in range(UNIT):
                    m, k = divmod(unit * UNIT + n, KB)
                    if k == 0 and m == 4:
                        token_means("var", ssq_b)
                    if k == 0 and m == 6:
                        spread("var", diag_b)
                    if k == 0:
                        free("B", m % 2, m // 2)
                    if m == 0:
                        pe.wait_ge(lo_ready, SPLIT["GB"] + k + 1)
                    first, last = tile_product(m % 2, unit % 2, n, gb_hi, gb_lo, k, k == 0, k == KB - 1)
                    if n == 0:
                        first.then_inc(w_passed, 1)
                    if k == KB - 1:
                        last.then_inc(psum_ready[m % 2], 1)
            with pe.Fori(0, KD // 2) as i:
                for j in range(2):
                    product("AO", j, i, W0["AO"] + 2 * i + j, j, a_hi, a_lo, SPLIT["A"])
            with pe.Fori(0, KD // 2) as i:
                for j in range(2):
                    product("O", j, i, W0["O"] + 2 * i + j, j, m_hi, m_lo, SPLIT["M"])
            def mixer_group(g, between=({}, {})):
                per = (FG + KD) // 2
                for j in range(FG):
                    product("F", j % 2, per * g + j // 2, W0["F"] + 8 * g + j, j % 2, xg_hi, xg_lo, SPLIT["H2"],
                            between[j] if j < 2 else {})
                for unit in range(KD // 2):
                    pe.wait_ge(w_ready, W0["F"] + 8 * g + FG + unit + 1)
                    if unit == 0:
                        order = [(k, m) for k in range(FG) for m in range(2)]
                    else:
                        order = [(k, m) for m in range(2) for k in range(FG)]
                    for k, m in order:
                        if k == 0:
                            free("F", m, per * g + FG // 2 + unit)
                        pe.wait_ge(lo_ready, SPLIT["F"] + FG * g + k + 1)
                        first, last = tile_product(m, unit % 2, m * FG + k, f_hi, f_lo, k, k == 0, k == FG - 1)
                        if (k, m) == (0, 0):
                            first.then_inc(w_passed, 1)
                        if k == FG - 1:
                            last.then_inc(psum_ready[m], 1)

            mixer_group(0, ({KD - 2: lambda: token_means("norm2", ssq)}, {KD // 2: lambda: spread("norm2", diag)}))
            with pe.Fori(1, NG) as g:
                mixer_group(g)

            for m in range(KD):
                unit = m * KP // UNIT
                if m == 2:
                    token_means("norm3", ssq)
                if m == 4:
                    spread("norm3", diag)
                free("PE", m % 2, m // 2)
                pe.wait_ge(w_ready, W0["PE"] + unit + 1)
                for k in range(KP):
                    pe.wait_ge(lo_ready, SPLIT["P"] + k + 1)
                    first, last = tile_product(m % 2, unit % 2, (m * KP + k) % UNIT, p_hi, p_lo, k, k == 0, k == KP - 1)
                    if (m * KP + k) % UNIT == 0:
                        first.then_inc(w_passed, 1)
                last.then_inc(psum_ready[m % 2], 1)
            with pe.Fori(0, KD // 2 - 1) as i:
                for j in range(2):
                    product("G", j, i, W0["G"] + 2 * i + j, j, xg_hi, xg_lo, SPLIT["H3"])
            product("G", 0, KD // 2 - 1, W0["G"] + KD - 2, 0, xg_hi, xg_lo, SPLIT["H3"])

            norm4 = NORM["norm4"]

            def last_piece(c, between=()):
                for k in range(KD):
                    if k in between:
                        between[k]()
                    for w, a in ((w_hi, xg_hi), (w_hi, xg_lo), (w_lo, xg_hi)):
                        last = pe.matmul(ps[:, 1, c, 0:TC], w[:, 1, k * P:(k + 1) * P], a[:, k, piece(c)],
                                         start=k == 0 and w is w_hi and a is xg_hi, stop=k == KD - 1 and w is w_lo)
                last.then_inc(last_ready, 1)

            def piece_means(c):
                pe.wait_ge(ssq_done, 10 * norm4 + 2 + KD + c)
                for j, t in enumerate(PIECE_TOK):
                    last = pe.matmul(pm[:, c % 2, MEAN_COL[c] + j:MEAN_COL[c] + j + 1], ssq[:, 0, c * TC + t:c * TC + t + P],
                                     ones[:, 0:1], start=True, stop=True)
                last.then_inc(norm_ready, 1)

            def piece_spread(c):
                pe.wait_ge(diag_ready, 2 * (norm4 + c + 1))
                if c == 2:
                    pe.wait_ge(norm_free, 4 * norm4 + 2)
                pe.matmul(pm[:, c % 2, 0:TC], ones[:, :], diag[:, 0, piece(c)], start=True, stop=True).then_inc(norm_ready, 1)

            free("G", 1, KD // 2 - 1)
            pe.wait_ge(w_ready, W0["G"] + KD)
            last_piece(0)
            last_piece(1)
            pe.wait_ge(norm_free, 4 * norm4)
            last_piece(2, {KD - 2: lambda: piece_means(0)})
            piece_spread(0)
            for c in (1, 2):
                piece_means(c)
                piece_spread(c)

        @block.scalar
        def _(act):
            act.dma_start(cols[:, 0:N_BIN + 7 * KD], io["cols"]).then_inc(const_loaded, 16)
            for k in range(1, KD, 2):
                act.dma_start(x1[:, k, :], io["xT"][k]).then_inc(x_loaded[k], 16)

            def load_tables():
                act.wait_ge(ws_zero, 1)
                act.dma_start(taps[:, :, :], io["taps"]).then_inc(tab_loaded, 16)
                act.dma_start(hist[:, :, :], io["state"]).then_inc(tab_loaded, 16)

            def load_layer_norm():
                act.dma_start(lnv_g[:, :], io["lnv_g"].partition_broadcast(P)).then_inc(lnv_loaded, 16)
                act.dma_start(lnv_b[:, :], io["lnv_b"].partition_broadcast(P)).then_inc(lnv_loaded, 16)

            def load_mixing_weights():
                act.dma_start(wm_raw[:, 0, 0:GROUPS * CHUNK], io["wsT"].rearrange("s g t -> s (g t)")).then_inc(wm_loaded, 16)
                for b in range(DEC_B):
                    act.dma_start(m2[b * DEC_S:(b + 1) * DEC_S, :, b * DEC_S:(b + 1) * DEC_S],
                                  io["wsT"][0:DEC_S, :, 0:DEC_S]).then_inc(wm_loaded, 16)

            def root(norm):
                act.wait_ge(tok_ready, NORM[norm] + 1)
                act.activation(tok[:, 1, 0:N_TOK], tok[:, 0, 0:N_TOK], ACT.Sqrt, scale=float(D * D)).then_inc(rms_ready, 1)

            act.wait_ge(w_loaded[0], 16)
            act.activation(w_hi[:, 0, :], w_raw[:, 0, :], ACT.Copy).then_inc(w_hi_done, 1)
            act.wait_ge(const_loaded, 16)
            for k in range(KD):
                act.wait_ge(x_loaded[k], 16)
                act.wait_ge(ssq_done, k + 1)
                act.activation(val[:, k % 2, :], x1[:, k, :], ACT.Square).then_inc(sq_done, 1)
                act.activation(x1g_hi[:, k, :], x1[:, k, :], ACT.Copy, scale=col(G_MIX, k)).then_inc(x1g_hi_done, 1)
            root("norm1")
            act.activation(tok[:, 1, 15:16], ones[:, 0:1], ACT.Sigmoid)

            def h1_high(k):
                act.wait_ge(val_ready, k + 1)
                act.activation(h1_hi[:, k, :], val[:, k % 2, :], ACT.Copy).then_inc(hi_ready, 1)

            def glu_and_gates(i, first):
                if first:
                    act.wait_ge(scaled, 1)
                    act.wait_ge(val_ready, 1)
                else:
                    act.wait_ge(glu_done, i + 1)
                    ready(act, "A", 0, 2 * i)
                act.activation(pieces(sig[:, 0, :]), bank(0), ACT.Sigmoid, bias=col(B_GATE, i)).then_inc(psum_free[0], 1)
                if first:
                    h1_high(0)
                    h1_high(1)
                    act.wait_ge(scaled, 2)
                else:
                    ready(act, "A", 1, 2 * i)
                act.activation(pieces(lin[:, 0, :]), bank(1), ACT.Identity, bias=col(B_LIN, i)).then_inc(psum_free[1], 1)
                if first:
                    for k in range(2, 5):
                        h1_high(k)
                for s, (bias, dst) in enumerate(((B_GA, sA_d), (B_GB, sB_d))):
                    if first:
                        act.wait_ge(scaled, 3 + s)
                    else:
                        ready(act, "A", s, 2 * i + 1)
                    act.activation(pieces(gate_st[:, s, :]), bank(s), ACT.Sigmoid, bias=col(bias, i)).then_inc(psum_free[s], 1)
                    out = drow(dst, i if first else act.snap(i))
                    act.wait_ge(psum_free[s], JOB["A"][s] + 2 * i + 2 + s)
                    act.dma_start(out, gate_st[:, s, :]).then_inc(gate_stored[s], 16)
                    if first and s == 0:
                        for k in range(5, KD):
                            h1_high(k)
                        load_tables()
                        load_mixing_weights()
                if first:
                    load_layer_norm()
                else:
                    out = drow(conv_d, act.snap(i - 1))
                    act.wait_ge(conv_done, i)
                    act.dma_start(out, conv_out[:, :]).then_inc(conv_stored, 16)
                for s in range(2):
                    act.wait_ge(gate_stored[s], 16 * (i + 1))

            glu_and_gates(0, True)
            act.wait_ge(wm_masked, 2)
            act.activation(wm_hi[:, :, :], m1, ACT.Copy).then_inc(wm_split, 1)
            act.activation(ws_hi[:, :, :], m2, ACT.Copy).then_inc(wm_split, 1)
            with act.Fori(1, KD) as i:
                glu_and_gates(i, False)

            def v_pair(i):
                for s in range(2):
                    ready(act, "V", s, i)
                    act.activation(pieces(row(vt, 2 * i + s)), bank(s), ACT.Gelu_apprx_tanh, bias=col(B_V, 2 * i + s))\
                        .then_inc(psum_free[s], 1)

            act.wait_ge(glu_done, KD + 1)
            v_pair(0)
            v_pair(1)
            act.wait_ge(conv_done, KD)
            act.dma_start(conv_d[KD - 1], conv_out[:, :]).then_inc(conv_stored, 16)
            act.dma_start(io["conv_sample"], hist[:, :, :]).then_inc(hist_stored, 16)
            act.dma_start(io["conv_prompt"], conv_tail[:, :, :]).then_inc(tail_stored, 16)
            act.wait_ge(conv_stored, 16 * (KD + 1))
            def convolved_back(i):
                for s in range(2):
                    src = drow(conv_d, 2 * i - 2 + s if isinstance(i, int) else act.snap(2 * i - 2 + s))
                    act.wait_ge(conv_sum, 2 * i - 1)
                    act.dma_start(conv_in[:, s, :], src).then_inc(conv_back[s], 16)

            with act.Fori(1, KD // 2) as i:
                convolved_back(i)
                v_pair(i + 1)
            convolved_back(KD // 2)
            act.wait_ge(conv_sum, 1 + KD)
            act.wait_ge(hist_stored, 16)
            act.wait_ge(tail_stored, 16)
            act.dma_start(bs_p[:, :, :].rearrange("p g t -> p (g t)"), io["bs_p"].partition_broadcast(P)).then_inc(bs_loaded, 16)
            act.dma_start(bs_s[:, :, :].rearrange("p g t -> p (g t)"), io["bs_s"].partition_broadcast(P)).then_inc(bs_loaded, 16)
            v_pair(KB // 2 - 1)
            ready(act, "mean", 0, 0)
            act.activation(pieces(conv_mean[:, 0, :]), bank(0), ACT.Identity).then_inc(psum_free[0], 1)

            def u_out(j, par, n):
                ready(act, "U", par, n)
                act.wait_ge(u_stored, 16 * j) if not (isinstance(j, int) and j == 0) else None
                act.activation(pieces(u_st[:, 0, :]), bank(par), ACT.Gelu_apprx_tanh, bias=col(B_U, j)).then_inc(psum_free[par], 1)
                out = drow(u_d, j if isinstance(j, int) else act.snap(j))
                act.wait_ge(psum_free[par], JOB["U"][par] + n + 1 + par)
                act.dma_start(out, u_st[:, 0, :]).then_inc(u_stored, 16)

            def u_stays(j, par, n):
                ready(act, "U", par, n)
                act.activation(pieces(gb[:, j, :]), bank(par), ACT.Gelu_apprx_tanh, bias=col(B_U, j)).then_inc(psum_free[par], 1)

            def take_chunk(n, w):
                src = vt[:, :, bass.ds(n * CHUNK, w)]
                act.activation(v_chunk[:, :, 0:w], src, ACT.Copy).then_inc(vc_done, 1)

            def layer_norm(n, next_width, store=None):
                if not (isinstance(n, int) and n == 0):
                    act.wait_ge(vlo_done, n)
                for g in range(3):
                    b = g % 2
                    before = 0 if isinstance(n, int) and n == 0 else (4 * n - 2 if b == 0 else 3 * n - 2)
                    act.wait_ge(pm_ready[b], before + g // 2 + 1)
                    act.activation(v_tok[:, g * 512:(g + 1) * 512], pm[:, b, :], ACT.Copy).then_inc(pm_free[b], 1)
                act.wait_ge(ln_step, LN_STEPS * n + 6)
                act.activation(rs_v[:, 0:1], rs_v[:, 0:1], ACT.Sqrt).then_inc(rs_ready, 1)
                act.wait_ge(ln_step, LN_STEPS * n + 7)
                act.activation(v_tok[:, :], v_tok[:, :], ACT.Identity, scale=rs_v[:, 0:1], bias=rs_v[:, 1:2])\
                    .then_inc(v_normed, 1)
                if next_width:
                    take_chunk(n + 1, next_width)
                act.wait_ge(ln_step, LN_STEPS * (n + 1))
                if store is not None:
                    act.dma_start(*store).then_inc(vout, 16)
                if not (isinstance(n, int) and n == 0):
                    act.wait_ge(pm_ready[0], 4 * n + 2)
                act.activation(v_hi[:, :], v_tok[:, :], ACT.Copy).then_inc(vhi_done, 1)

            def slot(n, par, product_n, next_width=CHUNK, store=None):
                layer_norm(n, next_width, store)
                u_out(n, par, product_n)

            act.wait_ge(psum_free[0], JOB["mean"][0])
            act.wait_ge(psum_free[1], JOB["U"][1] + 1)
            take_chunk(0, CHUNK)
            slot(0, 0, 0)
            with act.Fori(0, 3) as i:
                slot(2 * i + 1, 1, i)
                slot(2 * i + 2, 0, i + 1)
            slot(N_CHUNKS - 1, 1, 3, NS, (io["v_prompt"], v_tok[:, :]))
            act.wait_ge(vout, 16)
            slot(N_CHUNKS, 0, 4, 0, (io["v_sample"], v_tok[0:NS, :]))
            u_stays(9, 1, 4)
            act.wait_ge(vout, 32)
            act.wait_ge(pm_free[1], PM1_END)
            act.wait_ge(pm_free[0], PM0_END)
            act.wait_ge(u_stored, 16 * 9)
            for q in range(3):
                act.dma_start(gb[:, 3 * q:3 * q + 3, :], u_d[3 * q:3 * q + 3].rearrange("k p t -> p k t")).then_inc(u_back[q], 16)
            u_stays(10, 0, 5)

            def gb_high(a, b):
                with act.Fori(a, b) as k:
                    act.wait_ge(val_ready, KD + k + 1)
                    act.activation(row(gb_hi, k), row(gb, k), ACT.Copy).then_inc(hi_ready, 1)

            gb_high(0, 9)
            u_stays(11, 1, 5)
            act.dma_start(xc[:, :, :], conv_d.rearrange("k p t -> p k t")).then_inc(xc_loaded, 16)
            gb_high(9, KB)

            def gate_back(m):
                act.wait_ge(gated, m + 1)
                act.dma_start(sB_st[:, 0, :], sB_d[m]).then_inc(sB_loaded, 16)

            def centred_square(m):
                act.wait_ge(xc_done, m + 1)
                act.wait_ge(ssq_done, 10 * NORM["var"] + 2 + m)
                act.activation(sq_b[:, 0, :], row(xc, m), ACT.Square).then_inc(sq_done, 1)

            gate_back(0)
            with act.Fori(0, KD - 1) as m:
                centred_square(m)
            gate_back(1)
            centred_square(KD - 1)
            gate_back(2)
            gate_back(3)
            root("var")
            for m in range(4, 7):
                gate_back(m)
            with act.Fori(0, KD) as k:
                act.wait_ge(norm_y, k + 1)
                act.activation(row(xc, k), row(xc, k), ACT.Silu, bias=col(LNA_B, k), scale=col(LNA_G, k)).then_inc(silu_done, 1)
            gate_back(7)
            def branch_a_high(a, b):
                with act.Fori(a, b) as k:
                    act.activation(row(a_hi, k), row(xc, k), ACT.Copy).then_inc(hi_ready, 1)

            act.wait_ge(silu_done, KD)
            act.wait_ge(w_passed, W0["B"] + KB)
            branch_a_high(0, KD // 2)
            ready(act, "B", 1, KD // 2 - 1)
            branch_a_high(KD // 2, KD)

            def staged(m, par, dram, dst, loaded, freed, count):
                src = drow(dram, m if isinstance(m, int) else act.snap(m))
                act.wait_ge(freed, count)
                act.dma_start(dst[:, par, :], src).then_inc(loaded[par], 16)

            for m in range(2):
                staged(m, m, sA_d, sA_st, sA_loaded, gated, KD + 1)

            def mixed_high(m):
                act.wait_ge(mix_done, m + 1)
                act.activation(row(m_hi, m), row(mix, m), ACT.Copy).then_inc(hi_ready, 1)

            with act.Fori(0, KD // 2 - 1) as i:
                for s in range(2):
                    mixed_high(2 * i + s)
                    staged(2 * i + s + 2, s, sA_d, sA_st, sA_loaded, gated, KD + 2 + 2 * i + s)
            for m in (KD - 2, KD - 1):
                mixed_high(m)

            ready(act, "AO", 1, KD // 2 - 1)
            for m in range(2):
                act.dma_start(x[:, m, :], io["xT"][m]).then_inc(x_back[m], 16)

            def square_and_high(norm, name, gain, k, s, src):
                act.wait_ge(ssq_done, 10 * NORM[norm] + k + 1)
                act.activation(val[:, s, :], src, ACT.Square).then_inc(sq_done, 1)
                act.activation(row(xg_hi, k), src, ACT.Copy, scale=col(gain, k)).then_inc(hi_ready, 1)

            def x_sum_done(m, s):
                act.wait_ge(x_done, m + 2)
                square_and_high("norm2", "H2", G_FFN, m, s, row(x, m))

            with act.Fori(0, KD // 2 - 1) as i:
                for s in range(2):
                    m = 2 * i + s
                    src, dst = drow(io["xT"], act.snap(m + 2)), row(x, act.snap(m + 2))
                    x_sum_done(m, s)
                    act.dma_start(dst, src).then_inc(x_back[s], 16)
            for m in (KD - 2, KD - 1):
                x_sum_done(m, m % 2)
            root("norm2")
            act.dma_start(p_raw[:, :, :], io["pT"].rearrange("k p t -> p k t")).then_inc(p_loaded, 16)

            act.wait_ge(p_loaded, 16)
            for k in range(KP):
                act.activation(p_hi[:, k, :], p_raw[:, k, :], ACT.Copy).then_inc(hi_ready, 1)

            def wide_tiles(g):
                for j in range(FG):
                    act.wait_ge(relu_done, FG * g + j + 1)
                    act.wait_ge(lo_ready, SPLIT["F"] + FG * g + j - 1)
                    act.activation(f_hi[:, j, :], relu[:, 0, :], ACT.Square).then_inc(sq_f, 1)
                    act.activation(val[:, j % 2, :], relu[:, 0, :], ACT.Square).then_inc(hi_ready, 1)
                    act.wait_ge(hi_ready, SPLIT["F"] + FG * g + j + 1)

            with act.Fori(0, NG) as g:
                wide_tiles(g)
            for m in range(KD):
                act.wait_ge(psum_free[m % 2], JOB["PE"][m % 2] + m % 2 - KD // 2 + m // 2 + 1)
                square_and_high("norm3", "H3", G_PLE, m, m % 2, x[:, m, :])

            for m in range(KD):
                ready(act, "PE", m % 2, m // 2)
                act.activation(pieces(pe_out[:, m, :]), bank(m % 2), ACT.Identity).then_inc(psum_free[m % 2], 1)
                if m == 1:
                    root("norm3")
            def gate(m, s):
                act.wait_ge(z_ready, m + 1)
                act.wait_ge(g_mul, m + 1)
                act.activation(val[:, s, :], z_g[:, s, :], ACT.Sigmoid, bias=col(B_PLE, m)).then_inc(sg_done, 1)

            def y_square(m, s):
                act.wait_ge(x_done, 1 + KD + m + 1)
                act.wait_ge(ssq_done, 10 * NORM["norm4"] + m + 1)
                act.activation(sq_g[:, s, :], row(x, m), ACT.Square).then_inc(sq_done, 1)

            with act.Fori(0, KD // 2 - 1) as i:
                for s in range(2):
                    gate(2 * i + s, s)
                    y_square(2 * i + s, s)
            def gained(k):
                act.activation(x[:, k, :], x[:, k, :], ACT.Copy, scale=col(G_FIN, k)).then_inc(xg_done, 1)

            def gate_piece(c):
                act.wait_ge(z_ready, KD + c)
                act.activation(val[:, 1, piece(c)], z_g[:, 1, piece(c)], ACT.Sigmoid, bias=col(B_PLE, KD - 1)).then_inc(sg_done, 1)

            def square_piece(c):
                act.wait_ge(x_done, 1 + 2 * KD + c)
                act.activation(sq_g[:, 1, piece(c)], x[:, KD - 1, piece(c)], ACT.Square).then_inc(sq_done, 1)

            def piece_root(c):
                act.wait_ge(tok_ready, NORM["norm4"] + c + 1)
                act.activation(tok[:, 1, 4 * c:4 * c + 3], tok[:, 0, 4 * c:4 * c + 3], ACT.Sqrt, scale=float(D * D))\
                    .then_inc(rms_ready, 1)

            for k in range(Y_DVE, KD - 2):
                gained(k)
            gate(KD - 2, 0)
            y_square(KD - 2, 0)
            act.wait_ge(g_mul, KD)
            act.wait_ge(ssq_done, 10 * NORM["norm4"] + KD)
            gate_piece(0)
            square_piece(0)
            gate_piece(1)
            gained(KD - 2)
            square_piece(1)
            gate_piece(2)
            piece_root(0)
            square_piece(2)
            act.wait_ge(sq_done, KD * NORM["norm4"] + KD + 2)
            gained(KD - 1)
            piece_root(1)
            piece_root(2)
            for c in range(NC):
                act.wait_ge(y_pool, (KD - Y_DVE) * (c + 1))
                act.dma_start(io["y"][Y_DVE:KD, :, piece(c)].rearrange("k p t -> p k t"), y[:, Y_DVE:KD, piece(c)])\
                    .then_inc(y_stored, 16)
            act.wait_ge(y_stored, 16 * 2 * NC)

        @block.vector
        def _(dve):
            dve.memset(ones[:, :], 1.0 / D).then_inc(ones_set, 1)
            dve.sem_inc(psum_free[1], 1)
            dve.sem_inc(conv_stored, 16)

            def token_diagonals(norm, dst):
                n = NORM[norm]
                dve.wait_ge(norm_ready, 4 * n + 1)
                dve.tensor_scalar(tok[:, 0, 0:N_TOK], pm[:, 0, 0:N_TOK], EPS, None, ALU.add).then_inc(norm_free, 1)
                dve.wait_ge(norm_free, 4 * n + 1)
                dve.reciprocal(tok[:, 0, 0:N_TOK], tok[:, 0, 0:N_TOK]).then_inc(tok_ready, 1)
                dve.wait_ge(rms_ready, n + 1)
                full = SEQ // P
                dve.tensor_tensor(dst[:, 0, 0:SEQ].rearrange("p (c t) -> p c t", c=full),
                                  ident[:, :].unsqueeze(1).to_broadcast([P, full, P]),
                                  tok[:, 1, 0:full].unsqueeze(2).to_broadcast([P, full, P]), ALU.mult).then_inc(diag_ready, 1)
                dve.tensor_scalar(dst[:, 0, SEQ:T], ident[:, P - NS:P], tok[:, 1, full:full + 1], None, ALU.mult)\
                    .then_inc(diag_ready, 1)

            def spread_out(norm, dst):
                n = NORM[norm]
                for j, (b, t, w) in enumerate(NORM_PIECES):
                    dve.wait_ge(norm_ready, 4 * n + 2 + j)
                    dve.tensor_copy(dst[:, 0, t:t + w], pm[:, b, 0:w]).then_inc(norm_free, 1)
                dve.wait_ge(norm_free, 4 * n + 4)

            def add_row(norm, k, src):
                dve.wait_ge(sq_done, KD * NORM[norm] + k + 1)
                dve.wait_ge(ssq_done, 10 * NORM[norm] + 2 + k)
                dve.tensor_tensor(ssq[:, 0, :], ssq[:, 0, :], src, ALU.add).then_inc(ssq_done, 1)

            def gain_low(name, gain, k):
                dve.wait_ge(hi_ready, SPLIT[name] + k + 1)
                dve.scalar_tensor_tensor(out=row(xg_lo, k), in0=row(x, k), scalar=col(gain, k), in1=row(xg_hi, k).bitcast(F32),
                                         op0=ALU.mult, op1=ALU.subtract).then_inc(lo_ready, 1)

            dve.memset(ssq[:, 0, :], 0.0).then_inc(ssq_done, 2)
            dve.wait_ge(const_loaded, 16)
            for k in range(KD):
                add_row("norm1", k, val[:, k % 2, :])
                dve.wait_ge(x1g_hi_done, k + 1)
                dve.scalar_tensor_tensor(out=x1g_lo[:, k, :], in0=x1[:, k, :], scalar=col(G_MIX, k),
                                         in1=x1g_hi[:, k, :].bitcast(F32), op0=ALU.mult, op1=ALU.subtract)\
                    .then_inc(x1g_lo_done, 1)
            dve.wait_ge(ident_set, 2)
            token_diagonals("norm1", diag)
            spread_out("norm1", rstd)

            def scale(n):
                ready(dve, "A", n % 2, n // 2)
                dve.tensor_tensor(bank(n % 2), bank(n % 2), pieces(rstd[:, 0, :]), ALU.mult).then_inc(scaled, 1)

            def h1_value(k):
                dve.scalar_tensor_tensor(out=val[:, k % 2, :], in0=x1[:, k, :], scalar=col(G_MIX, k), in1=rstd[:, 0, :],
                                         op0=ALU.mult, op1=ALU.mult).then_inc(val_ready, 1)

            def h1_low(k):
                dve.wait_ge(hi_ready, SPLIT["H1"] + k + 1)
                dve.tensor_tensor(h1_lo[:, k, :], val[:, k % 2, :], h1_hi[:, k, :].bitcast(F32), ALU.subtract).then_inc(lo_ready, 1)
                dve.wait_ge(lo_ready, SPLIT["H1"] + k + 1)

            scale(0)
            h1_value(0)
            scale(1)
            h1_low(0)
            h1_value(1)
            for k in range(2, KD):
                h1_value(k)
                h1_low(k - 1)
                if k == 4:
                    scale(2)
            h1_low(KD - 1)
            scale(3)

            dve.memset(glu[:, 0:HIST], 0.0).then_inc(glu_done, 1)
            dve.wait_ge(tab_loaded, 32)

            with dve.Fori(0, KD) as i:
                step = CONV_STEPS * i
                dve.tensor_copy(tap[:, :], taps[:, bass.ds(i, 1), :].rearrange("p a n -> p (a n)")).then_inc(tap_set, 1)
                dve.wait_ge(psum_free[1], JOB["A"][1] + 2 * i + 2)
                dve.tensor_tensor(glu[:, HIST:HIST + T], lin[:, 0, :], sig[:, 0, :], ALU.mult).then_inc(glu_done, 1)
                dve.wait_ge(glu_done, i + 2)
                dve.wait_ge(tap_set, i + 1)
                new = glu[:, HIST + SEQ:HIST + T].rearrange("p (b t) -> p b t", b=DEC_B)
                h_i = hist[:, bass.ds(DEC_B * i, DEC_B), :]
                dve.tensor_copy(h_i[:, :, HIST:HIST + DEC_S], new).then_inc(conv_step, 1)
                dve.tensor_copy(conv_tail[:, bass.ds(i, 1), :].rearrange("p a n -> p (a n)"),
                                glu[:, SEQ:SEQ + HIST]).then_inc(conv_step, 1)
                dve.tensor_scalar(acc0[:, :], glu[:, 0:SEQ], tap[:, 0:1], tap[:, TAPS:TAPS + 1], ALU.mult, ALU.add)\
                    .then_inc(conv_step, 1)
                dve.tensor_scalar(acc1[:, :], glu[:, 1:1 + SEQ], tap[:, 1:2], None, ALU.mult).then_inc(conv_step, 1)
                for j in range(2, TAPS):
                    acc = acc0 if j % 2 == 0 else acc1
                    dve.wait_ge(conv_step, step + 2 + j - 1)
                    dve.scalar_tensor_tensor(out=acc[:, :], in0=glu[:, j:j + SEQ], scalar=tap[:, j:j + 1], in1=acc[:, :],
                                             op0=ALU.mult, op1=ALU.add).then_inc(conv_step, 1)
                w = tap[:, 0:TAPS].unsqueeze(1).to_broadcast([P, DEC_B, TAPS])
                for t in range(DEC_S):
                    dve.tensor_tensor(prod[:, t, :, :], h_i[:, :, t:t + TAPS], w, ALU.mult).then_inc(conv_step, 1)
                dve.wait_ge(conv_step, step + 2 + TAPS + DEC_S)
                dve.tensor_reduce(samp[:, :].rearrange("p (t b) -> p t b", t=DEC_S), prod[:, :, :, :], AX_X, ALU.add)\
                    .then_inc(conv_step, 1)
                dve.wait_ge(conv_step, step + CONV_STEPS)
                dve.wait_ge(conv_stored, 16 * i + 16)
                dve.tensor_scalar(conv_out[:, SEQ:T].rearrange("p (b t) -> p t b", b=DEC_B),
                                  samp[:, :].rearrange("p (t b) -> p t b", t=DEC_S), tap[:, TAPS:TAPS + 1], None, ALU.add)
                dve.tensor_tensor(conv_out[:, 0:SEQ], acc0[:, :], acc1[:, :], ALU.add).then_inc(conv_done, 1)
                dve.wait_ge(conv_done, i + 1)

            dve.memset(conv_mean[:, 0, :], 0.0).then_inc(conv_sum, 1)
            with dve.Fori(0, KD // 2) as i:
                for s in range(2):
                    dve.wait_ge(conv_back[s], 16 * (i + 1))
                    dve.wait_ge(conv_sum, 2 * i + s + 1)
                    dve.tensor_tensor(conv_mean[:, 0, :], conv_mean[:, 0, :], conv_in[:, s, :], ALU.add).then_inc(conv_sum, 1)

            dve.wait_ge(psum_free[1], JOB["U"][1] + 1)
            dve.wait_ge(psum_free[0], JOB["mean"][0])
            dve.wait_ge(bs_loaded, 32)
            dve.wait_ge(lnv_loaded, 32)

            def statistics(n):
                s = LN_STEPS * n
                first = isinstance(n, int) and n == 0
                dve.wait_ge(pm_free[0], 2 if first else 4 * n)
                dve.wait_ge(pm_free[1], 1 if first else 3 * n - 1)
                for g in range(3):
                    dve.bn_stats(stats[:, g, :], v_tok[:, g * 512:(g + 1) * 512]).then_inc(ln_step, 1)
                dve.wait_ge(ln_step, s + 3)
                dve.memset(rs_v[:, 0:1], EPS)
                dve.bn_aggr(mv[:, :], stats[:, :, :]).then_inc(ln_step, 1)
                dve.wait_ge(ln_step, s + 4)
                dve.tensor_tensor(rs_v[:, 0:1], rs_v[:, 0:1], mv[:, 1:2], ALU.add).then_inc(ln_step, 1)
                dve.wait_ge(ln_step, s + 5)
                dve.reciprocal(rs_v[:, 0:1], rs_v[:, 0:1]).then_inc(ln_step, 1)

            def shift(n):
                dve.wait_ge(rs_ready, n + 1)
                dve.scalar_tensor_tensor(out=rs_v[:, 1:2], in0=mv[:, 0:1], scalar=-1.0, in1=rs_v[:, 0:1],
                                         op0=ALU.mult, op1=ALU.mult).then_inc(ln_step, 1)

            def gain(n):
                dve.wait_ge(v_normed, n + 1)
                dve.tensor_tensor(v_tok[:, :], v_tok[:, :], lnv_g[:, :], ALU.mult).then_inc(ln_step, 1)

            def bias(n):
                dve.wait_ge(ln_step, LN_STEPS * n + 8)
                dve.tensor_tensor(v_tok[:, :], v_tok[:, :], lnv_b[:, :], ALU.add).then_inc(ln_step, 1)

            def low(n):
                dve.wait_ge(vhi_done, n + 1)
                dve.tensor_tensor(v_lo[:, :], v_tok[:, :], v_hi[:, :].bitcast(F32), ALU.subtract).then_inc(vlo_done, 1)

            def mixed_out(n, q, w, bs, last_chunk=False):
                b = (q + 1) % 2
                before = (4 * n + 4 - 2 * last_chunk if b == 0 else 3 * n + 2 - last_chunk) + q // 2
                dve.wait_ge(pm_ready[b], before + 1)
                for c, p0, p1, off, g in ((0, 0, P, 0, 0), (1, 0, 64, 128, 0), (1, 64, P, 128 + w, 1), (2, 0, P, 384, 1)):
                    dst = vt[p0:p1, 3 * q + c, bass.ds(n * CHUNK, w)]
                    last = dve.tensor_tensor(dst, pm[p0:p1, b, off:off + w], bs[p0:p1, 2 * q + g, :], ALU.add)
                last.then_inc(pm_free[b], 1)

            statistics(0)
            shift(0)
            gain(0)
            bias(0)
            low(0)

            def slot(n):
                statistics(n)
                shift(n)
                mixed_out(n - 1, 0, CHUNK, bs_p)
                mixed_out(n - 1, 1, CHUNK, bs_p)
                gain(n)
                mixed_out(n - 1, 2, CHUNK, bs_p)
                bias(n)
                mixed_out(n - 1, 3, CHUNK, bs_p)
                low(n)

            with dve.Fori(1, N_CHUNKS + 1) as n:
                slot(n)
            for q in range(4):
                mixed_out(N_CHUNKS, q, NS, bs_s, True)

            dve.wait_ge(pm_free[0], PM0_END)
            dve.wait_ge(pm_free[1], PM1_END)

            def gb_product(a, b):
                with dve.Fori(a, b) as k:
                    dve.tensor_tensor(row(gb, k), row(gb, k), row(vt, k), ALU.mult).then_inc(val_ready, 1)

            def gb_low(a, b):
                with dve.Fori(a, b) as k:
                    dve.wait_ge(hi_ready, SPLIT["GB"] + k + 1)
                    dve.tensor_tensor(row(gb_lo, k), row(gb, k), row(gb_hi, k).bitcast(F32), ALU.subtract).then_inc(lo_ready, 1)

            for q in range(3):
                dve.wait_ge(u_back[q], 16)
                gb_product(3 * q, 3 * q + 3)
                if q:
                    gb_low(3 * q - 3, 3 * q)
            gb_low(6, 9)
            dve.wait_ge(psum_free[1], JOB["U"][1] + 5 + 1)
            dve.wait_ge(psum_free[0], JOB["U"][0] + 6)
            gb_product(9, 11)
            dve.wait_ge(psum_free[1], JOB["U"][1] + 6 + 1)
            gb_product(11, KB)
            gb_low(9, KB)
            dve.memset(ssq_b[:, 0, :], 0.0).then_inc(ssq_done, 2)
            dve.sem_inc(gated, 1)
            dve.wait_ge(xc_loaded, 16)

            def centre(m):
                dve.tensor_tensor(row(xc, m), row(xc, m), conv_mean[:, 0, :], ALU.subtract).then_inc(xc_done, 1)

            def add_square(m):
                dve.wait_ge(sq_done, KD * NORM["var"] + m + 1)
                dve.wait_ge(ssq_done, 10 * NORM["var"] + 2 + m)
                dve.tensor_tensor(ssq_b[:, 0, :], ssq_b[:, 0, :], sq_b[:, 0, :], ALU.add).then_inc(ssq_done, 1)

            def gate_b(m):
                s, n = m % 2, m // 2
                ready(dve, "B", s, n)
                dve.wait_ge(sB_loaded, 16 * (m + 1))
                dve.tensor_tensor(pieces(mix[:, m, :]), bank(s), pieces(sB_st[:, 0, :]), ALU.mult).then_inc(psum_free[s], 1)
                dve.wait_ge(psum_free[s], JOB["B"][s] + n + 1 + s)
                dve.sem_inc(gated, 1)

            centre(0)
            with dve.Fori(1, KD - 1) as m:
                centre(m)
                add_square(m - 1)
            gate_b(0)
            centre(KD - 1)
            add_square(KD - 2)
            add_square(KD - 1)
            for m in range(1, 4):
                gate_b(m)
            token_diagonals("var", diag_b)
            for m in range(4, 6):
                gate_b(m)
            spread_out("var", rstd_b)
            with dve.Fori(0, KD) as k:
                dve.tensor_tensor(row(xc, k), row(xc, k), rstd_b[:, 0, :], ALU.mult).then_inc(norm_y, 1)
            gate_b(6)

            def branch_a_low(a, b):
                with dve.Fori(a, b) as k:
                    dve.wait_ge(hi_ready, SPLIT["A"] + k + 1)
                    dve.tensor_tensor(row(a_lo, k), row(xc, k), row(a_hi, k).bitcast(F32), ALU.subtract).then_inc(lo_ready, 1)

            branch_a_low(0, KD // 2)
            gate_b(7)
            branch_a_low(KD // 2, KD)
            with dve.Fori(0, KD // 2) as i:
                for s in range(2):
                    m = 2 * i + s
                    ready(dve, "AO", s, i)
                    dve.wait_ge(sA_loaded[s], 16 * (i + 1))
                    dve.tensor_tensor(pieces(val[:, s, :]), bank(s), pieces(sA_st[:, s, :]), ALU.mult).then_inc(psum_free[s], 1)
                    dve.wait_ge(psum_free[s], JOB["AO"][s] + i + 1 + s)
                    dve.sem_inc(gated, 1)
                    dve.tensor_tensor(row(mix, m), row(mix, m), val[:, s, :], ALU.add).then_inc(mix_done, 1)
                    dve.wait_ge(hi_ready, SPLIT["M"] + m + 1)
                    dve.tensor_tensor(row(m_lo, m), row(mix, m), row(m_hi, m).bitcast(F32), ALU.subtract).then_inc(lo_ready, 1)
            dve.wait_ge(lo_ready, SPLIT["M"] + KD)
            dve.sem_inc(x_done, 1)

            dve.memset(ssq[:, 0, :], 0.0).then_inc(ssq_done, 2)
            with dve.Fori(0, KD // 2) as i:
                for s in range(2):
                    m = 2 * i + s
                    ready(dve, "O", s, i)
                    dve.wait_ge(x_back[s], 16 * (i + 1))
                    dve.tensor_tensor(pieces(row(x, m)), bank(s), pieces(row(x, m)), ALU.add).then_inc(psum_free[s], 1)
                    dve.wait_ge(psum_free[s], JOB["O"][s] + i + 1 + s)
                    dve.sem_inc(x_done, 1)
                    add_row("norm2", m, val[:, s, :])
                    gain_low("H2", G_FFN, m)
            token_diagonals("norm2", diag)
            spread_out("norm2", rstd)

            per = (FG + KD) // 2

            def wide_low(g):
                for j in range(FG):
                    ready(dve, "F", j % 2, per * g + j // 2)
                    dve.scalar_tensor_tensor(out=pieces(relu[:, 0, :]), in0=bank(j % 2), scalar=0.0, in1=pieces(rstd[:, 0, :]),
                                             op0=ALU.max, op1=ALU.mult).then_inc(psum_free[j % 2], 1)
                    dve.wait_ge(psum_free[j % 2], JOB["F"][j % 2] + per * g + j // 2 + 1 + j % 2)
                    dve.sem_inc(relu_done, 1)
                    dve.wait_ge(hi_ready, SPLIT["F"] + FG * g + j + 1)
                    dve.tensor_tensor(f_lo[:, j, :], val[:, j % 2, :], f_hi[:, j, :].bitcast(F32), ALU.subtract)\
                        .then_inc(lo_ready, 1)

            def add_to_x(g, m):
                ready(dve, "F", m % 2, per * g + (FG + m) // 2)
                dve.tensor_tensor(pieces(x[:, m, :]), bank(m % 2), pieces(x[:, m, :]), ALU.add).then_inc(psum_free[m % 2], 1)

            def embedding_low():
                for k in range(KP):
                    dve.wait_ge(hi_ready, SPLIT["P"] + k + 1)
                    dve.tensor_tensor(p_lo[:, k, :], p_raw[:, k, :], p_hi[:, k, :].bitcast(F32), ALU.subtract).then_inc(lo_ready, 1)

            embedding_low()
            with dve.Fori(0, NG - 1) as g:
                wide_low(g)
                for m in range(KD):
                    add_to_x(g, m)
            wide_low(NG - 1)
            dve.memset(ssq[:, 0, :], 0.0).then_inc(ssq_done, 2)
            for m in range(KD):
                add_to_x(NG - 1, m)
                if m:
                    add_row("norm3", m - 1, val[:, (m - 1) % 2, :])
                    gain_low("H3", G_PLE, m - 1)
            add_row("norm3", KD - 1, val[:, (KD - 1) % 2, :])
            gain_low("H3", G_PLE, KD - 1)
            token_diagonals("norm3", diag)
            spread_out("norm3", rstd)
            dve.sem_inc(g_mul, 2)
            dve.memset(ssq[:, 0, :], 0.0).then_inc(ssq_done, 2)
            def gated_embedding(m, s, i):
                ready(dve, "G", s, i)
                dve.tensor_tensor(pieces(z_g[:, s, :]), bank(s), pieces(rstd[:, 0, :]), ALU.mult).then_inc(psum_free[s], 1)
                dve.wait_ge(psum_free[s], JOB["G"][s] + i + 1 + s)
                dve.sem_inc(z_ready, 1)
                dve.wait_ge(sg_done, m + 1)
                dve.tensor_tensor(row(pe_out, m), row(pe_out, m), val[:, s, :], ALU.mult).then_inc(g_mul, 1)
                dve.wait_ge(g_mul, m + 3)
                dve.tensor_tensor(row(x, m), row(x, m), row(pe_out, m), ALU.add).then_inc(x_done, 1)

            with dve.Fori(0, KD // 2 - 1) as i:
                for s in range(2):
                    gated_embedding(2 * i + s, s, i)
                    add_row("norm4", 2 * i + s, sq_g[:, s, :])
            gated_embedding(KD - 2, 0, KD // 2 - 1)

            norm4, m = NORM["norm4"], KD - 1

            def z_piece(c):
                dve.wait_ge(last_ready, c + 1)
                dve.tensor_tensor(z_g[:, 1, piece(c)], ps[:, 1, c, 0:TC], rstd[:, 0, piece(c)], ALU.mult).then_inc(z_ready, 1)

            def sum_piece(c):
                dve.wait_ge(sg_done, KD + c)
                dve.tensor_tensor(pe_out[:, m, piece(c)], pe_out[:, m, piece(c)], val[:, 1, piece(c)], ALU.mult).then_inc(g_mul, 1)
                dve.wait_ge(g_mul, m + 3 + c)
                dve.tensor_tensor(x[:, m, piece(c)], x[:, m, piece(c)], pe_out[:, m, piece(c)], ALU.add).then_inc(x_done, 1)

            def square_sum_piece(c):
                dve.wait_ge(sq_done, KD * norm4 + KD + c)
                dve.wait_ge(ssq_done, 10 * norm4 + 1 + KD)
                dve.tensor_tensor(ssq[:, 0, piece(c)], ssq[:, 0, piece(c)], sq_g[:, 1, piece(c)], ALU.add).then_inc(ssq_done, 1)

            def piece_inverse(c):
                t = tok[:, 0, 4 * c:4 * c + 3]
                dve.wait_ge(norm_ready, 4 * norm4 + 2 * c + 1)
                dve.tensor_scalar(t, pm[:, c % 2, MEAN_COL[c]:MEAN_COL[c] + 3], EPS, None, ALU.add).then_inc(norm_free, 1)
                dve.wait_ge(norm_free, 4 * norm4 + 2 * c + 1)
                dve.reciprocal(t, t).then_inc(tok_ready, 1)

            def piece_diagonals(c):
                dve.wait_ge(rms_ready, norm4 + c + 1)
                d = diag[:, 0, piece(c)]
                dve.tensor_tensor(d[:, 0:2 * P].rearrange("p (c t) -> p c t", c=2), ident[:, :].unsqueeze(1).to_broadcast([P, 2, P]),
                                  tok[:, 1, 4 * c:4 * c + 2].unsqueeze(2).to_broadcast([P, 2, P]), ALU.mult).then_inc(diag_ready, 1)
                dve.tensor_scalar(d[:, 2 * P:TC], ident[:, 3 * P - TC:P], tok[:, 1, 4 * c + 2:4 * c + 3], None, ALU.mult)\
                    .then_inc(diag_ready, 1)

            def piece_rstd(c):
                dve.wait_ge(norm_ready, 4 * norm4 + 2 * c + 2)
                dve.tensor_copy(rstd[:, 0, piece(c)], pm[:, c % 2, 0:TC]).then_inc(norm_free, 1)

            def y_piece(c):
                dve.wait_ge(norm_free, 4 * norm4 + 2 * c + 2)
                for k in range(Y_DVE):
                    dve.scalar_tensor_tensor(out=y[:, k, piece(c)], in0=x[:, k, piece(c)], scalar=col(G_FIN, k),
                                             in1=rstd[:, 0, piece(c)], op0=ALU.mult, op1=ALU.mult).then_inc(y_ready, 1)

            z_piece(0)
            add_row("norm4", KD - 2, sq_g[:, 0, :])
            sum_piece(0)
            z_piece(1)
            square_sum_piece(0)
            sum_piece(1)
            z_piece(2)
            square_sum_piece(1)
            piece_inverse(0)
            sum_piece(2)
            piece_diagonals(0)
            square_sum_piece(2)
            piece_rstd(0)
            piece_inverse(1)
            piece_diagonals(1)
            y_piece(0)
            piece_rstd(1)
            piece_inverse(2)
            piece_diagonals(2)
            y_piece(1)
            piece_rstd(2)
            y_piece(2)


PIECE_TOK = (0, P, TC - P)
MEAN_COL = (400, 404, 408)
WARM_UP = 20
LAG = 3
LN_STEPS = 9
NORM_PIECES = ((0, 0, 512), (1, 512, 512), (0, 1024, T - 1024))
CONV_STEPS = 2 + TAPS + DEC_S + 1
PM0_END = 4 * (N_CHUNKS + 1)
PM1_END = 3 * (N_CHUNKS + 1)


def kernel(**inputs):
    import numpy as np
    import concourse.bacc as bacc
    from concourse.bass_utils import run_bass_kernel_spmd

    a = {k: np.asarray(v) for k, v in inputs.items()}

    def tokens(prompt, sample, k):
        both = np.concatenate([prompt.reshape(SEQ, -1), sample.reshape(NS, -1)], axis=0)
        return np.ascontiguousarray(both.T).reshape(k, P, T)

    def by_output(w):
        k, n = w.shape[0] // P, w.shape[1] // P
        return w.reshape(k, P, n, P).transpose(2, 1, 0, 3).reshape(n, P, k * P)

    def by_tile(w):
        return w.reshape(w.shape[0] // P, P, w.shape[1] // P, P).transpose(2, 0, 1, 3)

    def packed(tiles):
        return tiles.reshape(-1, UNIT, P, P).transpose(0, 2, 1, 3).reshape(-1, P, UNIT * P)

    w_in = by_output(a["w_in"][0])
    order = [b + m for m in range(KD) for b in (B_GATE, B_LIN, B_GA, B_GB)]
    order += [B_V + m for m in range(KB)] + [B_U + m for m in range(KB)]
    ff1 = by_output(a["w_ff1"][0]).reshape(NG, FG, P, UNIT * P)
    ff2 = np.stack([packed(by_tile(a["w_ff2"][0][g * FG * P:(g + 1) * FG * P])) for g in range(NG)])
    weights = np.concatenate([
        w_in[order], packed(by_tile(a["w_b_out"][0])), by_output(a["w_a_out"][0]), by_output(a["w_o"][0]),
        np.concatenate([ff1, ff2], axis=1).reshape(-1, P, UNIT * P),
        packed(by_tile(a["w_ple"][0])), by_output(a["w_ple_gate"][0])])

    def column(v):
        return v.reshape(-1, P).T

    arrays = {
        "xT": tokens(a["x_prompt"], a["x_sample"], KD),
        "pT": tokens(a["p_prompt"][0], a["p_sample"][0], KP),
        "weights": weights,
        "cols": np.concatenate([column(v) for v in (
            a["b_in"][0], a["g_mix"][0], a["g_ffn"][0], a["g_ple"][0], a["g_final"], a["ln_a_g"][0],
            a["ln_a_b"][0], a["b_ple_gate"][0])], axis=1),
        "taps": np.concatenate([a["conv_w"][0], a["conv_b"]], axis=0).reshape(TAPS + 1, KD, P).transpose(2, 1, 0),
        "state": np.pad(a["state_conv"][0].reshape(DEC_B, HIST, KD, P).transpose(3, 2, 0, 1).reshape(P, KD * DEC_B, HIST),
                        ((0, 0), (0, 0), (0, DEC_S))),
        "wsT": a["w_s"][0].transpose(2, 0, 1),
        "lnv_g": a["ln_v_g"][0],
        "lnv_b": a["ln_v_b"][0],
        "bs_p": a["b_s"][0].reshape(-1),
        "bs_s": np.tile(a["b_s"][0][:, None, :DEC_S], (1, DEC_B, 1)).reshape(-1),
    }
    outs = {"y": (KD, P, T), "conv_prompt": (P, KD, HIST), "conv_sample": (P, KD * DEC_B, HIST + DEC_S),
            "v_prompt": (CHUNK, C_B), "v_sample": (NS, C_B)}
    nc = bacc.Bacc("TRN2", target_bir_lowering=False, num_devices=1)
    io = {}
    arrays = {k: np.ascontiguousarray(v) for k, v in arrays.items()}
    for k, v in arrays.items():
        io[k] = nc.dram_tensor(k, v.shape, mybir.dt.from_np(v.dtype), kind="ExternalInput").ap()
    for k, shape in outs.items():
        io[k] = nc.dram_tensor(k, shape, F32, kind="ExternalOutput").ap()
    build(nc, io)
    r = run_bass_kernel_spmd(nc, [arrays], core_ids=[0]).results[0]
    y = r["y"].reshape(D, T).T
    conv_p = r["conv_prompt"].transpose(2, 1, 0).reshape(1, 1, HIST, D)
    conv_s = r["conv_sample"][:, :, DEC_S:].reshape(P, KD, DEC_B, HIST).transpose(2, 3, 1, 0).reshape(1, DEC_B, HIST, D)
    return (np.ascontiguousarray(y[:SEQ]).reshape(1, SEQ, D), np.ascontiguousarray(y[SEQ:]).reshape(DEC_B, DEC_S, D),
            np.ascontiguousarray(conv_p), np.ascontiguousarray(conv_s),
            r["v_prompt"].reshape(1, 1, CHUNK, C_B), r["v_sample"].reshape(1, DEC_B, DEC_S, C_B))
```
